# Optimizing a Trainium2 kernel written in Bass

```python
import math
import jax, jax.numpy as jnp
from jax import lax
import numpy as np

'''Hybrid bidirectional encoder trunk (DEPTH layers), run on two request batches with shared weights.

Each layer (sandwich RMSNorm around both sub-layers):
  h = RMSNorm(x); z = h @ w_in  (one combined projection, columns partitioned over head groups)
    group A: multi-head latent attention (low-rank q and kv, decoupled 1-D rotary key), 4 heads
    group B: LongNet dilated sliding-window attention, 4 heads, (window, dilation) in
             (128,1),(512,4),(2048,16), combined by softmax denominators, T5 relative bias
    group C: grouped-query attention (8 q heads / 2 kv heads), per-head RMS q/k norm,
             2-D axial rotary over the (row, column) token grid
  x = x + RMSNorm(concat(A, B, C) @ w_out)
  x = x + RMSNorm(ConvGatedMLP(RMSNorm(x)))   (depthwise centred conv width 3 before GELU gate)

Inputs: x_prompt (BATCH, SEQ, D_MODEL), x_sample (DEC_BATCH, DEC_SEQ, D_MODEL), weights.
Outputs: (y_prompt (BATCH, SEQ, D_MODEL), y_sample (DEC_BATCH, DEC_SEQ, D_MODEL)).
'''

D_MODEL = 1024
BATCH = 1
SEQ = 1024
DEPTH = 2
DEC_BATCH = 1
DEC_SEQ = 256
PAST_LEN = 128

GRID_W = 64
HD = 64
H_A = 4
Q_LORA = 256
KV_LORA = 128
NOPE_A = 64
ROPE_A = 32
V_A = 64
H_B = 4
DIL_PATTERNS = ((128, 1), (512, 4), (2048, 16))
N_BUCKETS = 32
MAX_DISTANCE = 1024
H_C = 8
KV_C = 2
D_MIX = H_A * V_A + H_B * HD + H_C * HD
IN_SIZES = (Q_LORA, KV_LORA, ROPE_A, H_B * HD, H_B * HD, H_B * HD, H_C * HD, KV_C * HD, KV_C * HD)
N_IN = sum(IN_SIZES)
D_FF = 2816
CONV_W = 3
Q_BLOCK = 128
ROPE_THETA = 10000.0
EPS = 1e-6

kernel_name = 'hybrid_parallel_encoder'

def rms_norm(x, g):
    xf = x.astype(jnp.float32)
    y = xf * lax.rsqrt(jnp.mean(xf * xf, axis=-1, keepdims=True) + EPS)
    return (y * g.astype(jnp.float32)).astype(x.dtype)

def rope_angles(pos, n_freq):
    inv = ROPE_THETA ** (-jnp.arange(n_freq, dtype=jnp.float32) / n_freq)
    return pos.astype(jnp.float32)[:, None] * inv[None, :]

def apply_rope(x, ang):
    shape = (ang.shape[0],) + (1,) * (x.ndim - 3) + (ang.shape[1],)
    cos = jnp.cos(ang).reshape(shape).astype(x.dtype)
    sin = jnp.sin(ang).reshape(shape).astype(x.dtype)
    x1, x2 = jnp.split(x, 2, axis=-1)
    return jnp.concatenate([x1 * cos - x2 * sin, x2 * cos + x1 * sin], axis=-1)

def t5_bucket(rel):
    half = N_BUCKETS // 2
    exact = half // 2
    n = np.abs(rel)
    large = exact + (np.log(np.maximum(n, 1) / exact) / math.log(MAX_DISTANCE / exact) * (half - exact)).astype(np.int32)
    large = np.minimum(large, half - 1)
    return (np.where(rel > 0, half, 0) + np.where(n < exact, n, large)).astype(np.int32)

def block_attention(q, k, v, scale):
    b, s = q.shape[0], q.shape[1]
    nq = s // Q_BLOCK
    qb = q.reshape((b, nq, Q_BLOCK) + q.shape[2:]).swapaxes(0, 1)

    def one(qblk):
        logits = jnp.einsum('bqhgd,bkhd->bhgqk', qblk, k).astype(jnp.float32) * scale
        p = jax.nn.softmax(logits, axis=-1)
        return jnp.einsum('bhgqk,bkhd->bqhgd', p.astype(v.dtype), v)

    out = lax.map(one, qb)
    return out.swapaxes(0, 1).reshape(b, s, -1)

def dilated_window_attention(q, k, v, rel_bias, window, dilation):
    b, s, h, dh = q.shape
    w = window // (2 * dilation)
    L = s // dilation
    nb = -(-L // w)
    lp = nb * w

    def strided(a):
        return a.reshape(b, L, dilation, h, dh).transpose(0, 2, 1, 3, 4)

    qs = jnp.pad(strided(q), ((0, 0), (0, 0), (0, lp - L), (0, 0), (0, 0))).reshape(b, dilation, nb, w, h, dh)

    def windows(a):
        ap = jnp.pad(strided(a), ((0, 0), (0, 0), (w, lp - L + w), (0, 0), (0, 0))).reshape(b, dilation, nb + 2, w, h, dh)
        return jnp.concatenate([ap[:, :, :-2], ap[:, :, 1:-1], ap[:, :, 2:]], axis=3)

    kw, vw = windows(k), windows(v)
    rel = np.arange(3 * w)[None, :] - w - np.arange(w)[:, None]
    key_l = np.arange(nb)[:, None] * w + np.arange(3 * w)[None, :] - w
    mask = (np.abs(rel) <= w)[None] & ((key_l >= 0) & (key_l < L))[:, None, :]
    bias = jnp.transpose(rel_bias[t5_bucket(rel * dilation)], (2, 0, 1)).astype(jnp.float32)
    logits = jnp.einsum('brnqhd,brnkhd->brnhqk', qs, kw).astype(jnp.float32) * (dh ** -0.5) + bias
    logits = jnp.where(mask[:, None], logits, -jnp.inf)
    m = jnp.max(logits, axis=-1, keepdims=True)
    e = jnp.exp(logits - m)
    den = jnp.sum(e, axis=-1, keepdims=True)
    o = jnp.einsum('brnhqk,brnkhd->brnqhd', (e / den).astype(v.dtype), vw)
    lse = (m + jnp.log(den))[..., 0]
    o = o.reshape(b, dilation, lp, h, dh)[:, :, :L].transpose(0, 2, 1, 3, 4).reshape(b, s, h, dh)
    lse = lse.transpose(0, 1, 2, 4, 3).reshape(b, dilation, lp, h)[:, :, :L].transpose(0, 2, 1, 3).reshape(b, s, h)
    return o, lse

def mla_mixer(cq, ckv, krope, q_lora_norm, w_uq, kv_norm, w_ukv, ang):
    b, s, _ = cq.shape
    q = (rms_norm(cq, q_lora_norm) @ w_uq).reshape(b, s, H_A, NOPE_A + ROPE_A)
    kv = (rms_norm(ckv, kv_norm) @ w_ukv).reshape(b, s, H_A, NOPE_A + V_A)
    q = jnp.concatenate([q[..., :NOPE_A], apply_rope(q[..., NOPE_A:], ang)], axis=-1)
    kr = apply_rope(krope, ang)
    k = jnp.concatenate([kv[..., :NOPE_A], jnp.broadcast_to(kr[:, :, None, :], (b, s, H_A, ROPE_A))], axis=-1)
    v = kv[..., NOPE_A:]
    return block_attention(q[:, :, :, None, :], k, v, (NOPE_A + ROPE_A) ** -0.5)

def dilated_mixer(zq, zk, zv, rel_bias):
    b, s, _ = zq.shape
    q = zq.reshape(b, s, H_B, HD)
    k = zk.reshape(b, s, H_B, HD)
    v = zv.reshape(b, s, H_B, HD)
    outs, lses = [], []
    for window, dilation in DIL_PATTERNS:
        o, l = dilated_window_attention(q, k, v, rel_bias, window, dilation)
        outs.append(o)
        lses.append(l)
    wts = jax.nn.softmax(jnp.stack(lses, axis=0), axis=0)
    out = jnp.einsum('pbsh,pbshd->bshd', wts, jnp.stack(outs, axis=0).astype(jnp.float32))
    return out.astype(zq.dtype).reshape(b, s, H_B * HD)

def axial_rope(x, ang_row, ang_col):
    half = HD // 2
    return jnp.concatenate([apply_rope(x[..., :half], ang_row), apply_rope(x[..., half:], ang_col)], axis=-1)

def gqa_axial_mixer(zq, zk, zv, c_q_norm, c_k_norm, ang_row, ang_col):
    b, s, _ = zq.shape
    q = axial_rope(rms_norm(zq.reshape(b, s, H_C, HD), c_q_norm), ang_row, ang_col)
    k = axial_rope(rms_norm(zk.reshape(b, s, KV_C, HD), c_k_norm), ang_row, ang_col)
    v = zv.reshape(b, s, KV_C, HD)
    return block_attention(q.reshape(b, s, KV_C, H_C // KV_C, HD), k, v, HD ** -0.5)

def conv_gated_mlp(h, w_up, conv_w, conv_b, w_down):
    s = h.shape[1]
    u = h @ w_up
    half = CONV_W // 2
    up = jnp.pad(u, ((0, 0), (half, half), (0, 0)))
    c = conv_b
    for i in range(CONV_W):
        c = c + up[:, i:i + s] * conv_w[i]
    gate, val = jnp.split(c, 2, axis=-1)
    return (jax.nn.gelu(gate, approximate=True) * val) @ w_down

def trunk(x, rel_bias, norm_mix_pre, norm_mix_post, w_in, q_lora_norm, w_uq, kv_norm, w_ukv,
          c_q_norm, c_k_norm, w_out, norm_ffn_pre, norm_ffn_post, w_up, conv_w, conv_b, w_down):
    b, s, _ = x.shape
    rows = s // GRID_W
    ang_a = rope_angles(jnp.arange(s), ROPE_A // 2)
    row_ids = jnp.repeat(jnp.arange(rows), GRID_W)
    col_ids = jnp.tile(jnp.arange(GRID_W), rows)
    ang_row = rope_angles(row_ids, HD // 4)
    ang_col = rope_angles(col_ids, HD // 4)
    splits = [int(c) for c in np.cumsum(IN_SIZES)[:-1]]
    for l in range(DEPTH):
        h = rms_norm(x, norm_mix_pre[l])
        z = h @ w_in[l]
        a_q, a_kv, a_kr, b_q, b_k, b_v, c_q, c_k, c_v = jnp.split(z, splits, axis=-1)
        oa = mla_mixer(a_q, a_kv, a_kr, q_lora_norm[l], w_uq[l], kv_norm[l], w_ukv[l], ang_a)
        ob = dilated_mixer(b_q, b_k, b_v, rel_bias)
        oc = gqa_axial_mixer(c_q, c_k, c_v, c_q_norm[l], c_k_norm[l], ang_row, ang_col)
        mix = jnp.concatenate([oa, ob, oc], axis=-1) @ w_out[l]
        x = x + rms_norm(mix, norm_mix_post[l])
        h = rms_norm(x, norm_ffn_pre[l])
        x = x + rms_norm(conv_gated_mlp(h, w_up[l], conv_w[l], conv_b[l], w_down[l]), norm_ffn_post[l])
    return x

def setup_inputs(seed: int = 0) -> dict:
    key = jax.random.key(seed)
    ks = jax.random.split(key, 20)
    f32 = jnp.float32

    def nrm(k, shape, scale):
        return jax.random.normal(k, shape, f32) * scale

    def gain(k, shape):
        return 1.0 + 0.05 * jax.random.normal(k, shape, f32)

    return {
        'x_prompt': nrm(ks[0], (BATCH, SEQ, D_MODEL), 1.0),
        'x_sample': nrm(ks[1], (DEC_BATCH, DEC_SEQ, D_MODEL), 1.0),
        'rel_bias': nrm(ks[2], (N_BUCKETS, H_B), 0.5),
        'norm_mix_pre': gain(ks[3], (DEPTH, D_MODEL)),
        'norm_mix_post': gain(ks[4], (DEPTH, D_MODEL)),
        'w_in': nrm(ks[5], (DEPTH, D_MODEL, N_IN), D_MODEL ** -0.5),
        'q_lora_norm': gain(ks[6], (DEPTH, Q_LORA)),
        'w_uq': nrm(ks[7], (DEPTH, Q_LORA, H_A * (NOPE_A + ROPE_A)), Q_LORA ** -0.5),
        'kv_norm': gain(ks[8], (DEPTH, KV_LORA)),
        'w_ukv': nrm(ks[9], (DEPTH, KV_LORA, H_A * (NOPE_A + V_A)), KV_LORA ** -0.5),
        'c_q_norm': gain(ks[10], (DEPTH, HD)),
        'c_k_norm': gain(ks[11], (DEPTH, HD)),
        'w_out': nrm(ks[12], (DEPTH, D_MIX, D_MODEL), D_MIX ** -0.5),
        'norm_ffn_pre': gain(ks[13], (DEPTH, D_MODEL)),
        'norm_ffn_post': gain(ks[14], (DEPTH, D_MODEL)),
        'w_up': nrm(ks[15], (DEPTH, D_MODEL, 2 * D_FF), D_MODEL ** -0.5),
        'conv_w': nrm(ks[16], (DEPTH, CONV_W, 2 * D_FF), CONV_W ** -0.5),
        'conv_b': nrm(ks[17], (DEPTH, 2 * D_FF), 0.01),
        'w_down': nrm(ks[18], (DEPTH, D_FF, D_MODEL), D_FF ** -0.5),
    }

def reference(x_prompt, x_sample, rel_bias, norm_mix_pre, norm_mix_post, w_in, q_lora_norm, w_uq, kv_norm,
              w_ukv, c_q_norm, c_k_norm, w_out, norm_ffn_pre, norm_ffn_post, w_up, conv_w, conv_b, w_down):
    y_prompt = trunk(x_prompt, rel_bias, norm_mix_pre, norm_mix_post, w_in, q_lora_norm, w_uq, kv_norm, w_ukv,
                     c_q_norm, c_k_norm, w_out, norm_ffn_pre, norm_ffn_post, w_up, conv_w, conv_b, w_down)
    y_sample = trunk(x_sample, rel_bias, norm_mix_pre, norm_mix_post, w_in, q_lora_norm, w_uq, kv_norm, w_ukv,
                     c_q_norm, c_k_norm, w_out, norm_ffn_pre, norm_ffn_post, w_up, conv_w, conv_b, w_down)
    return (y_prompt, y_sample)


_drawn_inputs = setup_inputs


def setup_inputs(seed=0):
    import zlib

    import numpy as np

    out = dict(_drawn_inputs(seed))
    spreads = {}
    factors = {'conv_b': 4.592}
    for name, (base, spread) in spreads.items():
        noise = np.random.default_rng([zlib.crc32(name.encode()), seed]).standard_normal(out[name].shape)
        drawn = base * np.exp(spread * noise) if base else spread * noise
        out[name] = __import__('jax').numpy.asarray(drawn.astype(out[name].dtype))
    for name, factor in factors.items():
        out[name] = (out[name] * factor).astype(out[name].dtype)
    return out
```

```python
import math
from contextlib import ExitStack

import numpy as np

import concourse.bass as bass
from concourse import mybir
from concourse.alu_op_type import AluOpType as ALU

F32 = mybir.dt.float32
F32R = mybir.dt.float32r
ACT = mybir.ActivationFunctionType
AX = mybir.AxisListType

P = 128
D = 1024
DEPTH = 2
SEGS = ((0, 1024), (1024, 256))
T = 1280
BLOCKS = ((0, 512), (512, 512), (1024, 256))
KC = D // P
NT = T // P
H_A, H_B, H_C = 4, 4, 8
HEADS = H_A + H_B + H_C
D_FF = 2816
FF_PAIRS = D_FF // (2 * P)
EPS = 1e-6
MASKED = -1e30
N_DIST = 2048
GW = 1920
LOG_SET = "natural_log_exp_and_others"

QAN, QAR, KAN, KAR, VA = 0, 256, 384, 640, 672
QB, KB, VB = 928, 1184, 1440
QC, KC_ROW, VC = 1696, 2208, 2336
Z_ROWS = 2464

G_MIX_PRE, G_MIX_POST, G_FFN_PRE, G_FFN_POST, G_QL, G_KV, G_CQ, G_CK, N_GAINS = 0, 8, 16, 24, 32, 34, 35, 36, 37


class Ctx:
    pass


def place_buffers(nc, c):
    at = [(nc.sbuf_base + 31) // 32 * 32]

    def take(name, shape, dt=F32):
        t = nc.alloc_sbuf_tensor_at(name, shape, dt, offset=at[0])
        at[0] += 4 * int(np.prod(shape[1:]))
        at[0] = (at[0] + 31) // 32 * 32
        return t

    c.ident = take("ident", [P, P])
    c.ident_r = take("ident_r", [P, P], F32R)
    c.ones = take("ones", [P, P])
    c.block_ones = take("block_ones", [P, P])
    c.perm_c = take("perm_c", [P, P])
    c.perm_a = take("perm_a", [P, P])
    c.gain = take("gain", [P, N_GAINS])
    c.conv = take("conv", [P, 4, 2 * D_FF // P])
    c.eps = take("eps", [P, 1])
    h_at = at[0]
    c.hh = take("hh", [P, KC, T], F32R)
    c.hl = take("hl", [P, KC, T], F32R)
    c.raw = [take(f"raw{i}", [P, KC, P]) for i in range(2)]
    c.wh = [take(f"wh{i}", [P, KC, P], F32R) for i in range(2)]
    c.wl = [take(f"wl{i}", [P, KC, P], F32R) for i in range(2)]
    arena = at[0]
    end = nc.sbuf_usable_end

    c.y = take("y", [P, KC, T])
    after_y = at[0]
    c.r = take("r", [P, T])
    c.lnt = take("lnt", [P, T])
    c.sq = [take(f"sq{i}", [P, 512]) for i in range(4)]
    c.tmp = [take(f"tmp{i}", [P, 512]) for i in range(4)]
    c.xo = [take(f"xo{i}", [P, 512]) for i in range(4)]
    at[0] = after_y
    c.tok = [take(f"tok{i}", [P, D]) for i in range(4)]
    at[0] = after_y
    c.gain_rows = take("gain_rows", [N_GAINS, P])
    c.conv_rows = take("conv_rows", [2 * D_FF // P, 4, P])
    at[0] = after_y
    c.onehot = take("onehot", [32, N_DIST])
    c.logc = take("logc", [4, N_DIST])
    c.line = take("line", [4, N_DIST])
    c.rel = take("rel", [32, H_B])
    at[0] = arena
    c.stage = [take(f"stage{i}", [P, T]) for i in range(3)]
    c.pr = take("pr", [P, T])
    c.cos = take("cos", [P, T])
    c.sin = take("sin", [P, T])
    c.psq = [take(f"psq{i}", [P, T]) for i in range(2)]
    c.pln = take("pln", [P, T])
    after_common = at[0]
    c.lat = [take(f"lat{i}", [P, T]) for i in range(3)]
    c.lath = take("lath", [P, 3, T], F32R)
    c.latl = take("latl", [P, 3, T], F32R)
    assert at[0] <= end
    at[0] = after_common
    c.rot = [take(f"rot{i}", [P, T]) for i in range(2)]
    c.st2 = [take(f"st2_{i}", [P, T]) for i in range(2)]
    at[0] = arena
    c.q1 = [take(f"q1_{i}", [P, T], F32R) for i in range(2)]
    c.q2 = [take(f"q2_{i}", [P, T], F32R) for i in range(2)]
    c.k1 = [take(f"k1_{i}", [P, T], F32R) for i in range(2)]
    c.k2 = [take(f"k2_{i}", [P, T], F32R) for i in range(2)]
    c.rq = take("rq", [P, T])
    c.rk = take("rk", [P, T])
    c.vt = take("vt", [P, T])
    c.vh = [take(f"vh{i}", [P, NT, P], F32R) for i in range(2)]
    c.vl = [take(f"vl{i}", [P, NT, P], F32R) for i in range(2)]
    c.p = [take(f"p{i}", [P, 512]) for i in range(3)]
    c.ph = [take(f"ph{i}", [P, 512], F32R) for i in range(3)]
    c.pl = [take(f"pl{i}", [P, 512], F32R) for i in range(3)]
    c.ln_den = take("ln_den", [P, 512])
    c.rden = take("rden", [P, 512])
    c.ot = take("ot", [P, 512])
    c.mx = take("mx", [P, 8, 2])
    c.m = take("m", [P, NT])
    assert at[0] <= end, (at[0], end)
    chunk = 4 * T
    c.graw = [nc.alloc_sbuf_tensor_at(f"graw{i}", [P, GW // 2], F32, offset=h_at + (8 * i + 4) * chunk) for i in range(2)]
    c.gh = [nc.alloc_sbuf_tensor_at(f"gh{i}", [P, GW], F32R, offset=h_at + (8 * i + 5) * chunk) for i in range(2)]
    c.gl = [nc.alloc_sbuf_tensor_at(f"gl{i}", [P, GW], F32R, offset=h_at + (8 * i + 5) * chunk + 4 * GW) for i in range(2)]
    at[0] = after_y
    c.ah = take("ah", [P, 2, T], F32R)
    c.al = take("al", [P, 2, T], F32R)
    c.cb = [take(f"cb{i}", [P, T]) for i in range(4)]
    c.wh.append(take("wh2", [P, KC, P], F32R))
    c.wl.append(take("wl2", [P, KC, P], F32R))
    assert at[0] <= end, (at[0], end)
    c.ps = nc.alloc_psum_tensor("ps", [P, 8 * 512], F32)


def bank(c, b, w=512, rows=slice(0, P), off=0):
    return c.ps[rows, b * 512 + off:b * 512 + off + w]



def end_phase(nc, sems):
    nums = [s.num for s in sems]
    nc.multi_engine_barrier(list(nc.engines), sems_to_clear=range(min(nums), max(nums) + 1))


def product(pe, c, out, b, pairs):
    for k, (wh, wl, xh, xl) in enumerate(pairs):
        pe.matmul(out, wh, xh, start=(k == 0), stop=False)
        pe.matmul(out, wh, xl, start=False, stop=False)
        last = pe.matmul(out, wl, xh, start=False, stop=(k == len(pairs) - 1))
    return last


def project(pe, c, slot, half):
    for b, (t0, w) in enumerate(BLOCKS):
        last = product(pe, c, bank(c, 3 * half + b, w), b,
                       [(c.wh[slot][:, k, :], c.wl[slot][:, k, :], c.hh[:, k, t0:t0 + w], c.hl[:, k, t0:t0 + w])
                        for k in range(KC)])
    return last


def unit_psum(c, half, t0=0, t1=T, rows=slice(0, P)):
    return c.ps[rows, half * 1536 + t0:half * 1536 + t1]



def build_tables(nc, c):
    with ExitStack() as ex:
        def sem(name):
            return ex.enter_context(nc.semaphore(name))
        loaded, products, added, stored, const = sem("loaded"), sem("products"), sem("added"), sem("stored"), sem("const")
        with nc.Block() as block:
            @block.sync
            def _(sp):
                for dst, src in ((c.onehot[:], c.d_onehot), (c.logc[:], c.d_logc), (c.rel[:], c.rel_bias),
                                 (c.ident[:], c.d_ident), (c.ones[:], c.d_ones), (c.block_ones[:], c.d_block_ones),
                                 (c.perm_c[:], c.d_perm_c), (c.perm_a[:], c.d_perm_a)):
                    sp.dma_start(dst, src).then_inc(loaded, 16)
                sp.wait_ge(added, 4)
                sp.dma_start(c.s_line, c.line[:]).then_inc(stored, 16)
                sp.wait_ge(stored, 16)
                for h in range(H_B):
                    sp.dma_start(c.s_lines[h], bass.AP(tensor=c.s_line.tensor, offset=h * N_DIST, ap=[[0, P], [1, N_DIST]])).then_inc(stored, 16)
                sp.wait_ge(stored, 16 * (1 + H_B))

            @block.tensor
            def _(pe):
                pe.wait_ge(loaded, 16 * 8)
                for j in range(4):
                    pe.matmul(bank(c, j, rows=slice(0, H_B)), c.rel[:], c.onehot[:, 512 * j:512 * j + 512],
                              start=True, stop=True).then_inc(products, 1)

            @block.vector
            def _(dve):
                dve.memset(c.eps[:], EPS).then_inc(const, 1)
                for j in range(4):
                    dve.wait_ge(products, j + 1)
                    sl = slice(512 * j, 512 * j + 512)
                    dve.tensor_tensor(c.line[:, sl], bank(c, j, rows=slice(0, H_B)), c.logc[:, sl], ALU.add).then_inc(added, 1)
                dve.tensor_copy(c.ident_r[:], c.ident[:]).then_inc(const, 1)
        end_phase(nc, [loaded, products, added, stored, const])



def turn_input(nc, c):
    with ExitStack() as ex:
        def sem(name):
            return ex.enter_context(nc.semaphore(name))
        arrived = [sem(f"arrived{i}") for i in range(4)]
        turned, copied, stored = sem("turned"), sem("copied"), sem("stored")
        with nc.Block() as block:
            @block.sync
            def _(sp):
                for t in range(NT):
                    if t >= 4:
                        sp.wait_ge(turned, 2 * (t - 3))
                    src = c.x_prompt[0, t * P:(t + 1) * P, :] if t < 8 else c.x_sample[0, (t - 8) * P:(t - 7) * P, :]
                    sp.dma_start(c.tok[t % 4][:], src).then_inc(arrived[t % 4], 16)
                sp.wait_ge(copied, 2 * NT)
                sp.dma_start(c.s_x, c.y[:]).then_inc(stored, 16)
                sp.wait_ge(stored, 16)

            @block.tensor
            def _(pe):
                for t in range(NT):
                    pe.wait_ge(arrived[t % 4], 16 * (t // 4 + 1))
                    for g in range(2):
                        n = 2 * t + g
                        if n >= 8:
                            pe.wait_ge(copied, n - 7)
                        for j in range(4):
                            last = pe.transpose(bank(c, n % 8, P, off=j * P), c.tok[t % 4][:, (4 * g + j) * P:(4 * g + j + 1) * P],
                                                c.ident[:])
                        last.then_inc(turned, 1)

            @block.vector
            def _(dve):
                for n in range(2 * NT):
                    t, g = n // 2, n % 2
                    dve.wait_ge(turned, n + 1)
                    dve.tensor_copy(c.y[:, 4 * g:4 * g + 4, t * P:(t + 1) * P],
                                    bank(c, n % 8).rearrange("p (k t) -> p k t", k=4)).then_inc(copied, 1)
        end_phase(nc, arrived + [turned, copied, stored])


def turn_output(nc, c):
    with ExitStack() as ex:
        def sem(name):
            return ex.enter_context(nc.semaphore(name))
        stored = [sem(f"stored{i}") for i in range(4)]
        turned, copied = sem("turned"), sem("copied")
        with nc.Block() as block:
            @block.tensor
            def _(pe):
                for n in range(2 * NT):
                    t, g = n // 2, n % 2
                    if n >= 8:
                        pe.wait_ge(copied, n - 7)
                    for j in range(4):
                        last = pe.transpose(bank(c, n % 8, P, off=j * P), c.y[:, 4 * g + j, t * P:(t + 1) * P], c.ident[:])
                    last.then_inc(turned, 1)

            @block.vector
            def _(dve):
                for n in range(2 * NT):
                    t, g = n // 2, n % 2
                    if t >= 4 and g == 0:
                        dve.wait_ge(stored[t % 4], 16 * (t // 4))
                    dve.wait_ge(turned, n + 1)
                    dve.tensor_copy(c.tok[t % 4][:, 512 * g:512 * g + 512], bank(c, n % 8)).then_inc(copied, 1)

            @block.sync
            def _(sp):
                for t in range(NT):
                    sp.wait_ge(copied, 2 * t + 2)
                    dst = c.y_prompt[0, t * P:(t + 1) * P, :] if t < 8 else c.y_sample[0, (t - 8) * P:(t - 7) * P, :]
                    sp.dma_start(dst, c.tok[t % 4][:]).then_inc(stored[t % 4], 16)
                for i in range(4):
                    sp.wait_ge(stored[i], 16 * ((NT - 1 - i) // 4 + 1))
        end_phase(nc, stored + [turned, copied])


def load_params(nc, c, L):
    with ExitStack() as ex:
        def sem(name):
            return ex.enter_context(nc.semaphore(name))
        loaded, turned, copied = sem("loaded"), sem("turned"), sem("copied")
        nj = 2 * D_FF // P
        with nc.Block() as block:
            @block.sync
            def _(sp):
                n = 0
                for ap, row, rows in ((c.norm_mix_pre, G_MIX_PRE, 8), (c.norm_mix_post, G_MIX_POST, 8),
                                      (c.norm_ffn_pre, G_FFN_PRE, 8), (c.norm_ffn_post, G_FFN_POST, 8),
                                      (c.q_lora_norm, G_QL, 2), (c.kv_norm, G_KV, 1)):
                    sp.dma_start(c.gain_rows[row:row + rows, :],
                                 ap[bass.ds(L, 1), :].rearrange("a (r p) -> (a r) p", p=P)).then_inc(loaded, 16)
                for ap, row in ((c.c_q_norm, G_CQ), (c.c_k_norm, G_CK)):
                    for half in range(2):
                        sp.dma_start(c.gain_rows[row:row + 1, 64 * half:64 * half + 64], ap[bass.ds(L, 1), :]).then_inc(loaded, 16)
                for t in range(3):
                    sp.dma_start(c.conv_rows[:, t, :], c.conv_w[bass.ds(L, 1), t, :].rearrange("a (j p) -> (a j) p", p=P)).then_inc(loaded, 16)
                sp.dma_start(c.conv_rows[:, 3, :], c.conv_b[bass.ds(L, 1), :].rearrange("a (j p) -> (a j) p", p=P)).then_inc(loaded, 16)

            @block.tensor
            def _(pe):
                pe.wait_ge(loaded, 16 * 14)
                pe.transpose(bank(c, 0, N_GAINS), c.gain_rows[:], c.ident[0:N_GAINS, 0:N_GAINS]).then_inc(turned, 1)
                for t in range(4):
                    last = pe.transpose(bank(c, 1, nj, off=t * nj), c.conv_rows[:, t, :], c.ident[0:nj, 0:nj])
                last.then_inc(turned, 1)

            @block.vector
            def _(dve):
                dve.wait_ge(turned, 1)
                dve.tensor_copy(c.gain[:], bank(c, 0, N_GAINS)).then_inc(copied, 1)
                dve.wait_ge(turned, 2)
                dve.tensor_copy(c.conv[:], bank(c, 1, 4 * nj).rearrange("p (t j) -> p t j", t=4)).then_inc(copied, 1)
        end_phase(nc, [loaded, turned, copied])



def norm(nc, c, gain, post):
    items = [(b, t0, w, k) for b, (t0, w) in enumerate(BLOCKS) for k in range(KC)]
    with ExitStack() as ex:
        def sem(name):
            return ex.enter_context(nc.semaphore(name))
        squared, summed, logged, root = sem("squared"), sem("summed"), sem("logged"), sem("root")
        scaled, hi_done, done = sem("scaled"), sem("hi_done"), sem("done")
        old = [sem(f"old{i}") for i in range(4)]
        stored = sem("stored")
        with nc.Block() as block:
            @block.tensor
            def _(pe):
                for n, (b, t0, w, k) in enumerate(items):
                    pe.wait_ge(squared, n + 1)
                    if b == 2 and k == 0:
                        pe.wait_ge(logged, 1)
                    pe.matmul(bank(c, 6 + b % 2, w), c.ones[:], c.sq[n % 4][:, 0:w], start=(k == 0),
                              stop=(k == KC - 1)).then_inc(summed, 1)

            @block.scalar
            def _(act):
                act.preload_act_table_set(LOG_SET)
                def squares(b):
                    for n, (bb, t0, w, k) in enumerate(items):
                        if bb == b:
                            if n >= 4:
                                act.wait_ge(summed, n - 3)
                            act.activation(c.sq[n % 4][:, 0:w], c.y[:, k, t0:t0 + w], ACT.Square).then_inc(squared, 1)

                squares(0)
                for b, (t0, w) in enumerate(BLOCKS):
                    if b < 2:
                        squares(b + 1)
                    act.wait_ge(summed, KC * (b + 1))
                    act.activation(c.lnt[:, t0:t0 + w], bank(c, 6 + b % 2, w), ACT.Ln, scale=1.0 / D, bias=c.eps[:]).then_inc(logged, 1)
                    act.wait_ge(logged, b + 1)
                    act.activation(c.r[:, t0:t0 + w], c.lnt[:, t0:t0 + w], ACT.Exp, scale=-0.5).then_inc(root, 1)
                    if not post:
                        for n, (bb, _, _, k) in enumerate(items):
                            if bb == b:
                                act.wait_ge(scaled, n + 1)
                                act.activation(c.hh[:, k, t0:t0 + w], c.tmp[n % 4][:, 0:w], ACT.Copy).then_inc(hi_done, 1)

            @block.vector
            def _(dve):
                for n, (b, t0, w, k) in enumerate(items):
                    if k == 0:
                        dve.wait_ge(root, b + 1)
                    if n >= 4:
                        dve.wait_ge(done, n - 3)
                    dve.scalar_tensor_tensor(out=c.tmp[n % 4][:, 0:w], in0=c.y[:, k, t0:t0 + w], scalar=c.gain[:, gain + k:gain + k + 1],
                                             in1=c.r[:, t0:t0 + w], op0=ALU.mult, op1=ALU.mult).then_inc(scaled, 1)

            @block.gpsimd
            def _(pool):
                for n, (b, t0, w, k) in enumerate(items):
                    tmp = c.tmp[n % 4][:, 0:w]
                    if post:
                        pool.wait_ge(scaled, n + 1)
                        pool.wait_ge(old[n % 4], 16 * (n // 4 + 1))
                        pool.tensor_tensor(c.y[:, k, t0:t0 + w], tmp, c.xo[n % 4][:, 0:w], ALU.add).then_inc(done, 1)
                    else:
                        pool.wait_ge(hi_done, n + 1)
                        pool.tensor_tensor(c.hl[:, k, t0:t0 + w], tmp, c.hh[:, k, t0:t0 + w].bitcast(F32), ALU.subtract).then_inc(done, 1)

            if post:
                @block.sync
                def _(sp):
                    def store(n):
                        b, t0, w, k = items[n]
                        sp.wait_ge(done, n + 1)
                        sp.dma_start(c.s_x[:, k, t0:t0 + w], c.y[:, k, t0:t0 + w]).then_inc(stored, 16)

                    for n, (b, t0, w, k) in enumerate(items):
                        if n >= 4:
                            store(n - 4)
                        sp.dma_start(c.xo[n % 4][:, 0:w], c.s_x[:, k, t0:t0 + w]).then_inc(old[n % 4], 16)
                    for n in range(len(items) - 4, len(items)):
                        store(n)
                    sp.wait_ge(stored, 16 * len(items))
        end_phase(nc, [squared, summed, logged, root, scaled, hi_done, done] + old + [stored])



def w_in_chunk(c, L, col):
    return c.w_in[bass.ds(L, 1), :, col:col + P].rearrange("a (k p) n -> p (a k) n", p=P)


def load_weights(sp, c, n, dst, src, raw_arrived, w_lo):
    if n >= 2:
        sp.wait_ge(w_lo, n - 1)
    sp.dma_start(dst, src).then_inc(raw_arrived[n % 2], 16)


def split_hi(act, c, n, raw_arrived, w_used, w_hi, part=lambda t: t[:], arrivals=None):
    act.wait_ge(raw_arrived[n % 2], 16 * (arrivals or n // 2 + 1))
    if n >= 2:
        act.wait_ge(w_used, n - 1)
    act.activation(part(c.wh[n % 2]), part(c.raw[n % 2]), ACT.Copy).then_inc(w_hi, 1)


def split_lo(pool, c, n, w_hi, w_lo, part=lambda t: t[:]):
    pool.wait_ge(w_hi, n + 1)
    pool.tensor_tensor(part(c.wl[n % 2]), part(c.raw[n % 2]), part(c.wh[n % 2]).bitcast(F32), ALU.subtract).then_inc(w_lo, 1)


def latent_projections(nc, c, L):
    HQ, HV = 96, 128
    wide = {4: lambda t: t[:].rearrange("p k n -> p (k n)")[:, 0:2 * H_A * HQ],
            5: lambda t: t[:].rearrange("p k n -> p (k n)")[:, 0:H_A * HV]}
    outs = [(4, 0, (0, 1), QAR), (4, P, (0, 1), QAN), (4, 2 * P, (0, 1), QAN + P),
            (5, 0, (2,), KAN), (5, P, (2,), KAN + P), (5, 2 * P, (2,), VA), (5, 3 * P, (2,), VA + P)]
    with ExitStack() as ex:
        def sem(name):
            return ex.enter_context(nc.semaphore(name))
        raw_arrived = [sem("raw_arrived0"), sem("raw_arrived1")]
        w_hi, w_lo, w_used = sem("w_hi"), sem("w_lo"), sem("w_used")
        tables, unit_done, evacuated, squared = sem("tables"), sem("unit_done"), sem("evacuated"), sem("squared")
        aux_done, aux_read_act, aux_read_dve = sem("aux_done"), sem("aux_read_act"), sem("aux_read_dve")
        root, normed, lat_hi, lat_lo = sem("root"), sem("normed"), sem("lat_hi"), sem("lat_lo")
        cos_done, roped = sem("cos_done"), sem("roped")
        stored = [sem(f"stored{i}") for i in range(3)]
        with nc.Block() as block:
            @block.sync
            def _(sp):
                sp.dma_start(c.cos[:], c.d_cos_a).then_inc(tables, 16)
                sp.dma_start(c.sin[:], c.d_sin_a).then_inc(tables, 16)
                for n in range(4):
                    load_weights(sp, c, n, c.raw[n % 2][:], w_in_chunk(c, L, P * n), raw_arrived, w_lo)
                sp.wait_ge(w_lo, 3)
                for k in range(2):
                    src = c.w_uq[bass.ds(L, 1), k * P:k * P + P, :].rearrange("a p (h n) -> (a p) h n", h=H_A)
                    dst = wide[4](c.raw[0]).rearrange("p (k n) -> p k n", k=2)[:, k, :]
                    sp.dma_start(dst[:, 0:P].rearrange("p (h n) -> p h n", h=H_A), src[:, :, 64:96]).then_inc(raw_arrived[0], 16)
                    sp.dma_start(dst[:, P:3 * P].rearrange("p (h n) -> p h n", h=H_A), src[:, :, 0:64]).then_inc(raw_arrived[0], 16)
                sp.wait_ge(w_lo, 4)
                src = c.w_ukv[bass.ds(L, 1), :, :].rearrange("a p (h n) -> (a p) h n", h=H_A)
                for part in range(2):
                    dst = wide[5](c.raw[1])[:, 256 * part:256 * part + 256].rearrange("p (h n) -> p h n", h=H_A)
                    sp.dma_start(dst, src[:, :, 64 * part:64 * part + 64]).then_inc(raw_arrived[1], 16)
                sp.wait_ge(roped, 1)
                sp.dma_start(c.s_z[KAR:KAR + 32, :], c.stage[0][0:32, :]).then_inc(stored[0], 16)
                sp.wait_ge(roped, 2)
                sp.dma_start(c.s_z[QAR:QAR + P, :], c.stage[1][:]).then_inc(stored[1], 16)
                for j in range(2, 8):
                    sp.wait_ge(evacuated, 4 + j)
                    row = outs[j - 1][3]
                    sp.dma_start(c.s_z[row:row + P, :], c.stage[j % 3][:]).then_inc(stored[j % 3], 16)
                for i in range(3):
                    sp.wait_ge(stored[i], 16 * ((7 - i) // 3 + 1))

            @block.tensor
            def _(pe):
                def aux(x, lhs_rhs, rows, w):
                    if 2 <= x < 8:
                        pe.wait_ge(aux_read_act, x - 1)
                    elif x >= 8:
                        pe.wait_ge(aux_read_dve, x - 7)
                    for k, (lhs, rhs) in enumerate(lhs_rhs):
                        last = pe.matmul(bank(c, 6 + x % 2, w, rows), lhs, rhs, start=(k == 0), stop=(k == len(lhs_rhs) - 1))
                    last.then_inc(aux_done, 1)

                for n in range(3):
                    pe.wait_ge(w_lo, n + 1)
                    if n >= 2:
                        pe.wait_ge(evacuated, n - 1)
                    last = project(pe, c, n % 2, n % 2)
                    last.then_inc(w_used, 1)
                pe.wait_ge(squared, 2)
                for b, (t0, w) in enumerate(BLOCKS):
                    aux(b, [(c.ones[:], c.psq[i][:, t0:t0 + w]) for i in range(2)], slice(0, P), w)
                pe.wait_ge(w_lo, 4)
                pe.wait_ge(evacuated, 2)
                project(pe, c, 1, 1).then_inc(w_used, 1)
                pe.wait_ge(squared, 3)
                for b, (t0, w) in enumerate(BLOCKS):
                    aux(3 + b, [(c.ones[:], c.psq[0][:, t0:t0 + w])], slice(0, P), w)
                pe.wait_ge(evacuated, 4)
                for b, (t0, w) in enumerate(BLOCKS):
                    aux(6 + b, [(c.perm_a[0:32, 0:32], c.stage[0][0:32, t0:t0 + w])], slice(0, 32), w)
                for j, (unit, col, chunks, row) in enumerate(outs):
                    m = 4 + j
                    pe.wait_ge(w_lo, unit + 1)
                    pe.wait_ge(lat_lo, 1 + max(chunks))
                    pe.wait_ge(evacuated, m - 1)
                    row_len = H_A * (HQ if unit == 4 else HV)
                    pairs = [tuple(wide[unit](t[unit % 2])[:, i * row_len + col:i * row_len + col + P] for t in (c.wh, c.wl)) + (k,)
                             for i, k in enumerate(chunks)]
                    for b, (t0, w) in enumerate(BLOCKS):
                        last = product(pe, c, bank(c, 3 * (m % 2) + b, w), b,
                                       [(wh, wl, c.lath[:, k, t0:t0 + w], c.latl[:, k, t0:t0 + w]) for wh, wl, k in pairs])
                    last.then_inc(unit_done, 1)
                    if j == 0:
                        continue
                    if j == 1:
                        pe.wait_ge(evacuated, 5)
                        for b, (t0, w) in enumerate(BLOCKS):
                            aux(9 + b, [(c.perm_a[:], c.stage[1][:, t0:t0 + w])], slice(0, P), w)

            @block.scalar
            def _(act):
                act.preload_act_table_set(LOG_SET)
                def sums(x, b, width):
                    t0, w = BLOCKS[b]
                    act.wait_ge(aux_done, x + 1)
                    if x == 3:
                        act.wait_ge(normed, 2)
                    act.activation(c.pln[:, t0:t0 + w], bank(c, 6 + x % 2, w), ACT.Ln, scale=1.0 / width, bias=c.eps[:]).then_inc(aux_read_act, 1)
                    act.wait_ge(aux_read_act, x + 1)
                    act.activation(c.pr[:, t0:t0 + w], c.pln[:, t0:t0 + w], ACT.Exp, scale=-0.5).then_inc(root, 1)

                split_hi(act, c, 0, raw_arrived, w_used, w_hi)
                split_hi(act, c, 1, raw_arrived, w_used, w_hi)
                for n in range(3):
                    if n == 2:
                        for b in range(3):
                            sums(b, b, 256)
                    act.wait_ge(w_used, n + 1)
                    if n == 2:
                        act.wait_ge(aux_done, 3)
                    act.activation(c.psq[n % 2][:], unit_psum(c, n % 2), ACT.Square).then_inc(squared, 1)
                    act.activation(c.lat[n][:], unit_psum(c, n % 2), ACT.Copy).then_inc(evacuated, 1)
                    if n < 2:
                        split_hi(act, c, n + 2, raw_arrived, w_used, w_hi)
                split_hi(act, c, 4, raw_arrived, w_used, w_hi, wide[4], 6)
                act.wait_ge(w_used, 4)
                act.activation(c.stage[0][0:32, :], unit_psum(c, 1, rows=slice(0, 32)), ACT.Copy).then_inc(evacuated, 1)
                split_hi(act, c, 5, raw_arrived, w_used, w_hi, wide[5], 4)
                for i in range(2):
                    act.wait_ge(normed, i + 1)
                    act.activation(c.lath[:, i, :], c.lat[i][:], ACT.Copy).then_inc(lat_hi, 1)
                for b in range(3):
                    sums(3 + b, b, 128)
                act.wait_ge(normed, 3)
                act.activation(c.lath[:, 2, :], c.lat[2][:], ACT.Copy).then_inc(lat_hi, 1)
                for j in range(1, 8):
                    m = 3 + j
                    act.wait_ge(unit_done, j)
                    if j >= 3:
                        act.wait_ge(stored[j % 3], 16 * (j // 3))
                    act.activation(c.stage[j % 3][:], unit_psum(c, m % 2), ACT.Copy).then_inc(evacuated, 1)

            @block.gpsimd
            def _(pool):
                for n in range(4):
                    split_lo(pool, c, n, w_hi, w_lo)
                split_lo(pool, c, 4, w_hi, w_lo, wide[4])
                split_lo(pool, c, 5, w_hi, w_lo, wide[5])
                for i in range(2):
                    pool.wait_ge(lat_hi, i + 1)
                    pool.tensor_tensor(c.latl[:, i, :], c.lat[i][:], c.lath[:, i, :].bitcast(F32), ALU.subtract).then_inc(lat_lo, 1)
                pool.wait_ge(tables, 32)
                pool.wait_ge(evacuated, 4)
                pool.wait_ge(aux_done, 3)
                pool.tensor_tensor(c.psq[1][0:32, :], c.stage[0][0:32, :], c.cos[0:32, :], ALU.mult).then_inc(cos_done, 1)
                pool.wait_ge(lat_hi, 3)
                pool.tensor_tensor(c.latl[:, 2, :], c.lat[2][:], c.lath[:, 2, :].bitcast(F32), ALU.subtract).then_inc(lat_lo, 1)
                pool.wait_ge(evacuated, 5)
                pool.wait_ge(roped, 1)
                pool.tensor_tensor(c.psq[1][:], c.stage[1][:], c.cos[:], ALU.mult).then_inc(cos_done, 1)

            @block.vector
            def _(dve):
                def scale_latent(i, gain):
                    dve.scalar_tensor_tensor(out=c.lat[i][:], in0=c.lat[i][:], scalar=c.gain[:, gain:gain + 1], in1=c.pr[:],
                                             op0=ALU.mult, op1=ALU.mult).then_inc(normed, 1)

                def rope(x0, rows, r, j):
                    for b, (t0, w) in enumerate(BLOCKS):
                        dve.wait_ge(aux_done, x0 + b + 1)
                        dve.tensor_tensor(c.psq[0][rows, t0:t0 + w], bank(c, 6 + (x0 + b) % 2, w, rows), c.sin[rows, t0:t0 + w],
                                          ALU.mult).then_inc(aux_read_dve, 1)
                    dve.wait_ge(aux_read_dve, x0 + 3 - 6)
                    dve.wait_ge(cos_done, r + 1)
                    dve.tensor_tensor(c.stage[j][rows, :], c.psq[0][rows, :], c.psq[1][rows, :], ALU.add).then_inc(roped, 1)

                dve.wait_ge(root, 3)
                dve.wait_ge(evacuated, 2)
                scale_latent(0, G_QL)
                scale_latent(1, G_QL + 1)
                dve.wait_ge(root, 6)
                dve.wait_ge(evacuated, 3)
                scale_latent(2, G_KV)
                dve.wait_ge(tables, 32)
                rope(6, slice(0, 32), 0, 0)
                dve.wait_ge(roped, 1)
                rope(9, slice(0, P), 1, 1)
        end_phase(nc, raw_arrived + [w_hi, w_lo, w_used, tables, unit_done, evacuated, squared, aux_done, aux_read_act,
                                     aux_read_dve, root, normed, lat_hi, lat_lo, cos_done, roped] + stored)


def head_projections(nc, c, L):
    UNITS = 12
    rows = [QB, QB + P, KB, KB + P, VB, VB + P, QC, QC + P, QC + 2 * P, QC + 3 * P, KC_ROW, VC]
    ROPED = range(6, 11)
    with ExitStack() as ex:
        def sem(name):
            return ex.enter_context(nc.semaphore(name))
        raw_arrived = [sem("raw_arrived0"), sem("raw_arrived1")]
        w_hi, w_lo, w_used = sem("w_hi"), sem("w_lo"), sem("w_used")
        tables, evacuated, squared, unit_sum, turned = sem("tables"), sem("evacuated"), sem("squared"), sem("unit_sum"), sem("turned")
        sum_read, turn_read, root, cos_done, added, roped = (sem("sum_read"), sem("turn_read"), sem("root"), sem("cos_done"),
                                                             sem("added"), sem("roped"))
        stored = [sem(f"stored{i}") for i in range(3)]
        with nc.Block() as block:
            @block.sync
            def _(sp):
                sp.dma_start(c.cos[:], c.d_cos_c).then_inc(tables, 16)
                sp.dma_start(c.sin[:], c.d_sin_c).then_inc(tables, 16)

                def store(n):
                    if n in ROPED:
                        sp.wait_ge(roped, n - 5)
                    else:
                        sp.wait_ge(evacuated, n + 1)
                    sp.dma_start(c.s_z[rows[n]:rows[n] + P, :], c.stage[n % 3][:]).then_inc(stored[n % 3], 16)

                for n in range(UNITS):
                    col = 416 + P * n if n < 6 else 1184 + P * (n - 6)
                    load_weights(sp, c, n, c.raw[n % 2][:], w_in_chunk(c, L, col), raw_arrived, w_lo)
                    if n >= 4:
                        store(n - 4)
                for n in range(UNITS - 4, UNITS):
                    store(n)
                for i in range(3):
                    sp.wait_ge(stored[i], 16 * 4)

            @block.tensor
            def _(pe):
                def norm_and_turn(n):
                    r = n - 6
                    pe.wait_ge(evacuated, n + 1)
                    for b, (t0, w) in enumerate(BLOCKS):
                        if 3 * r + b >= 1:
                            pe.wait_ge(sum_read, 3 * r + b)
                        pe.matmul(bank(c, 6, w), c.block_ones[:], c.psq[n % 2][:, t0:t0 + w], start=True, stop=True).then_inc(unit_sum, 1)
                        if 3 * r + b >= 1:
                            pe.wait_ge(turn_read, 3 * r + b)
                        pe.matmul(bank(c, 7, w), c.perm_c[:], c.stage[n % 3][:, t0:t0 + w], start=True, stop=True).then_inc(turned, 1)

                for n in range(UNITS):
                    pe.wait_ge(w_lo, n + 1)
                    if n >= 2:
                        pe.wait_ge(evacuated, n - 1)
                    project(pe, c, n % 2, n % 2).then_inc(w_used, 1)
                    if n - 1 in ROPED:
                        norm_and_turn(n - 1)

            @block.scalar
            def _(act):
                act.preload_act_table_set(LOG_SET)
                def roots(n):
                    r = n - 6
                    for b, (t0, w) in enumerate(BLOCKS):
                        x = 3 * r + b
                        act.wait_ge(unit_sum, x + 1)
                        if r >= 1:
                            act.wait_ge(roped, r)
                        act.activation(c.pln[:, t0:t0 + w], bank(c, 6, w), ACT.Ln, scale=1.0 / 64, bias=c.eps[:]).then_inc(sum_read, 1)
                        act.wait_ge(sum_read, x + 1)
                        act.activation(c.pr[:, t0:t0 + w], c.pln[:, t0:t0 + w], ACT.Exp, scale=-0.5).then_inc(root, 1)

                split_hi(act, c, 0, raw_arrived, w_used, w_hi)
                split_hi(act, c, 1, raw_arrived, w_used, w_hi)
                for n in range(UNITS):
                    act.wait_ge(w_used, n + 1)
                    if n >= 3:
                        act.wait_ge(stored[n % 3], 16 * (n // 3))
                    if n in ROPED:
                        if n >= 8:
                            act.wait_ge(unit_sum, 3 * (n - 7))
                        act.activation(c.psq[n % 2][:], unit_psum(c, n % 2), ACT.Square).then_inc(squared, 1)
                        g = G_CK if n == 10 else G_CQ
                        act.activation(c.stage[n % 3][:], unit_psum(c, n % 2), ACT.Identity, scale=c.gain[:, g:g + 1]).then_inc(evacuated, 1)
                    else:
                        act.activation(c.stage[n % 3][:], unit_psum(c, n % 2), ACT.Copy, scale=0.125 if n < 2 else 1.0).then_inc(evacuated, 1)
                    if n + 2 < UNITS:
                        split_hi(act, c, n + 2, raw_arrived, w_used, w_hi)
                    if n - 1 in ROPED:
                        roots(n - 1)

            @block.gpsimd
            def _(pool):
                split_lo(pool, c, 0, w_hi, w_lo)
                split_lo(pool, c, 1, w_hi, w_lo)
                pool.wait_ge(tables, 32)
                for n in range(UNITS):
                    if n + 2 < UNITS:
                        split_lo(pool, c, n + 2, w_hi, w_lo)
                    if n in ROPED:
                        pool.wait_ge(evacuated, n + 1)
                        if n >= 8:
                            pool.wait_ge(roped, n - 7)
                        pool.tensor_tensor(c.st2[n % 2][:], c.stage[n % 3][:], c.cos[:], ALU.mult).then_inc(cos_done, 1)

            @block.vector
            def _(dve):
                dve.wait_ge(tables, 32)
                for n in ROPED:
                    r = n - 6
                    rot = c.rot[n % 2]
                    for b, (t0, w) in enumerate(BLOCKS):
                        dve.wait_ge(turned, 3 * r + b + 1)
                        dve.tensor_tensor(rot[:, t0:t0 + w], bank(c, 7, w), c.sin[:, t0:t0 + w], ALU.mult).then_inc(turn_read, 1)
                    dve.wait_ge(turn_read, 3 * r + 3)
                    dve.wait_ge(cos_done, r + 1)
                    dve.tensor_tensor(rot[:], rot[:], c.st2[n % 2][:], ALU.add).then_inc(added, 1)
                    dve.wait_ge(added, r + 1)
                    dve.wait_ge(root, 3 * r + 3)
                    dve.tensor_tensor(c.stage[n % 3][:], rot[:], c.pr[:], ALU.mult).then_inc(roped, 1)
        end_phase(nc, raw_arrived + [w_hi, w_lo, w_used, tables, evacuated, squared, unit_sum, turned, sum_read, turn_read,
                                     root, cos_done, added, roped] + stored)



def attention(nc, c):
    STEPS = [(0, 512 * qb, 512, kt, kt == 0, kt == 7) for qb in range(2) for kt in range(8)] + \
            [(1, 1024, 256, 8 + kt, kt == 0, kt == 1) for kt in range(2)]
    NS = len(STEPS)
    MAXES = [(qt, 512 * kb, 512, kb) for qt in range(8) for kb in range(2)] + [(8, 1024, 256, 0), (9, 1024, 256, 0)]
    NM = len(MAXES)
    ROW_TILES = ((0, 4), (4, 8), (8, 10))
    MAX_FROM = 4
    SM, ST, OB, MISC = 0, 2, 5, 7
    PV_LAG = 2

    def kind(h):
        return "A" if h < 4 else "B" if h < 8 else "C"

    def kv(h):
        return h % 2 if h < 8 else (h - 8) // 4

    def new_kv(h):
        return h <= 8 or h == 12

    def kv_count(h):
        return sum(new_kv(i) for i in range(h + 1))

    def pl_engine(g):
        i = g % NS
        return "dve" if (i >= MAX_FROM + NM // 2 or i < 2) else "pool"

    def pl_count(g, who):
        return sum(pl_engine(x) == who for x in range(g + 1))

    STEP_SCALE = {"A": 96 ** -0.5, "B": 1.0, "C": 0.125}
    G_TOTAL = HEADS * NS

    with ExitStack() as ex:
        def sem(name):
            return ex.enter_context(nc.semaphore(name))
        q_raw, k_raw, v_raw, table_raw = sem("q_raw"), sem("k_raw"), sem("v_raw"), sem("table_raw")
        k_hi_low = sem("k_hi_low")
        consts, q_hi, k_hi, q_lo, k_lo, table_hi, table_lo = (sem("consts"), sem("q_hi"), sem("k_hi"), sem("q_lo"), sem("k_lo"),
                                                             sem("table_hi"), sem("table_lo"))
        v_turned, v_hi, v_lo = sem("v_turned"), sem("v_hi"), sem("v_lo")
        max_scored, max_taken, max_ready, row_turned, row_copied = (sem("max_scored"), sem("max_taken"), sem("max_ready"),
                                                                    sem("row_turned"), sem("row_copied"))
        scored, exp_done, hi_done, lo_pool, lo_dve, pv_done = (sem("scored"), sem("exp_done"), sem("hi_done"), sem("lo_pool"),
                                                               sem("lo_dve"), sem("pv_done"))
        ln_done, rden_done, scaled, out_hi, out_lo = sem("ln_done"), sem("rden_done"), sem("scaled"), sem("out_hi"), sem("out_lo")
        out_i = [(s[0], s[1], s[2]) for s in STEPS if s[4]]

        def last_step(o):
            return (o // 3) * NS + (7, 15, 17)[o % 3]

        with nc.Block() as block:
            @block.sync
            def _(sp):
                for h in range(HEADS):
                    if h >= 1:
                        sp.wait_ge(q_hi, h)
                        sp.wait_ge(q_lo, h)
                    if kind(h) == "A":
                        sp.dma_start(c.rq[0:64, :], c.s_z[QAN + 64 * h:QAN + 64 * h + 64, :]).then_inc(q_raw, 16)
                        sp.dma_start(c.rq[64:96, :], c.s_z[QAR + 32 * h:QAR + 32 * h + 32, :]).then_inc(q_raw, 16)
                    else:
                        row = QB + 64 * (h - 4) if h < 8 else QC + 64 * (h - 8)
                        for half in range(2):
                            sp.dma_start(c.rq[64 * half:64 * half + 64, :], c.s_z[row:row + 64, :]).then_inc(q_raw, 16)
                    if not new_kv(h):
                        continue
                    n = kv_count(h) - 1
                    if n >= 1:
                        sp.wait_ge(k_lo, n)
                        sp.wait_ge(v_turned, 2 * n)
                    if kind(h) == "A":
                        sp.dma_start(c.rk[0:64, :], c.s_z[KAN + 64 * h:KAN + 64 * h + 64, :]).then_inc(k_raw, 16)
                        sp.dma_start(c.rk[64:96, :], c.s_z[KAR:KAR + 32, :]).then_inc(k_raw, 16)
                        vrow = VA + 64 * h
                    else:
                        krow, vrow = (KB + 64 * (h - 4), VB + 64 * (h - 4)) if h < 8 else (KC_ROW + 64 * kv(h), VC + 64 * kv(h))
                        for half in range(2):
                            sp.dma_start(c.rk[64 * half:64 * half + 64, :], c.s_z[krow:krow + 64, :]).then_inc(k_raw, 16)
                    sp.dma_start(c.vt[0:64, :], c.s_z[vrow:vrow + 64, :]).then_inc(v_raw, 16)
                    if kind(h) == "B":
                        if h > 4:
                            sp.wait_ge(table_lo, 2 * (h - 4))
                        for i in range(2):
                            src = bass.AP(tensor=c.s_lines.tensor, offset=(h - 4) * P * N_DIST + P - 1 + i * GW // 2,
                                          ap=[[N_DIST - 1, P], [1, GW // 2]])
                            sp.dma_start(c.graw[i][:], src).then_inc(table_raw, 16)

            @block.tensor
            def _(pe):
                def scores(g):
                    h, i = divmod(g, NS)
                    seg, q0, w, kt, first, last = STEPS[i]
                    out = bank(c, ST + g % 3, w)
                    par, kp = h % 2, kv(h)
                    if g >= 3:
                        pe.wait_ge(exp_done, g - 2)
                    if i == 0:
                        pe.wait_ge(q_lo, h + 1)
                        pe.wait_ge(k_lo, kv_count(h))
                        if h == 0:
                            pe.wait_ge(consts, 6)
                        if h in (4, 5):
                            pe.wait_ge(consts, h + 3)
                        if h >= 4 and new_kv(h):
                            pe.wait_ge(k_hi_low, kv_count(h) - 4)
                        if kind(h) == "B":
                            pe.wait_ge(table_lo, 2 * (h - 3))
                    if i in (0, 8, 16):
                        pe.wait_ge(row_copied, 3 * h + (1, 2, 3)[i // 8])
                    ks, qs = slice(kt * P, kt * P + P), slice(q0, q0 + w)
                    if kind(h) == "A":
                        prods = [(c.k1[kp][0:97, ks], c.q1[par][0:97, qs]), (c.k2[kp][0:96, ks], c.q1[par][0:96, qs]),
                                 (c.k1[kp][0:96, ks], c.q2[par][0:96, qs])]
                    else:
                        prods = [(c.k1[kp][:, ks], c.q1[par][:, qs]), (c.k2[kp][0:65, ks], c.q2[par][0:65, qs])]
                    if kind(h) == "B":
                        x0 = (q0 - kt * P) + 896
                        prods += [(c.ident_r[:], c.gh[par][:, x0:x0 + w]), (c.ident_r[:], c.gl[par][:, x0:x0 + w])]
                    for k, (a, b) in enumerate(prods):
                        mm = pe.matmul(out, a, b, start=(k == 0), stop=(k == len(prods) - 1))
                    mm.then_inc(scored, 1)

                def values(g):
                    h, i = divmod(g, NS)
                    seg, q0, w, kt, first, last = STEPS[i]
                    o = 3 * h + (0 if i < 8 else 1 if i < 16 else 2)
                    if first and o >= 2:
                        pe.wait_ge(scaled, o - 1)
                    if i == 0:
                        pe.wait_ge(v_lo, 2 * kv_count(h))
                    who = pl_engine(g)
                    pe.wait_ge(lo_dve if who == "dve" else lo_pool, pl_count(g, who))
                    out = bank(c, OB + o % 2, w)
                    pe.matmul(out, c.vh[kv(h)][:, kt, :], c.ph[g % 3][:, 0:w], start=first, stop=False)
                    pe.matmul(out, c.vl[kv(h)][:, kt, :], c.ph[g % 3][:, 0:w], start=False, stop=False)
                    pe.matmul(out, c.vh[kv(h)][:, kt, :], c.pl[g % 3][:, 0:w], start=False, stop=last).then_inc(pv_done, 1)

                def max_scores(h, j):
                    qt, k0, w, kb = MAXES[j]
                    n = NM * h + j
                    if n >= 2:
                        pe.wait_ge(max_taken, n - 1)
                    if j == 0:
                        pe.wait_ge(q_hi, h + 1)
                        pe.wait_ge(k_lo, kv_count(h))
                        if kind(h) == "B":
                            pe.wait_ge(table_lo, 2 * (h - 3))
                    r = 96 if kind(h) == "A" else P
                    out = bank(c, SM + n % 2, w)
                    mm = pe.matmul(out, c.q1[h % 2][0:r, qt * P:qt * P + P], c.k1[kv(h)][0:r, k0:k0 + w], start=True, stop=kind(h) != "B")
                    if kind(h) == "B":
                        for kk in range(w // P):
                            x0 = qt * P - (k0 + kk * P) + 896
                            mm = pe.matmul(out[:, kk * P:kk * P + P], c.gh[h % 2][:, x0:x0 + P], c.ident_r[:],
                                           start=False, stop=(kk == w // P - 1))
                    mm.then_inc(max_scored, 1)

                def turn_values(h, part):
                    n = kv_count(h) - 1
                    if part == 0:
                        pe.wait_ge(v_raw, 16 * (n + 1))
                        if h >= 1:
                            pe.wait_ge(row_copied, 3 * h)
                    else:
                        pe.wait_ge(v_lo, 2 * n + 1)
                    for t in (range(8) if part == 0 else range(8, 10)):
                        mm = pe.transpose(bank(c, MISC, 64, off=(t % 8) * 64), c.vt[0:64, t * P:t * P + P], c.ident[0:64, 0:64])
                    mm.then_inc(v_turned, 1)

                def turn_row(h, r):
                    if r == 0:
                        pe.wait_ge(max_ready, h + 1)
                        pe.wait_ge(v_lo, 2 * kv_count(h))
                        if not new_kv(h):
                            pe.wait_ge(row_copied, 3 * h)
                    else:
                        pe.wait_ge(row_copied, 3 * h + r)
                    for k, qt in enumerate(range(*ROW_TILES[r])):
                        mm = pe.matmul(bank(c, MISC, P, slice(0, 1), off=k * P), c.m[:, qt:qt + 1], c.ident[:], start=True, stop=True)
                    mm.then_inc(row_turned, 1)

                turn_values(0, 0)
                turn_values(0, 1)
                for j in range(NM):
                    max_scores(0, j)
                for r in range(3):
                    turn_row(0, r)
                for g in range(G_TOTAL + PV_LAG):
                    h, i = divmod(g, NS)
                    if g < G_TOTAL:
                        scores(g)
                    if h + 1 < HEADS:
                        if i == 2 and new_kv(h + 1):
                            turn_values(h + 1, 0)
                        if i == 4 and new_kv(h + 1):
                            turn_values(h + 1, 1)
                        if MAX_FROM <= i < MAX_FROM + NM // 2:
                            max_scores(h + 1, 2 * (i - MAX_FROM))
                            max_scores(h + 1, 2 * (i - MAX_FROM) + 1)
                        if i >= 15:
                            turn_row(h + 1, i - 15)
                    if g >= PV_LAG:
                        values(g - PV_LAG)

            @block.scalar
            def _(act):
                act.preload_act_table_set(LOG_SET)
                def split_q(h):
                    act.wait_ge(q_raw, 32 * (h + 1))
                    if h >= 2:
                        act.wait_ge(scored, NS * (h - 1))
                    r = 96 if kind(h) == "A" else P
                    act.activation(c.q1[h % 2][0:r, :], c.rq[0:r, :], ACT.Copy).then_inc(q_hi, 1)

                def split_k(h):
                    n = kv_count(h) - 1
                    act.wait_ge(k_raw, 32 * (n + 1))
                    if kind(h) == "A":
                        act.activation(c.k1[kv(h)][0:96, :], c.rk[0:96, :], ACT.Copy).then_inc(k_hi, 1)
                    else:
                        act.activation(c.k2[kv(h)][0:64, :], c.rk[0:64, :], ACT.Copy).then_inc(k_hi_low, 1)
                        act.activation(c.k1[kv(h)][:, :], c.rk[:, :], ACT.Copy).then_inc(k_hi, 1)

                def split_table(h):
                    for i in range(2):
                        act.wait_ge(table_raw, 32 * (h - 3))
                        act.activation(c.gh[h % 2][:, i * GW // 2:(i + 1) * GW // 2], c.graw[i][:], ACT.Copy).then_inc(table_hi, 1)

                def copy_row(h, r):
                    act.wait_ge(row_turned, 3 * h + r + 1)
                    t0, t1 = (x * P for x in ROW_TILES[r])
                    row = c.q1[h % 2][96:97, t0:t1] if kind(h) == "A" else c.q2[h % 2][64:65, t0:t1]
                    act.activation(row, bank(c, MISC, t1 - t0, slice(0, 1)), ACT.Copy).then_inc(row_copied, 1)

                def denominators(o):
                    w = out_i[o % 3][2]
                    act.wait_ge(pv_done, last_step(o) + 1)
                    if o >= 1:
                        act.wait_ge(scaled, o)
                    act.activation(c.ln_den[0:64, 0:w], bank(c, OB + o % 2, w, slice(64, P)), ACT.Ln).then_inc(ln_done, 1)
                    act.wait_ge(ln_done, o + 1)
                    act.activation(c.rden[0:64, 0:w], c.ln_den[0:64, 0:w], ACT.Exp, scale=-1.0).then_inc(rden_done, 1)

                def output_hi(o):
                    h = o // 3
                    _, q0, w = out_i[o % 3]
                    rows = slice(64 * (h % 2), 64 * (h % 2) + 64)
                    act.wait_ge(scaled, o + 1)
                    act.activation(c.hh[rows, h // 2, q0:q0 + w], c.ot[rows, 0:w], ACT.Copy).then_inc(out_hi, 1)

                split_q(0)
                split_k(0)
                for r in range(3):
                    copy_row(0, r)
                done_o, hi_o = 0, 0
                for g in range(G_TOTAL + 8):
                    h, i = divmod(g, NS)
                    if g < G_TOTAL:
                        w = STEPS[i][2]
                        act.wait_ge(scored, g + 1)
                        if g >= 3:
                            who = pl_engine(g - 3)
                            act.wait_ge(lo_dve if who == "dve" else lo_pool, pl_count(g - 3, who))
                        act.activation(c.p[g % 3][:, 0:w], bank(c, ST + g % 3, w), ACT.Exp, scale=STEP_SCALE[kind(h)]).then_inc(exp_done, 1)
                        act.wait_ge(exp_done, g + 1)
                        if g >= 3:
                            act.wait_ge(pv_done, g - 2)
                        act.activation(c.ph[g % 3][:, 0:w], c.p[g % 3][:, 0:w], ACT.Copy).then_inc(hi_done, 1)
                    if h + 1 < HEADS:
                        if i == 0:
                            split_q(h + 1)
                        if i == 1 and new_kv(h + 1):
                            split_k(h + 1)
                        if i == 2 and kind(h + 1) == "B":
                            split_table(h + 1)
                        if i == 16:
                            copy_row(h + 1, 0)
                        if i == 17:
                            copy_row(h + 1, 1)
                            copy_row(h + 1, 2)
                    if hi_o < 3 * HEADS and g >= last_step(hi_o) + PV_LAG + 4:
                        output_hi(hi_o)
                        hi_o += 1
                    if done_o < 3 * HEADS and g >= last_step(done_o) + PV_LAG + 1 and done_o - hi_o < 1:
                        denominators(done_o)
                        done_o += 1
                while done_o < 3 * HEADS or hi_o < 3 * HEADS:
                    if hi_o < done_o:
                        output_hi(hi_o)
                        hi_o += 1
                    else:
                        denominators(done_o)
                        done_o += 1

            @block.gpsimd
            def _(pool):
                before = [None, None, 0]

                def settle(rows, semaphore, count):
                    if before[0] is not None and before[0] != rows:
                        pool.wait_ge(before[1], before[2])
                    before[:] = [rows, semaphore, count]

                def lo_parts(h):
                    n = kv_count(h)
                    if new_kv(h):
                        pool.wait_ge(k_hi, n)
                        if kind(h) == "A":
                            settle((0, 96), k_lo, n)
                            pool.tensor_tensor(c.k2[kv(h)][0:96, :], c.rk[0:96, :], c.k1[kv(h)][0:96, :].bitcast(F32), ALU.subtract).then_inc(k_lo, 1)
                        else:
                            settle((64, P), k_lo, n)
                            pool.tensor_tensor(c.k1[kv(h)][64:P, :], c.rk[64:P, :], c.k1[kv(h)][64:P, :].bitcast(F32), ALU.subtract).then_inc(k_lo, 1)
                    pool.wait_ge(q_hi, h + 1)
                    r = 96 if kind(h) == "A" else 64
                    settle((0, r), q_lo, h + 1)
                    pool.tensor_tensor(c.q2[h % 2][0:r, :], c.rq[0:r, :], c.q1[h % 2][0:r, :].bitcast(F32), ALU.subtract).then_inc(q_lo, 1)
                    if kind(h) == "B":
                        for i in range(2):
                            sl = slice(i * GW // 2, (i + 1) * GW // 2)
                            pool.wait_ge(table_hi, 2 * (h - 4) + i + 1)
                            settle((0, P), table_lo, 2 * (h - 4) + i + 1)
                            pool.tensor_tensor(c.gl[h % 2][:, sl], c.graw[i][:], c.gh[h % 2][:, sl].bitcast(F32), ALU.subtract).then_inc(table_lo, 1)

                lo_parts(0)
                hi_o = 0
                for g in range(G_TOTAL + 8):
                    h, i = divmod(g, NS)
                    if g < G_TOTAL and pl_engine(g) == "pool":
                        w = STEPS[i][2]
                        pool.wait_ge(hi_done, g + 1)
                        settle((0, P), lo_pool, pl_count(g, "pool"))
                        pool.tensor_tensor(c.pl[g % 3][:, 0:w], c.p[g % 3][:, 0:w], c.ph[g % 3][:, 0:w].bitcast(F32), ALU.subtract).then_inc(lo_pool, 1)
                    if i == 1 and h + 1 < HEADS:
                        lo_parts(h + 1)
                    while hi_o < 3 * HEADS and (g >= last_step(hi_o) + PV_LAG + 5 or g == G_TOTAL + 7):
                        hh, (_, q0, w) = hi_o // 3, out_i[hi_o % 3]
                        r0 = 64 * (hh % 2)
                        rows = slice(r0, r0 + 64)
                        pool.wait_ge(out_hi, hi_o + 1)
                        settle((r0, r0 + 64), out_lo, hi_o + 1)
                        pool.tensor_tensor(c.hl[rows, hh // 2, q0:q0 + w], c.ot[rows, 0:w], c.hh[rows, hh // 2, q0:q0 + w].bitcast(F32), ALU.subtract).then_inc(out_lo, 1)
                        hi_o += 1

            @block.vector
            def _(dve):
                def take_max(h, j):
                    qt, k0, w, kb = MAXES[j]
                    n = NM * h + j
                    if j == 0 and h >= 1:
                        dve.wait_ge(row_turned, 3 * h)
                    dve.wait_ge(max_scored, n + 1)
                    if qt < 8:
                        dve.tensor_reduce(c.mx[:, qt, kb:kb + 1], bank(c, SM + n % 2, w), AX.X, ALU.max).then_inc(max_taken, 1)
                    else:
                        dve.tensor_reduce(c.m[:, qt:qt + 1], bank(c, SM + n % 2, w), AX.X, ALU.max, negate=True).then_inc(max_taken, 1)

                def join_max(h):
                    dve.wait_ge(max_taken, NM * (h + 1))
                    dve.tensor_reduce(c.m[:, 0:8], c.mx[:, :, :], AX.X, ALU.max, negate=True).then_inc(max_ready, 1)

                def split_values(h, part):
                    n = kv_count(h) - 1
                    tiles, nt = (slice(0, 8), 8) if part == 0 else (slice(8, 10), 2)
                    src = bank(c, MISC, 64 * nt).rearrange("p (t v) -> p t v", v=64)
                    dve.wait_ge(v_turned, 2 * n + part + 1)
                    if h >= 2:
                        dve.wait_ge(pv_done, NS * (h - 1))
                    elif part == 0:
                        dve.wait_ge(consts, 6)
                    dve.tensor_copy(c.vh[kv(h)][:, tiles, 0:64], src).then_inc(v_hi, 1)
                    dve.wait_ge(v_hi, 2 * n + part + 1)
                    dve.tensor_tensor(c.vl[kv(h)][:, tiles, 0:64], src, c.vh[kv(h)][:, tiles, 0:64].bitcast(F32), ALU.subtract).then_inc(v_lo, 1)

                def scale_output(o):
                    h = o // 3
                    w = out_i[o % 3][2]
                    rows = slice(64 * (h % 2), 64 * (h % 2) + 64)
                    dve.wait_ge(rden_done, o + 1)
                    if o >= 1:
                        dve.wait_ge(out_lo, o)
                    dve.tensor_tensor(c.ot[rows, 0:w], bank(c, OB + o % 2, w, slice(0, 64)), c.rden[0:64, 0:w], ALU.mult).then_inc(scaled, 1)

                for i in range(2):
                    dve.memset(c.k1[i][96:97, :].bitcast(F32), 1.0).then_inc(consts, 1)
                    dve.memset(c.vh[i][:, :, 64:P].bitcast(F32), 1.0).then_inc(consts, 1)
                    dve.memset(c.vl[i][:, :, 64:P].bitcast(F32), 0.0).then_inc(consts, 1)
                split_values(0, 0)
                split_values(0, 1)
                for j in range(NM):
                    take_max(0, j)
                join_max(0)
                o = 0
                for g in range(G_TOTAL + 8):
                    h, i = divmod(g, NS)
                    if h + 1 < HEADS:
                        if i == 1 and h + 1 in (4, 5):
                            dve.wait_ge(scored, NS * h)
                            dve.memset(c.k2[kv(h + 1)][64:65, :].bitcast(F32), 1.0).then_inc(consts, 1)
                        if i == 2 and new_kv(h + 1):
                            split_values(h + 1, 0)
                        if i == 4 and new_kv(h + 1):
                            split_values(h + 1, 1)
                        if MAX_FROM <= i < MAX_FROM + NM // 2:
                            take_max(h + 1, 2 * (i - MAX_FROM))
                            take_max(h + 1, 2 * (i - MAX_FROM) + 1)
                        if i == MAX_FROM + NM // 2:
                            join_max(h + 1)
                    if g < G_TOTAL and pl_engine(g) == "dve":
                        w = STEPS[i][2]
                        dve.wait_ge(hi_done, g + 1)
                        dve.tensor_tensor(c.pl[g % 3][:, 0:w], c.p[g % 3][:, 0:w], c.ph[g % 3][:, 0:w].bitcast(F32), ALU.subtract).then_inc(lo_dve, 1)
                    while o < 3 * HEADS and (g >= last_step(o) + PV_LAG + 2 or g == G_TOTAL + 7):
                        scale_output(o)
                        o += 1
        end_phase(nc, [q_raw, k_raw, v_raw, table_raw, k_hi_low, consts, q_hi, k_hi, q_lo, k_lo, table_hi, table_lo, v_turned, v_hi, v_lo,
                       max_scored, max_taken, max_ready, row_turned, row_copied, scored, exp_done, hi_done, lo_pool, lo_dve,
                       pv_done, ln_done, rden_done, scaled, out_hi, out_lo])



def output_projection(nc, c, L):
    with ExitStack() as ex:
        def sem(name):
            return ex.enter_context(nc.semaphore(name))
        raw_arrived = [sem("raw_arrived0"), sem("raw_arrived1")]
        w_hi, w_lo, w_used, evacuated = sem("w_hi"), sem("w_lo"), sem("w_used"), sem("evacuated")
        with nc.Block() as block:
            @block.sync
            def _(sp):
                for n in range(KC):
                    load_weights(sp, c, n, c.raw[n % 2][:],
                                 c.w_out[bass.ds(L, 1), :, n * P:n * P + P].rearrange("a (k p) n -> p (a k) n", p=P), raw_arrived, w_lo)

            @block.tensor
            def _(pe):
                for n in range(KC):
                    pe.wait_ge(w_lo, n + 1)
                    if n >= 2:
                        pe.wait_ge(evacuated, n - 1)
                    project(pe, c, n % 2, n % 2).then_inc(w_used, 1)

            @block.scalar
            def _(act):
                split_hi(act, c, 0, raw_arrived, w_used, w_hi)
                split_hi(act, c, 1, raw_arrived, w_used, w_hi)
                for n in range(KC):
                    act.wait_ge(w_used, n + 1)
                    act.activation(c.y[:, n, :], unit_psum(c, n % 2), ACT.Copy).then_inc(evacuated, 1)
                    if n + 2 < KC:
                        split_hi(act, c, n + 2, raw_arrived, w_used, w_hi)

            @block.gpsimd
            def _(pool):
                for n in range(KC):
                    split_lo(pool, c, n, w_hi, w_lo)
        end_phase(nc, raw_arrived + [w_hi, w_lo, w_used, evacuated])



def gated_mlp(nc, c, L):
    def first(i):
        return 4 + 6 * (i - 1)

    with ExitStack() as ex:
        def sem(name):
            return ex.enter_context(nc.semaphore(name))
        raw_arrived = [sem("raw_arrived0"), sem("raw_arrived1")]
        w_hi, w_lo, w_used = sem("w_hi"), sem("w_lo"), sem("w_used")
        up_done, centred, shifted, gelu_done, gated, act_hi, act_lo = (sem("up_done"), sem("centred"), sem("shifted"),
            sem("gelu_done"), sem("gated"), sem("act_hi"), sem("act_lo"))
        down_done, down_added, cleared, left = sem("down_done"), sem("down_added"), sem("cleared"), sem("left")
        with nc.Block() as block:
            def up_src(i, unit):
                col = (i * 2 + unit // 2) * P + (unit % 2) * D_FF
                return c.w_up[bass.ds(L, 1), :, bass.ds(col, P)].rearrange("a (k p) n -> p (a k) n", p=P)

            def down_src(i, k):
                return c.w_down[bass.ds(L, 1), bass.ds((i * 2 + k) * P, P), :].rearrange("a p n -> p (a n)")

            @block.sync
            def _(sp):
                def load(n, parity, src, flat=False):
                    sp.wait_ge(w_lo, n - 1)
                    dst = c.raw[parity][:].rearrange("p k n -> p (k n)") if flat else c.raw[parity][:]
                    sp.dma_start(dst, src).then_inc(raw_arrived[parity], 16)

                sp.dma_start(c.raw[0][:], up_src(0, 0)).then_inc(raw_arrived[0], 16)
                sp.dma_start(c.raw[1][:], up_src(0, 1)).then_inc(raw_arrived[1], 16)
                load(2, 0, up_src(0, 2))
                load(3, 1, up_src(0, 3))
                with sp.Fori(1, FF_PAIRS) as i:
                    n = first(i)
                    load(n, 0, up_src(i, 0))
                    load(n + 1, 1, down_src(i - 1, 0), True)
                    load(n + 2, 0, down_src(i - 1, 1), True)
                    load(n + 3, 1, up_src(i, 1))
                    load(n + 4, 0, up_src(i, 2))
                    load(n + 5, 1, up_src(i, 3))
                n = first(FF_PAIRS)
                load(n, 0, down_src(FF_PAIRS - 1, 0), True)
                load(n + 1, 1, down_src(FF_PAIRS - 1, 1), True)

            @block.tensor
            def _(pe):
                def up(n, slot, m, half, wait=True):
                    pe.wait_ge(w_lo, n + 1)
                    if wait:
                        pe.wait_ge(shifted, m - 1)
                    project(pe, c, slot, half).then_inc(w_used, 1)

                def down(n, slots, it, wait=True):
                    pe.wait_ge(w_lo, n + 2)
                    pe.wait_ge(act_lo, it * 2)
                    for u in range(24):
                        o, (t0, w) = u // 3, BLOCKS[u % 3]
                        if u >= 2:
                            pe.wait_ge(down_added, (it - 1) * 24 + u - 1)
                        elif wait:
                            pe.wait_ge(down_added, (it - 1) * 24 + u - 1)
                        last = product(pe, c, bank(c, 6 + u % 2, w), 0,
                                       [(c.wh[s][:, o, :], c.wl[s][:, o, :], c.ah[:, k, t0:t0 + w], c.al[:, k, t0:t0 + w])
                                        for k, s in enumerate(slots)])
                        if u == 23:
                            last.then_inc(w_used, 2)
                        else:
                            last.then_inc(down_done, 1)

                up(0, 0, 0, 0, False)
                up(1, 1, 1, 1, False)
                up(2, 2, 2, 0)
                up(3, 0, 3, 1)
                n = first(1)
                up(n, 1, 4, 0)
                down(n + 1, (2, 0), 1, False)
                up(n + 3, 1, 5, 1)
                up(n + 4, 2, 6, 0)
                up(n + 5, 0, 7, 1)
                with pe.Fori(2, FF_PAIRS) as i:
                    n = first(i)
                    up(n, 1, 4 * i, 0)
                    down(n + 1, (2, 0), i)
                    up(n + 3, 1, 4 * i + 1, 1)
                    up(n + 4, 2, 4 * i + 2, 0)
                    up(n + 5, 0, 4 * i + 3, 1)
                down(first(FF_PAIRS), (1, 2), FF_PAIRS)

            def split(act, n, slot, parity, raws, wait=True):
                act.wait_ge(raw_arrived[parity], 16 * raws)
                if wait:
                    act.wait_ge(w_used, n - 2)
                act.activation(c.wh[slot][:], c.raw[parity][:], ACT.Copy).then_inc(w_hi, 1)

            @block.scalar
            def _(act):
                def centre(i, unit, used):
                    act.wait_ge(w_used, used)
                    j = i * 2 + unit // 2 + (unit % 2) * (D_FF // P)
                    act.activation(c.cb[unit][:], unit_psum(c, unit % 2), ACT.Identity, scale=c.conv[:, 1, bass.ds(j, 1)],
                                   bias=c.conv[:, 3, bass.ds(j, 1)]).then_inc(centred, 1)

                def gelu(i, k):
                    act.wait_ge(shifted, i * 4 + 2 * k + 1)
                    act.activation(c.cb[2 * k][:], c.cb[2 * k][:], ACT.Gelu_apprx_tanh).then_inc(gelu_done, 1)

                def hi(i, k):
                    act.wait_ge(gated, i * 2 + k + 1)
                    act.activation(c.ah[:, k, :], c.cb[2 * k][:], ACT.Copy).then_inc(act_hi, 1)

                split(act, 0, 0, 0, 1, False)
                split(act, 1, 1, 1, 1, False)
                split(act, 2, 2, 0, 2, False)
                centre(0, 0, 1)
                split(act, 3, 0, 1, 2)
                gelu(0, 0)
                centre(0, 1, 2)
                split(act, 4, 1, 0, 3)
                hi(0, 0)
                centre(0, 2, 3)
                split(act, 5, 2, 1, 3)
                gelu(0, 1)
                centre(0, 3, 4)
                hi(0, 1)
                with act.Fori(1, FF_PAIRS) as i:
                    n = first(i)
                    half = 2 + 3 * (i - 1)
                    split(act, n + 2, 0, 0, half + 2)
                    act.wait_ge(act_lo, i * 2)
                    centre(i, 0, n + 1)
                    split(act, n + 3, 1, 1, half + 2)
                    gelu(i, 0)
                    split(act, n + 4, 2, 0, half + 3)
                    split(act, n + 5, 0, 1, half + 3)
                    centre(i, 1, n + 4)
                    split(act, n + 6, 1, 0, half + 4)
                    hi(i, 0)
                    centre(i, 2, n + 5)
                    split(act, n + 7, 2, 1, half + 4)
                    gelu(i, 1)
                    centre(i, 3, n + 6)
                    hi(i, 1)

            @block.gpsimd
            def _(pool):
                def lo(n, slot, parity):
                    pool.wait_ge(w_hi, n + 1)
                    pool.tensor_tensor(c.wl[slot][:], c.raw[parity][:], c.wh[slot][:].bitcast(F32), ALU.subtract).then_inc(w_lo, 1)

                def act_low(i, k):
                    pool.wait_ge(act_hi, i * 2 + k + 1)
                    pool.tensor_tensor(c.al[:, k, :], c.cb[2 * k][:], c.ah[:, k, :].bitcast(F32), ALU.subtract).then_inc(act_lo, 1)

                lo(0, 0, 0)
                lo(1, 1, 1)
                pool.memset(c.y[:], 0.0).then_inc(cleared, 1)
                lo(2, 2, 0)
                lo(3, 0, 1)
                lo(4, 1, 0)
                act_low(0, 0)
                lo(5, 2, 1)
                act_low(0, 1)
                with pool.Fori(1, FF_PAIRS) as i:
                    n = first(i)
                    lo(n + 2, 0, 0)
                    lo(n + 3, 1, 1)
                    lo(n + 4, 2, 0)
                    lo(n + 5, 0, 1)
                    lo(n + 6, 1, 0)
                    act_low(i, 0)
                    lo(n + 7, 2, 1)
                    act_low(i, 1)

            @block.vector
            def _(dve):
                def shift(i, unit):
                    m = i * 4 + unit
                    j = i * 2 + unit // 2 + (unit % 2) * (D_FF // P)
                    dve.wait_ge(centred, m + 1)
                    for seg, (t0, s) in enumerate(SEGS):
                        dve.scalar_tensor_tensor(out=c.cb[unit][:, t0 + 1:t0 + s], in0=unit_psum(c, unit % 2, t0, t0 + s - 1),
                                                 scalar=c.conv[:, 0, bass.ds(j, 1)], in1=c.cb[unit][:, t0 + 1:t0 + s],
                                                 op0=ALU.mult, op1=ALU.add).then_inc(left, 1)
                    dve.wait_ge(left, m * 2 + 2)
                    for seg, (t0, s) in enumerate(SEGS):
                        mm = dve.scalar_tensor_tensor(out=c.cb[unit][:, t0:t0 + s - 1], in0=unit_psum(c, unit % 2, t0 + 1, t0 + s),
                                                      scalar=c.conv[:, 2, bass.ds(j, 1)], in1=c.cb[unit][:, t0:t0 + s - 1],
                                                      op0=ALU.mult, op1=ALU.add)
                    mm.then_inc(shifted, 1)

                def gate(i, k):
                    dve.wait_ge(gelu_done, i * 2 + k + 1)
                    dve.wait_ge(shifted, i * 4 + 2 * k + 2)
                    dve.tensor_tensor(c.cb[2 * k][:], c.cb[2 * k][:], c.cb[2 * k + 1][:], ALU.mult).then_inc(gated, 1)

                def add_down(it):
                    for u in range(24):
                        o, (t0, w) = u // 3, BLOCKS[u % 3]
                        if u == 23:
                            dve.wait_ge(w_used, first(it) + 3)
                        else:
                            dve.wait_ge(down_done, (it - 1) * 23 + u + 1)
                        dve.tensor_tensor(c.y[:, o, t0:t0 + w], bank(c, 6 + u % 2, w), c.y[:, o, t0:t0 + w], ALU.add).then_inc(down_added, 1)

                for unit in range(4):
                    shift(0, unit)
                    if unit % 2:
                        gate(0, unit // 2)
                dve.wait_ge(cleared, 1)
                with dve.Fori(1, FF_PAIRS) as i:
                    shift(i, 0)
                    add_down(i)
                    for unit in range(1, 4):
                        shift(i, unit)
                        if unit % 2:
                            gate(i, unit // 2)
                for u in range(24):
                    o, (t0, w) = u // 3, BLOCKS[u % 3]
                    if u == 23:
                        dve.wait_ge(w_used, first(FF_PAIRS) + 2)
                    else:
                        dve.wait_ge(down_done, (FF_PAIRS - 1) * 23 + u + 1)
                    dve.tensor_tensor(c.y[:, o, t0:t0 + w], bank(c, 6 + u % 2, w), c.y[:, o, t0:t0 + w], ALU.add).then_inc(down_added, 1)
        end_phase(nc, raw_arrived + [w_hi, w_lo, w_used, up_done, centred, shifted, gelu_done, gated, act_hi, act_lo,
                                     down_done, down_added, cleared, left])


def encoder(nc, c):
    c.s_x = nc.dram_tensor("residual", (P, KC, T), F32, kind="Internal").ap()
    c.s_z = nc.dram_tensor("heads", (Z_ROWS, T), F32, kind="Internal").ap()
    c.s_line = nc.dram_tensor("distance_lines", (H_B, N_DIST), F32, kind="Internal").ap()
    c.s_lines = nc.dram_tensor("distance_tables", (H_B, P, N_DIST), F32, kind="Internal").ap()
    place_buffers(nc, c)
    build_tables(nc, c)
    turn_input(nc, c)
    with nc.Fori(0, DEPTH) as L:
        load_params(nc, c, L)
        norm(nc, c, G_MIX_PRE, False)
        latent_projections(nc, c, L)
        head_projections(nc, c, L)
        attention(nc, c)
        output_projection(nc, c, L)
        norm(nc, c, G_MIX_POST, True)
        norm(nc, c, G_FFN_PRE, False)
        gated_mlp(nc, c, L)
        norm(nc, c, G_FFN_POST, True)
    turn_output(nc, c)



def rope_tables(positions, n_freq):
    inv = np.float32(10000.0) ** (-np.arange(n_freq, dtype=np.float32) / np.float32(n_freq))
    ang = positions.astype(np.float32)[None, :] * inv.astype(np.float32)[:, None]
    return np.cos(ang).astype(np.float32), np.sin(ang).astype(np.float32)


def swap_halves(n, width):
    m = np.zeros((n, n), np.float32)
    h = width // 2
    for g in range(0, n, width):
        for i in range(h):
            m[g + h + i, g + i] = -1.0
            m[g + i, g + h + i] = 1.0
    return m


def distance_constants():
    dist = 1023 - np.arange(N_DIST)
    half, exact = 16, 8
    n = np.abs(dist)
    large = exact + (np.log(np.maximum(n, 1) / exact) / math.log(1024 / exact) * (half - exact)).astype(np.int32)
    bucket = np.where(dist > 0, half, 0) + np.where(n < exact, n, np.minimum(large, half - 1))
    onehot = (bucket[None, :] == np.arange(32)[:, None]).astype(np.float32)
    count = np.zeros(N_DIST, np.int64)
    for window, dilation in ((128, 1), (512, 4), (2048, 16)):
        count += (n % dilation == 0) & (n // dilation <= window // (2 * dilation))
    logc = np.where(count > 0, np.log(np.maximum(count, 1)), MASKED).astype(np.float32)
    return onehot, np.ascontiguousarray(np.broadcast_to(logc, (H_B, N_DIST)))


def shape_constants():
    pos = np.concatenate([np.arange(s) for _, s in SEGS])
    cos_a, sin_a = rope_tables(pos, 16)
    cos_r, sin_r = rope_tables(pos // 64, 16)
    cos_l, sin_l = rope_tables(pos % 64, 16)
    onehot, logc = distance_constants()
    return {
        "cos_a": np.tile(cos_a, (8, 1)), "sin_a": np.tile(sin_a, (8, 1)),
        "cos_c": np.tile(np.concatenate([cos_r, cos_r, cos_l, cos_l]), (2, 1)),
        "sin_c": np.tile(np.concatenate([sin_r, sin_r, sin_l, sin_l]), (2, 1)),
        "onehot": onehot, "logc": logc, "ident": np.eye(P, dtype=np.float32), "ones": np.ones((P, P), np.float32),
        "block_ones": np.kron(np.eye(2, dtype=np.float32), np.ones((64, 64), np.float32)),
        "perm_c": swap_halves(P, 32), "perm_a": swap_halves(P, 32),
    }


INPUTS = ("x_prompt", "x_sample", "rel_bias", "norm_mix_pre", "norm_mix_post", "w_in", "q_lora_norm", "w_uq", "kv_norm",
          "w_ukv", "c_q_norm", "c_k_norm", "w_out", "norm_ffn_pre", "norm_ffn_post", "w_up", "conv_w", "conv_b", "w_down")


def kernel(**inputs):
    from concourse import bacc
    from concourse.bass_utils import run_bass_kernel_spmd

    nc = bacc.Bacc("TRN2", target_bir_lowering=False, num_devices=1)
    c = Ctx()
    arrays = {}

    def declare(name, a):
        a = np.ascontiguousarray(a)
        arrays[name] = a
        return nc.dram_tensor(name, a.shape, mybir.dt.from_np(a.dtype), kind="ExternalInput").ap()

    (c.x_prompt, c.x_sample, c.rel_bias, c.norm_mix_pre, c.norm_mix_post, c.w_in, c.q_lora_norm, c.w_uq, c.kv_norm, c.w_ukv,
     c.c_q_norm, c.c_k_norm, c.w_out, c.norm_ffn_pre, c.norm_ffn_post, c.w_up, c.conv_w, c.conv_b, c.w_down) = [
        declare(f"in_{name}", inputs[name]) for name in INPUTS]
    k = {name: declare(f"const_{name}", a) for name, a in shape_constants().items()}
    c.d_cos_a, c.d_sin_a, c.d_cos_c, c.d_sin_c, c.d_onehot, c.d_logc = (k["cos_a"], k["sin_a"], k["cos_c"], k["sin_c"],
                                                                        k["onehot"], k["logc"])
    c.d_ident, c.d_ones, c.d_block_ones, c.d_perm_c, c.d_perm_a = (k["ident"], k["ones"], k["block_ones"], k["perm_c"], k["perm_a"])
    c.y_prompt = nc.dram_tensor("y_prompt", (1, 1024, D), F32, kind="ExternalOutput").ap()
    c.y_sample = nc.dram_tensor("y_sample", (1, 256, D), F32, kind="ExternalOutput").ap()
    encoder(nc, c)
    r = run_bass_kernel_spmd(nc, [arrays], core_ids=[0])
    return r.results[0]["y_prompt"], r.results[0]["y_sample"]
```

```python
import math
from contextlib import ExitStack

import numpy as np

import concourse.bass as bass
from concourse import mybir
from concourse.alu_op_type import AluOpType as ALU

F32 = mybir.dt.float32
F32R = mybir.dt.float32r
ACT = mybir.ActivationFunctionType
AX = mybir.AxisListType

P = 128
D = 1024
DEPTH = 2
SEGS = ((0, 1024), (1024, 256))
T = 1280
BLOCKS = ((0, 512), (512, 512), (1024, 256))
KC = D // P
NT = T // P
H_A, H_B, H_C = 4, 4, 8
HEADS = H_A + H_B + H_C
D_FF = 2816
FF_PAIRS = D_FF // (2 * P)
EPS = 1e-6
MASKED = -1e30
N_DIST = 2048
GW = 1920
LOG_SET = "natural_log_exp_and_others"

QAN, QAR, KAN, KAR, VA = 0, 256, 384, 640, 672
QB, KB, VB = 928, 1184, 1440
QC, KC_ROW, VC = 1696, 2208, 2336
Z_ROWS = 2464

G_MIX_PRE, G_MIX_POST, G_FFN_PRE, G_FFN_POST, G_QL, G_KV, G_CQ, G_CK, N_GAINS = 0, 8, 16, 24, 32, 34, 35, 36, 37


class Ctx:
    pass


def place_buffers(nc, c):
    at = [(nc.sbuf_base + 31) // 32 * 32]

    def take(name, shape, dt=F32):
        t = nc.alloc_sbuf_tensor_at(name, shape, dt, offset=at[0])
        at[0] += 4 * int(np.prod(shape[1:]))
        at[0] = (at[0] + 31) // 32 * 32
        return t

    c.ident = take("ident", [P, P])
    c.ident_r = take("ident_r", [P, P], F32R)
    c.ones = take("ones", [P, P])
    c.block_ones = take("block_ones", [P, P])
    c.perm_c = take("perm_c", [P, P])
    c.perm_a = take("perm_a", [P, P])
    c.gain = take("gain", [P, N_GAINS])
    c.conv = take("conv", [P, 4, 2 * D_FF // P])
    c.eps = take("eps", [P, 1])
    h_at = at[0]
    c.hh = take("hh", [P, KC, T], F32R)
    c.hl = take("hl", [P, KC, T], F32R)
    raw_at = at[0]
    c.raw = [take(f"raw{i}", [P, KC, P]) for i in range(2)]
    c.wh = [take(f"wh{i}", [P, KC, P], F32R) for i in range(2)]
    c.wl = [take(f"wl{i}", [P, KC, P], F32R) for i in range(2)]
    arena = at[0]
    end = nc.sbuf_usable_end

    c.y = take("y", [P, KC, T])
    after_y = at[0]
    c.r = take("r", [P, T])
    c.lnt = take("lnt", [P, T])
    c.sq = [take(f"sq{i}", [P, 512]) for i in range(4)]
    c.tmp = [take(f"tmp{i}", [P, 512]) for i in range(4)]
    c.xo = [take(f"xo{i}", [P, 512]) for i in range(4)]
    at[0] = after_y
    c.tok = [take(f"tok{i}", [P, D]) for i in range(4)]
    at[0] = after_y
    c.gain_rows = take("gain_rows", [N_GAINS, P])
    c.conv_rows = take("conv_rows", [2 * D_FF // P, 4, P])
    at[0] = after_y
    c.onehot = take("onehot", [32, N_DIST])
    c.logc = take("logc", [4, N_DIST])
    c.line = take("line", [4, N_DIST])
    c.rel = take("rel", [32, H_B])
    at[0] = arena
    c.stage = [take(f"stage{i}", [P, T]) for i in range(3)]
    c.pr = take("pr", [P, T])
    c.cos = take("cos", [P, T])
    c.sin = take("sin", [P, T])
    c.psq = [take(f"psq{i}", [P, T]) for i in range(2)]
    c.pln = take("pln", [P, T])
    after_common = at[0]
    c.lat = [take(f"lat{i}", [P, T]) for i in range(3)]
    c.lath = take("lath", [P, 3, T], F32R)
    c.latl = take("latl", [P, 3, T], F32R)
    assert at[0] <= end
    at[0] = after_common
    c.rot = [take(f"rot{i}", [P, T]) for i in range(2)]
    c.st2 = [take(f"st2_{i}", [P, T]) for i in range(2)]
    at[0] = arena
    c.q1 = [take(f"q1_{i}", [P, T], F32R) for i in range(3)]
    c.q2 = [take(f"q2_{i}", [P, T], F32R) for i in range(3)]
    c.k1 = [take(f"k1_{i}", [P, T], F32R) for i in range(2)]
    c.k2 = [take(f"k2_{i}", [P, T], F32R) for i in range(2)]
    c.vt = take("vt", [P, T])
    c.vh = [take(f"vh{i}", [P, NT, P], F32R) for i in range(2)]
    vl0 = take("vl0", [P, NT, P], F32R)
    c.p = [take(f"p{i}", [P, 512]) for i in range(4)]
    c.ph = [take(f"ph{i}", [P, 512], F32R) for i in range(4)]
    c.pl = [take(f"pl{i}", [P, 512], F32R) for i in range(4)]
    c.mx = take("mx", [P, 8, 2])
    c.m = take("m", [P, NT])
    assert at[0] <= end, (at[0], end)
    at[0] = raw_at
    c.ln_den = take("ln_den", [P, 512])
    c.rden = take("rden", [P, 512])
    c.ot = take("ot", [P, 512])
    c.vl = [vl0, take("vl1", [P, NT, P], F32R)]
    c.rq = take("rq", [P, T])
    c.rk = take("rk", [P, T])
    assert at[0] <= arena
    chunk = 4 * T
    c.graw = [nc.alloc_sbuf_tensor_at(f"graw{i}", [P, GW // 2], F32, offset=h_at + (8 * i + 4) * chunk) for i in range(2)]
    c.gh = [nc.alloc_sbuf_tensor_at(f"gh{i}", [P, GW], F32R, offset=h_at + (8 * i + 5) * chunk) for i in range(2)]
    c.gl = [nc.alloc_sbuf_tensor_at(f"gl{i}", [P, GW], F32R, offset=h_at + (8 * i + 5) * chunk + 4 * GW) for i in range(2)]
    at[0] = after_y
    c.ah = take("ah", [P, 2, T], F32R)
    c.al = take("al", [P, 2, T], F32R)
    c.cb = [take(f"cb{i}", [P, T]) for i in range(4)]
    c.wh.append(take("wh2", [P, KC, P], F32R))
    c.wl.append(take("wl2", [P, KC, P], F32R))
    assert at[0] <= end, (at[0], end)
    c.ps = nc.alloc_psum_tensor("ps", [P, 8 * 512], F32)


def bank(c, b, w=512, rows=slice(0, P), off=0):
    return c.ps[rows, b * 512 + off:b * 512 + off + w]



def end_phase(nc, sems):
    nums = [s.num for s in sems]
    nc.multi_engine_barrier(list(nc.engines), sems_to_clear=range(min(nums), max(nums) + 1))


def product(pe, c, out, b, pairs):
    for k, (wh, wl, xh, xl) in enumerate(pairs):
        pe.matmul(out, wh, xh, start=(k == 0), stop=False)
        pe.matmul(out, wh, xl, start=False, stop=False)
        last = pe.matmul(out, wl, xh, start=False, stop=(k == len(pairs) - 1))
    return last


def project(pe, c, slot, half):
    for b, (t0, w) in enumerate(BLOCKS):
        last = product(pe, c, bank(c, 3 * half + b, w), b,
                       [(c.wh[slot][:, k, :], c.wl[slot][:, k, :], c.hh[:, k, t0:t0 + w], c.hl[:, k, t0:t0 + w])
                        for k in range(KC)])
    return last


def unit_psum(c, half, t0=0, t1=T, rows=slice(0, P)):
    return c.ps[rows, half * 1536 + t0:half * 1536 + t1]



def build_tables(nc, c):
    with ExitStack() as ex:
        def sem(name):
            return ex.enter_context(nc.semaphore(name))
        loaded, products, added, stored, const = sem("loaded"), sem("products"), sem("added"), sem("stored"), sem("const")
        with nc.Block() as block:
            @block.sync
            def _(sp):
                for dst, src in ((c.onehot[:], c.d_onehot), (c.logc[:], c.d_logc), (c.rel[:], c.rel_bias),
                                 (c.ident[:], c.d_ident), (c.ones[:], c.d_ones), (c.block_ones[:], c.d_block_ones),
                                 (c.perm_c[:], c.d_perm_c), (c.perm_a[:], c.d_perm_a)):
                    sp.dma_start(dst, src).then_inc(loaded, 16)
                sp.wait_ge(added, 4)
                sp.dma_start(c.s_line, c.line[:]).then_inc(stored, 16)
                sp.wait_ge(stored, 16)
                for h in range(H_B):
                    sp.dma_start(c.s_lines[h], bass.AP(tensor=c.s_line.tensor, offset=h * N_DIST, ap=[[0, P], [1, N_DIST]])).then_inc(stored, 16)
                sp.wait_ge(stored, 16 * (1 + H_B))

            @block.tensor
            def _(pe):
                pe.wait_ge(loaded, 16 * 8)
                for j in range(4):
                    pe.matmul(bank(c, j, rows=slice(0, H_B)), c.rel[:], c.onehot[:, 512 * j:512 * j + 512],
                              start=True, stop=True).then_inc(products, 1)

            @block.vector
            def _(dve):
                dve.memset(c.eps[:], EPS).then_inc(const, 1)
                for j in range(4):
                    dve.wait_ge(products, j + 1)
                    sl = slice(512 * j, 512 * j + 512)
                    dve.tensor_tensor(c.line[:, sl], bank(c, j, rows=slice(0, H_B)), c.logc[:, sl], ALU.add).then_inc(added, 1)
                dve.tensor_copy(c.ident_r[:], c.ident[:]).then_inc(const, 1)
        end_phase(nc, [loaded, products, added, stored, const])



def turn_input(nc, c):
    with ExitStack() as ex:
        def sem(name):
            return ex.enter_context(nc.semaphore(name))
        arrived = [sem(f"arrived{i}") for i in range(4)]
        turned, copied, stored = sem("turned"), sem("copied"), sem("stored")
        with nc.Block() as block:
            @block.sync
            def _(sp):
                for t in range(NT):
                    if t >= 4:
                        sp.wait_ge(turned, 2 * (t - 3))
                    src = c.x_prompt[0, t * P:(t + 1) * P, :] if t < 8 else c.x_sample[0, (t - 8) * P:(t - 7) * P, :]
                    sp.dma_start(c.tok[t % 4][:], src).then_inc(arrived[t % 4], 16)
                sp.wait_ge(copied, 2 * NT)
                sp.dma_start(c.s_x, c.y[:]).then_inc(stored, 16)
                sp.wait_ge(stored, 16)

            @block.tensor
            def _(pe):
                for t in range(NT):
                    pe.wait_ge(arrived[t % 4], 16 * (t // 4 + 1))
                    for g in range(2):
                        n = 2 * t + g
                        if n >= 8:
                            pe.wait_ge(copied, n - 7)
                        for j in range(4):
                            last = pe.transpose(bank(c, n % 8, P, off=j * P), c.tok[t % 4][:, (4 * g + j) * P:(4 * g + j + 1) * P],
                                                c.ident[:])
                        last.then_inc(turned, 1)

            @block.vector
            def _(dve):
                for n in range(2 * NT):
                    t, g = n // 2, n % 2
                    dve.wait_ge(turned, n + 1)
                    dve.tensor_copy(c.y[:, 4 * g:4 * g + 4, t * P:(t + 1) * P],
                                    bank(c, n % 8).rearrange("p (k t) -> p k t", k=4)).then_inc(copied, 1)
        end_phase(nc, arrived + [turned, copied, stored])


def turn_output(nc, c):
    with ExitStack() as ex:
        def sem(name):
            return ex.enter_context(nc.semaphore(name))
        stored = [sem(f"stored{i}") for i in range(4)]
        turned, copied = sem("turned"), sem("copied")
        with nc.Block() as block:
            @block.tensor
            def _(pe):
                for n in range(2 * NT):
                    t, g = n // 2, n % 2
                    if n >= 8:
                        pe.wait_ge(copied, n - 7)
                    for j in range(4):
                        last = pe.transpose(bank(c, n % 8, P, off=j * P), c.y[:, 4 * g + j, t * P:(t + 1) * P], c.ident[:])
                    last.then_inc(turned, 1)

            @block.vector
            def _(dve):
                for n in range(2 * NT):
                    t, g = n // 2, n % 2
                    if t >= 4 and g == 0:
                        dve.wait_ge(stored[t % 4], 16 * (t // 4))
                    dve.wait_ge(turned, n + 1)
                    dve.tensor_copy(c.tok[t % 4][:, 512 * g:512 * g + 512], bank(c, n % 8)).then_inc(copied, 1)

            @block.sync
            def _(sp):
                for t in range(NT):
                    sp.wait_ge(copied, 2 * t + 2)
                    dst = c.y_prompt[0, t * P:(t + 1) * P, :] if t < 8 else c.y_sample[0, (t - 8) * P:(t - 7) * P, :]
                    sp.dma_start(dst, c.tok[t % 4][:]).then_inc(stored[t % 4], 16)
                for i in range(4):
                    sp.wait_ge(stored[i], 16 * ((NT - 1 - i) // 4 + 1))
        end_phase(nc, stored + [turned, copied])


def load_params(nc, c, L):
    with ExitStack() as ex:
        def sem(name):
            return ex.enter_context(nc.semaphore(name))
        loaded, turned, copied = sem("loaded"), sem("turned"), sem("copied")
        nj = 2 * D_FF // P
        with nc.Block() as block:
            @block.sync
            def _(sp):
                n = 0
                for ap, row, rows in ((c.norm_mix_pre, G_MIX_PRE, 8), (c.norm_mix_post, G_MIX_POST, 8),
                                      (c.norm_ffn_pre, G_FFN_PRE, 8), (c.norm_ffn_post, G_FFN_POST, 8),
                                      (c.q_lora_norm, G_QL, 2), (c.kv_norm, G_KV, 1)):
                    sp.dma_start(c.gain_rows[row:row + rows, :],
                                 ap[bass.ds(L, 1), :].rearrange("a (r p) -> (a r) p", p=P)).then_inc(loaded, 16)
                for ap, row in ((c.c_q_norm, G_CQ), (c.c_k_norm, G_CK)):
                    for half in range(2):
                        sp.dma_start(c.gain_rows[row:row + 1, 64 * half:64 * half + 64], ap[bass.ds(L, 1), :]).then_inc(loaded, 16)
                for t in range(3):
                    sp.dma_start(c.conv_rows[:, t, :], c.conv_w[bass.ds(L, 1), t, :].rearrange("a (j p) -> (a j) p", p=P)).then_inc(loaded, 16)
                sp.dma_start(c.conv_rows[:, 3, :], c.conv_b[bass.ds(L, 1), :].rearrange("a (j p) -> (a j) p", p=P)).then_inc(loaded, 16)

            @block.tensor
            def _(pe):
                pe.wait_ge(loaded, 16 * 14)
                pe.transpose(bank(c, 0, N_GAINS), c.gain_rows[:], c.ident[0:N_GAINS, 0:N_GAINS]).then_inc(turned, 1)
                for t in range(4):
                    last = pe.transpose(bank(c, 1, nj, off=t * nj), c.conv_rows[:, t, :], c.ident[0:nj, 0:nj])
                last.then_inc(turned, 1)

            @block.vector
            def _(dve):
                dve.wait_ge(turned, 1)
                dve.tensor_copy(c.gain[:], bank(c, 0, N_GAINS)).then_inc(copied, 1)
                dve.wait_ge(turned, 2)
                dve.tensor_copy(c.conv[:], bank(c, 1, 4 * nj).rearrange("p (t j) -> p t j", t=4)).then_inc(copied, 1)
        end_phase(nc, [loaded, turned, copied])



def norm(nc, c, gain, post):
    items = [(b, t0, w, k) for b, (t0, w) in enumerate(BLOCKS) for k in range(KC)]
    with ExitStack() as ex:
        def sem(name):
            return ex.enter_context(nc.semaphore(name))
        squared, summed, logged, root = sem("squared"), sem("summed"), sem("logged"), sem("root")
        scaled, hi_done, done = sem("scaled"), sem("hi_done"), sem("done")
        old = [sem(f"old{i}") for i in range(4)]
        stored = sem("stored")
        with nc.Block() as block:
            @block.tensor
            def _(pe):
                for n, (b, t0, w, k) in enumerate(items):
                    pe.wait_ge(squared, n + 1)
                    if b == 2 and k == 0:
                        pe.wait_ge(logged, 1)
                    pe.matmul(bank(c, 6 + b % 2, w), c.ones[:], c.sq[n % 4][:, 0:w], start=(k == 0),
                              stop=(k == KC - 1)).then_inc(summed, 1)

            @block.scalar
            def _(act):
                act.preload_act_table_set(LOG_SET)
                def squares(b):
                    for n, (bb, t0, w, k) in enumerate(items):
                        if bb == b:
                            if n >= 4:
                                act.wait_ge(summed, n - 3)
                            act.activation(c.sq[n % 4][:, 0:w], c.y[:, k, t0:t0 + w], ACT.Square).then_inc(squared, 1)

                squares(0)
                for b, (t0, w) in enumerate(BLOCKS):
                    if b < 2:
                        squares(b + 1)
                    act.wait_ge(summed, KC * (b + 1))
                    act.activation(c.lnt[:, t0:t0 + w], bank(c, 6 + b % 2, w), ACT.Ln, scale=1.0 / D, bias=c.eps[:]).then_inc(logged, 1)
                    act.wait_ge(logged, b + 1)
                    act.activation(c.r[:, t0:t0 + w], c.lnt[:, t0:t0 + w], ACT.Exp, scale=-0.5).then_inc(root, 1)
                    if not post:
                        for n, (bb, _, _, k) in enumerate(items):
                            if bb == b:
                                act.wait_ge(scaled, n + 1)
                                act.activation(c.hh[:, k, t0:t0 + w], c.tmp[n % 4][:, 0:w], ACT.Copy).then_inc(hi_done, 1)

            @block.vector
            def _(dve):
                for n, (b, t0, w, k) in enumerate(items):
                    if k == 0:
                        dve.wait_ge(root, b + 1)
                    if n >= 4:
                        dve.wait_ge(done, n - 3)
                    dve.scalar_tensor_tensor(out=c.tmp[n % 4][:, 0:w], in0=c.y[:, k, t0:t0 + w], scalar=c.gain[:, gain + k:gain + k + 1],
                                             in1=c.r[:, t0:t0 + w], op0=ALU.mult, op1=ALU.mult).then_inc(scaled, 1)

            @block.gpsimd
            def _(pool):
                for n, (b, t0, w, k) in enumerate(items):
                    tmp = c.tmp[n % 4][:, 0:w]
                    if post:
                        pool.wait_ge(scaled, n + 1)
                        pool.wait_ge(old[n % 4], 16 * (n // 4 + 1))
                        pool.tensor_tensor(c.y[:, k, t0:t0 + w], tmp, c.xo[n % 4][:, 0:w], ALU.add).then_inc(done, 1)
                    else:
                        pool.wait_ge(hi_done, n + 1)
                        pool.tensor_tensor(c.hl[:, k, t0:t0 + w], tmp, c.hh[:, k, t0:t0 + w].bitcast(F32), ALU.subtract).then_inc(done, 1)

            if post:
                @block.sync
                def _(sp):
                    def store(n):
                        b, t0, w, k = items[n]
                        sp.wait_ge(done, n + 1)
                        sp.dma_start(c.s_x[:, k, t0:t0 + w], c.y[:, k, t0:t0 + w]).then_inc(stored, 16)

                    for n, (b, t0, w, k) in enumerate(items):
                        if n >= 4:
                            store(n - 4)
                        sp.dma_start(c.xo[n % 4][:, 0:w], c.s_x[:, k, t0:t0 + w]).then_inc(old[n % 4], 16)
                    for n in range(len(items) - 4, len(items)):
                        store(n)
                    sp.wait_ge(stored, 16 * len(items))
        end_phase(nc, [squared, summed, logged, root, scaled, hi_done, done] + old + [stored])



def w_in_chunk(c, L, col):
    return c.w_in[bass.ds(L, 1), :, col:col + P].rearrange("a (k p) n -> p (a k) n", p=P)


def load_weights(sp, c, n, dst, src, raw_arrived, w_lo):
    if n >= 2:
        sp.wait_ge(w_lo, n - 1)
    sp.dma_start(dst, src).then_inc(raw_arrived[n % 2], 16)


def split_hi(act, c, n, raw_arrived, w_used, w_hi, part=lambda t: t[:], arrivals=None):
    act.wait_ge(raw_arrived[n % 2], 16 * (arrivals or n // 2 + 1))
    if n >= 2:
        act.wait_ge(w_used, n - 1)
    act.activation(part(c.wh[n % 2]), part(c.raw[n % 2]), ACT.Copy).then_inc(w_hi, 1)


def split_lo(pool, c, n, w_hi, w_lo, part=lambda t: t[:]):
    pool.wait_ge(w_hi, n + 1)
    pool.tensor_tensor(part(c.wl[n % 2]), part(c.raw[n % 2]), part(c.wh[n % 2]).bitcast(F32), ALU.subtract).then_inc(w_lo, 1)


def latent_projections(nc, c, L):
    HQ, HV = 96, 128
    wide = {4: lambda t: t[:].rearrange("p k n -> p (k n)")[:, 0:2 * H_A * HQ],
            5: lambda t: t[:].rearrange("p k n -> p (k n)")[:, 0:H_A * HV]}
    outs = [(4, 0, (0, 1), QAR), (4, P, (0, 1), QAN), (4, 2 * P, (0, 1), QAN + P),
            (5, 0, (2,), KAN), (5, P, (2,), KAN + P), (5, 2 * P, (2,), VA), (5, 3 * P, (2,), VA + P)]
    with ExitStack() as ex:
        def sem(name):
            return ex.enter_context(nc.semaphore(name))
        raw_arrived = [sem("raw_arrived0"), sem("raw_arrived1")]
        w_hi, w_lo, w_used = sem("w_hi"), sem("w_lo"), sem("w_used")
        tables, unit_done, evacuated, squared = sem("tables"), sem("unit_done"), sem("evacuated"), sem("squared")
        aux_done, aux_read_act, aux_read_dve = sem("aux_done"), sem("aux_read_act"), sem("aux_read_dve")
        root, normed, lat_hi, lat_lo = sem("root"), sem("normed"), sem("lat_hi"), sem("lat_lo")
        cos_done, roped = sem("cos_done"), sem("roped")
        stored = [sem(f"stored{i}") for i in range(3)]
        with nc.Block() as block:
            @block.sync
            def _(sp):
                sp.dma_start(c.cos[:], c.d_cos_a).then_inc(tables, 16)
                sp.dma_start(c.sin[:], c.d_sin_a).then_inc(tables, 16)
                for n in range(4):
                    load_weights(sp, c, n, c.raw[n % 2][:], w_in_chunk(c, L, P * n), raw_arrived, w_lo)
                sp.wait_ge(w_lo, 3)
                for k in range(2):
                    src = c.w_uq[bass.ds(L, 1), k * P:k * P + P, :].rearrange("a p (h n) -> (a p) h n", h=H_A)
                    dst = wide[4](c.raw[0]).rearrange("p (k n) -> p k n", k=2)[:, k, :]
                    sp.dma_start(dst[:, 0:P].rearrange("p (h n) -> p h n", h=H_A), src[:, :, 64:96]).then_inc(raw_arrived[0], 16)
                    sp.dma_start(dst[:, P:3 * P].rearrange("p (h n) -> p h n", h=H_A), src[:, :, 0:64]).then_inc(raw_arrived[0], 16)
                sp.wait_ge(w_lo, 4)
                src = c.w_ukv[bass.ds(L, 1), :, :].rearrange("a p (h n) -> (a p) h n", h=H_A)
                for part in range(2):
                    dst = wide[5](c.raw[1])[:, 256 * part:256 * part + 256].rearrange("p (h n) -> p h n", h=H_A)
                    sp.dma_start(dst, src[:, :, 64 * part:64 * part + 64]).then_inc(raw_arrived[1], 16)
                sp.wait_ge(roped, 1)
                sp.dma_start(c.s_z[KAR:KAR + 32, :], c.stage[0][0:32, :]).then_inc(stored[0], 16)
                sp.wait_ge(roped, 2)
                sp.dma_start(c.s_z[QAR:QAR + P, :], c.stage[1][:]).then_inc(stored[1], 16)
                for j in range(2, 8):
                    sp.wait_ge(evacuated, 4 + j)
                    row = outs[j - 1][3]
                    sp.dma_start(c.s_z[row:row + P, :], c.stage[j % 3][:]).then_inc(stored[j % 3], 16)
                for i in range(3):
                    sp.wait_ge(stored[i], 16 * ((7 - i) // 3 + 1))

            @block.tensor
            def _(pe):
                def aux(x, lhs_rhs, rows, w):
                    if 2 <= x < 8:
                        pe.wait_ge(aux_read_act, x - 1)
                    elif x >= 8:
                        pe.wait_ge(aux_read_dve, x - 7)
                    for k, (lhs, rhs) in enumerate(lhs_rhs):
                        last = pe.matmul(bank(c, 6 + x % 2, w, rows), lhs, rhs, start=(k == 0), stop=(k == len(lhs_rhs) - 1))
                    last.then_inc(aux_done, 1)

                for n in range(3):
                    pe.wait_ge(w_lo, n + 1)
                    if n >= 2:
                        pe.wait_ge(evacuated, n - 1)
                    last = project(pe, c, n % 2, n % 2)
                    last.then_inc(w_used, 1)
                pe.wait_ge(squared, 2)
                for b, (t0, w) in enumerate(BLOCKS):
                    aux(b, [(c.ones[:], c.psq[i][:, t0:t0 + w]) for i in range(2)], slice(0, P), w)
                pe.wait_ge(w_lo, 4)
                pe.wait_ge(evacuated, 2)
                project(pe, c, 1, 1).then_inc(w_used, 1)
                pe.wait_ge(squared, 3)
                for b, (t0, w) in enumerate(BLOCKS):
                    aux(3 + b, [(c.ones[:], c.psq[0][:, t0:t0 + w])], slice(0, P), w)
                pe.wait_ge(evacuated, 4)
                for b, (t0, w) in enumerate(BLOCKS):
                    aux(6 + b, [(c.perm_a[0:32, 0:32], c.stage[0][0:32, t0:t0 + w])], slice(0, 32), w)
                for j, (unit, col, chunks, row) in enumerate(outs):
                    m = 4 + j
                    pe.wait_ge(w_lo, unit + 1)
                    pe.wait_ge(lat_lo, 1 + max(chunks))
                    pe.wait_ge(evacuated, m - 1)
                    row_len = H_A * (HQ if unit == 4 else HV)
                    pairs = [tuple(wide[unit](t[unit % 2])[:, i * row_len + col:i * row_len + col + P] for t in (c.wh, c.wl)) + (k,)
                             for i, k in enumerate(chunks)]
                    for b, (t0, w) in enumerate(BLOCKS):
                        last = product(pe, c, bank(c, 3 * (m % 2) + b, w), b,
                                       [(wh, wl, c.lath[:, k, t0:t0 + w], c.latl[:, k, t0:t0 + w]) for wh, wl, k in pairs])
                    last.then_inc(unit_done, 1)
                    if j == 0:
                        continue
                    if j == 1:
                        pe.wait_ge(evacuated, 5)
                        for b, (t0, w) in enumerate(BLOCKS):
                            aux(9 + b, [(c.perm_a[:], c.stage[1][:, t0:t0 + w])], slice(0, P), w)

            @block.scalar
            def _(act):
                act.preload_act_table_set(LOG_SET)
                def sums(x, b, width):
                    t0, w = BLOCKS[b]
                    act.wait_ge(aux_done, x + 1)
                    if x == 3:
                        act.wait_ge(normed, 2)
                    act.activation(c.pln[:, t0:t0 + w], bank(c, 6 + x % 2, w), ACT.Ln, scale=1.0 / width, bias=c.eps[:]).then_inc(aux_read_act, 1)
                    act.wait_ge(aux_read_act, x + 1)
                    act.activation(c.pr[:, t0:t0 + w], c.pln[:, t0:t0 + w], ACT.Exp, scale=-0.5).then_inc(root, 1)

                split_hi(act, c, 0, raw_arrived, w_used, w_hi)
                split_hi(act, c, 1, raw_arrived, w_used, w_hi)
                for n in range(3):
                    if n == 2:
                        for b in range(3):
                            sums(b, b, 256)
                    act.wait_ge(w_used, n + 1)
                    if n == 2:
                        act.wait_ge(aux_done, 3)
                    act.activation(c.psq[n % 2][:], unit_psum(c, n % 2), ACT.Square).then_inc(squared, 1)
                    act.activation(c.lat[n][:], unit_psum(c, n % 2), ACT.Copy).then_inc(evacuated, 1)
                    if n < 2:
                        split_hi(act, c, n + 2, raw_arrived, w_used, w_hi)
                split_hi(act, c, 4, raw_arrived, w_used, w_hi, wide[4], 6)
                act.wait_ge(w_used, 4)
                act.activation(c.stage[0][0:32, :], unit_psum(c, 1, rows=slice(0, 32)), ACT.Copy).then_inc(evacuated, 1)
                split_hi(act, c, 5, raw_arrived, w_used, w_hi, wide[5], 4)
                for i in range(2):
                    act.wait_ge(normed, i + 1)
                    act.activation(c.lath[:, i, :], c.lat[i][:], ACT.Copy).then_inc(lat_hi, 1)
                for b in range(3):
                    sums(3 + b, b, 128)
                act.wait_ge(normed, 3)
                act.activation(c.lath[:, 2, :], c.lat[2][:], ACT.Copy).then_inc(lat_hi, 1)
                for j in range(1, 8):
                    m = 3 + j
                    act.wait_ge(unit_done, j)
                    if j >= 3:
                        act.wait_ge(stored[j % 3], 16 * (j // 3))
                    act.activation(c.stage[j % 3][:], unit_psum(c, m % 2), ACT.Copy).then_inc(evacuated, 1)

            @block.gpsimd
            def _(pool):
                for n in range(4):
                    split_lo(pool, c, n, w_hi, w_lo)
                split_lo(pool, c, 4, w_hi, w_lo, wide[4])
                split_lo(pool, c, 5, w_hi, w_lo, wide[5])
                for i in range(2):
                    pool.wait_ge(lat_hi, i + 1)
                    pool.tensor_tensor(c.latl[:, i, :], c.lat[i][:], c.lath[:, i, :].bitcast(F32), ALU.subtract).then_inc(lat_lo, 1)
                pool.wait_ge(tables, 32)
                pool.wait_ge(evacuated, 4)
                pool.wait_ge(aux_done, 3)
                pool.tensor_tensor(c.psq[1][0:32, :], c.stage[0][0:32, :], c.cos[0:32, :], ALU.mult).then_inc(cos_done, 1)
                pool.wait_ge(lat_hi, 3)
                pool.tensor_tensor(c.latl[:, 2, :], c.lat[2][:], c.lath[:, 2, :].bitcast(F32), ALU.subtract).then_inc(lat_lo, 1)
                pool.wait_ge(evacuated, 5)
                pool.wait_ge(roped, 1)
                pool.tensor_tensor(c.psq[1][:], c.stage[1][:], c.cos[:], ALU.mult).then_inc(cos_done, 1)

            @block.vector
            def _(dve):
                def scale_latent(i, gain):
                    dve.scalar_tensor_tensor(out=c.lat[i][:], in0=c.lat[i][:], scalar=c.gain[:, gain:gain + 1], in1=c.pr[:],
                                             op0=ALU.mult, op1=ALU.mult).then_inc(normed, 1)

                def rope(x0, rows, r, j):
                    for b, (t0, w) in enumerate(BLOCKS):
                        dve.wait_ge(aux_done, x0 + b + 1)
                        dve.tensor_tensor(c.psq[0][rows, t0:t0 + w], bank(c, 6 + (x0 + b) % 2, w, rows), c.sin[rows, t0:t0 + w],
                                          ALU.mult).then_inc(aux_read_dve, 1)
                    dve.wait_ge(aux_read_dve, x0 + 3 - 6)
                    dve.wait_ge(cos_done, r + 1)
                    dve.tensor_tensor(c.stage[j][rows, :], c.psq[0][rows, :], c.psq[1][rows, :], ALU.add).then_inc(roped, 1)

                dve.wait_ge(root, 3)
                dve.wait_ge(evacuated, 2)
                scale_latent(0, G_QL)
                scale_latent(1, G_QL + 1)
                dve.wait_ge(root, 6)
                dve.wait_ge(evacuated, 3)
                scale_latent(2, G_KV)
                dve.wait_ge(tables, 32)
                rope(6, slice(0, 32), 0, 0)
                dve.wait_ge(roped, 1)
                rope(9, slice(0, P), 1, 1)
        end_phase(nc, raw_arrived + [w_hi, w_lo, w_used, tables, unit_done, evacuated, squared, aux_done, aux_read_act,
                                     aux_read_dve, root, normed, lat_hi, lat_lo, cos_done, roped] + stored)


def head_projections(nc, c, L):
    UNITS = 12
    rows = [QB, QB + P, KB, KB + P, VB, VB + P, QC, QC + P, QC + 2 * P, QC + 3 * P, KC_ROW, VC]
    ROPED = range(6, 11)
    with ExitStack() as ex:
        def sem(name):
            return ex.enter_context(nc.semaphore(name))
        raw_arrived = [sem("raw_arrived0"), sem("raw_arrived1")]
        w_hi, w_lo, w_used = sem("w_hi"), sem("w_lo"), sem("w_used")
        tables, evacuated, squared, unit_sum, turned = sem("tables"), sem("evacuated"), sem("squared"), sem("unit_sum"), sem("turned")
        sum_read, turn_read, root, cos_done, added, roped = (sem("sum_read"), sem("turn_read"), sem("root"), sem("cos_done"),
                                                             sem("added"), sem("roped"))
        stored = [sem(f"stored{i}") for i in range(3)]
        with nc.Block() as block:
            @block.sync
            def _(sp):
                sp.dma_start(c.cos[:], c.d_cos_c).then_inc(tables, 16)
                sp.dma_start(c.sin[:], c.d_sin_c).then_inc(tables, 16)

                def store(n):
                    if n in ROPED:
                        sp.wait_ge(roped, n - 5)
                    else:
                        sp.wait_ge(evacuated, n + 1)
                    sp.dma_start(c.s_z[rows[n]:rows[n] + P, :], c.stage[n % 3][:]).then_inc(stored[n % 3], 16)

                for n in range(UNITS):
                    col = 416 + P * n if n < 6 else 1184 + P * (n - 6)
                    load_weights(sp, c, n, c.raw[n % 2][:], w_in_chunk(c, L, col), raw_arrived, w_lo)
                    if n >= 4:
                        store(n - 4)
                for n in range(UNITS - 4, UNITS):
                    store(n)
                for i in range(3):
                    sp.wait_ge(stored[i], 16 * 4)

            @block.tensor
            def _(pe):
                def norm_and_turn(n):
                    r = n - 6
                    pe.wait_ge(evacuated, n + 1)
                    for b, (t0, w) in enumerate(BLOCKS):
                        if 3 * r + b >= 1:
                            pe.wait_ge(sum_read, 3 * r + b)
                        pe.matmul(bank(c, 6, w), c.block_ones[:], c.psq[n % 2][:, t0:t0 + w], start=True, stop=True).then_inc(unit_sum, 1)
                        if 3 * r + b >= 1:
                            pe.wait_ge(turn_read, 3 * r + b)
                        pe.matmul(bank(c, 7, w), c.perm_c[:], c.stage[n % 3][:, t0:t0 + w], start=True, stop=True).then_inc(turned, 1)

                for n in range(UNITS):
                    pe.wait_ge(w_lo, n + 1)
                    if n >= 2:
                        pe.wait_ge(evacuated, n - 1)
                    project(pe, c, n % 2, n % 2).then_inc(w_used, 1)
                    if n - 1 in ROPED:
                        norm_and_turn(n - 1)

            @block.scalar
            def _(act):
                act.preload_act_table_set(LOG_SET)
                def roots(n):
                    r = n - 6
                    for b, (t0, w) in enumerate(BLOCKS):
                        x = 3 * r + b
                        act.wait_ge(unit_sum, x + 1)
                        if r >= 1:
                            act.wait_ge(roped, r)
                        act.activation(c.pln[:, t0:t0 + w], bank(c, 6, w), ACT.Ln, scale=1.0 / 64, bias=c.eps[:]).then_inc(sum_read, 1)
                        act.wait_ge(sum_read, x + 1)
                        act.activation(c.pr[:, t0:t0 + w], c.pln[:, t0:t0 + w], ACT.Exp, scale=-0.5).then_inc(root, 1)

                split_hi(act, c, 0, raw_arrived, w_used, w_hi)
                split_hi(act, c, 1, raw_arrived, w_used, w_hi)
                for n in range(UNITS):
                    act.wait_ge(w_used, n + 1)
                    if n >= 3:
                        act.wait_ge(stored[n % 3], 16 * (n // 3))
                    if n in ROPED:
                        if n >= 8:
                            act.wait_ge(unit_sum, 3 * (n - 7))
                        act.activation(c.psq[n % 2][:], unit_psum(c, n % 2), ACT.Square).then_inc(squared, 1)
                        g = G_CK if n == 10 else G_CQ
                        act.activation(c.stage[n % 3][:], unit_psum(c, n % 2), ACT.Identity, scale=c.gain[:, g:g + 1]).then_inc(evacuated, 1)
                    else:
                        act.activation(c.stage[n % 3][:], unit_psum(c, n % 2), ACT.Copy, scale=0.125 if n < 2 else 1.0).then_inc(evacuated, 1)
                    if n + 2 < UNITS:
                        split_hi(act, c, n + 2, raw_arrived, w_used, w_hi)
                    if n - 1 in ROPED:
                        roots(n - 1)

            @block.gpsimd
            def _(pool):
                split_lo(pool, c, 0, w_hi, w_lo)
                split_lo(pool, c, 1, w_hi, w_lo)
                pool.wait_ge(tables, 32)
                for n in range(UNITS):
                    if n + 2 < UNITS:
                        split_lo(pool, c, n + 2, w_hi, w_lo)
                    if n in ROPED:
                        pool.wait_ge(evacuated, n + 1)
                        if n >= 8:
                            pool.wait_ge(roped, n - 7)
                        pool.tensor_tensor(c.st2[n % 2][:], c.stage[n % 3][:], c.cos[:], ALU.mult).then_inc(cos_done, 1)

            @block.vector
            def _(dve):
                dve.wait_ge(tables, 32)
                for n in ROPED:
                    r = n - 6
                    rot = c.rot[n % 2]
                    for b, (t0, w) in enumerate(BLOCKS):
                        dve.wait_ge(turned, 3 * r + b + 1)
                        dve.tensor_tensor(rot[:, t0:t0 + w], bank(c, 7, w), c.sin[:, t0:t0 + w], ALU.mult).then_inc(turn_read, 1)
                    dve.wait_ge(turn_read, 3 * r + 3)
                    dve.wait_ge(cos_done, r + 1)
                    dve.tensor_tensor(rot[:], rot[:], c.st2[n % 2][:], ALU.add).then_inc(added, 1)
                    dve.wait_ge(added, r + 1)
                    dve.wait_ge(root, 3 * r + 3)
                    dve.tensor_tensor(c.stage[n % 3][:], rot[:], c.pr[:], ALU.mult).then_inc(roped, 1)
        end_phase(nc, raw_arrived + [w_hi, w_lo, w_used, tables, evacuated, squared, unit_sum, turned, sum_read, turn_read,
                                     root, cos_done, added, roped] + stored)



def attention(nc, c):
    STEPS = []
    for half in range(2):
        block = [(2 * half, 512 * half, 512, kt, kt == 0, kt == 7) for kt in range(8)]
        STEPS += block[0:4] + [(1, 1024, 256, 8 + half, half == 0, half == 1)] + block[4:8]
    NS = len(STEPS)
    FIRST = [i for i, step in enumerate(STEPS) if step[4]]
    LAST = [8, 13, 17]
    assert all(STEPS[i][0] == block and STEPS[i][5] for block, i in enumerate(LAST))
    MAXES = [(qt, 512 * kb, 512, kb) for qt in range(8) for kb in range(2)]
    MAXES[8:8] = [(8, 1024, 256, 2), (9, 1024, 256, 2)]
    NM = len(MAXES)
    assert NM == NS
    ROW_TILES = ((0, 4), (8, 10), (4, 8))
    MAX_LEAD = 12
    SIDE, ST, OB = 0, 2, 5
    RING = 4
    PV_LAG = 3
    G_TOTAL = HEADS * NS
    G_END = G_TOTAL + PV_LAG + 4
    STEP_SCALE = {"A": 96 ** -0.5, "B": 1.0, "C": 0.125}

    def kind(h):
        return "A" if h < 4 else "B" if h < 8 else "C"

    def kv(h):
        return h % 2 if h < 8 else (h - 8) // 4

    def new_kv(h):
        return 0 <= h <= 8 or h == 12

    def kv_count(h):
        return sum(new_kv(i) for i in range(h + 1))

    def pl_engine(g):
        h, i = divmod(g, NS)
        start = 0 if not new_kv(h + 1) else 7 if kind(h + 1) == "B" else 4
        return "pool" if i >= start and i % 2 else "dve"

    def pl_count(g, who):
        return sum(pl_engine(x) == who for x in range(g + 1))

    def side_work(h, i):
        work = []
        if i < NM - MAX_LEAD and 0 <= h < HEADS:
            work.append(("max", h, MAX_LEAD + i))
        if i >= NS - MAX_LEAD and 0 <= h + 1 < HEADS:
            work.append(("max", h + 1, i - (NS - MAX_LEAD)))
        if i in (3, 11) and new_kv(h + 1):
            work.append(("values", h + 1, (i - 3) // 8))
        if i == 7 and 0 <= h < HEADS:
            work.append(("row", h, 2))
        if i in (15, 17) and 0 <= h + 1 < HEADS:
            work.append(("row", h + 1, (i - 15) // 2))
        return work

    side_order = [item for g in range(-2 * NS, G_TOTAL) for item in side_work(*divmod(g, NS))]
    side_bank = {item: SIDE + n % 2 for n, item in enumerate(side_order)}

    def ended(g, lag):
        h, i = divmod(g - lag, NS)
        return [3 * h + LAST.index(i)] if 0 <= h < HEADS and i in LAST else []

    def out_block(o):
        q0, w = STEPS[LAST[o % 3]][1:3]
        r0 = 64 * (o // 3 % 2)
        return q0, w, slice(r0, r0 + 64)

    with ExitStack() as ex:
        def sem(name):
            return ex.enter_context(nc.semaphore(name))
        q_raw, k_raw, v_raw, table_raw = sem("q_raw"), sem("k_raw"), sem("v_raw"), sem("table_raw")
        consts, q_hi, k_hi, k_hi_low, q_lo, k_lo = (sem("consts"), sem("q_hi"), sem("k_hi"), sem("k_hi_low"), sem("q_lo"),
                                                    sem("k_lo"))
        table_hi, table_lo, v_turned, v_hi, v_lo = (sem("table_hi"), sem("table_lo"), sem("v_turned"), sem("v_hi"),
                                                    sem("v_lo"))
        max_scored, max_taken, max_ready, row_turned, row_copied = (sem("max_scored"), sem("max_taken"), sem("max_ready"),
                                                                    sem("row_turned"), sem("row_copied"))
        scored, exp_done, lo_pool, lo_dve, pv_done = sem("scored"), sem("exp_done"), sem("lo_pool"), sem("lo_dve"), sem("pv_done")
        ln_done, rden_done, scaled, out_hi, out_lo = sem("ln_done"), sem("rden_done"), sem("scaled"), sem("out_hi"), sem("out_lo")

        def side_read(item):
            what, h, j = item
            if what == "max":
                return max_taken, NM * h + j + 1
            if what == "values":
                return v_lo, 2 * (kv_count(h) - 1) + j + 1
            return row_copied, 3 * h + j + 1

        with nc.Block() as block:
            @block.sync
            def _(sp):
                for h in range(HEADS):
                    if h >= 1:
                        sp.wait_ge(q_hi, 3 * h)
                        sp.wait_ge(q_lo, 3 * h)
                    if kind(h) == "A":
                        sp.dma_start(c.rq[0:64, :], c.s_z[QAN + 64 * h:QAN + 64 * h + 64, :]).then_inc(q_raw, 16)
                        sp.dma_start(c.rq[64:96, :], c.s_z[QAR + 32 * h:QAR + 32 * h + 32, :]).then_inc(q_raw, 16)
                    else:
                        row = QB + 64 * (h - 4) if h < 8 else QC + 64 * (h - 8)
                        for half in range(2):
                            sp.dma_start(c.rq[64 * half:64 * half + 64, :], c.s_z[row:row + 64, :]).then_inc(q_raw, 16)
                    if not new_kv(h):
                        continue
                    n = kv_count(h) - 1
                    if n >= 1:
                        sp.wait_ge(k_lo, 3 * n)
                        if kind(h) != "A" and n > 4:
                            sp.wait_ge(k_hi_low, 3 * (n - 4))
                    if kind(h) == "A":
                        sp.dma_start(c.rk[0:64, :], c.s_z[KAN + 64 * h:KAN + 64 * h + 64, :]).then_inc(k_raw, 16)
                        sp.dma_start(c.rk[64:96, :], c.s_z[KAR:KAR + 32, :]).then_inc(k_raw, 16)
                        vrow = VA + 64 * h
                    else:
                        krow, vrow = (KB + 64 * (h - 4), VB + 64 * (h - 4)) if h < 8 else (KC_ROW + 64 * kv(h), VC + 64 * kv(h))
                        for half in range(2):
                            sp.dma_start(c.rk[64 * half:64 * half + 64, :], c.s_z[krow:krow + 64, :]).then_inc(k_raw, 16)
                    if kind(h) == "B":
                        if h > 4:
                            sp.wait_ge(table_lo, 2 * (h - 4))
                        for i in range(2):
                            src = bass.AP(tensor=c.s_lines.tensor, offset=(h - 4) * P * N_DIST + P - 1 + i * GW // 2,
                                          ap=[[N_DIST - 1, P], [1, GW // 2]])
                            sp.dma_start(c.graw[i][:], src).then_inc(table_raw, 16)
                    if n >= 1:
                        sp.wait_ge(v_turned, 2 * n)
                    sp.dma_start(c.vt[0:64, :], c.s_z[vrow:vrow + 64, :]).then_inc(v_raw, 16)

            @block.tensor
            def _(pe):
                def scores(g):
                    h, i = divmod(g, NS)
                    block, q0, w, kt, first, last = STEPS[i]
                    out = bank(c, ST + g % 3, w)
                    q1, q2, k1, k2 = c.q1[h % 3], c.q2[h % 3], c.k1[kv(h)], c.k2[kv(h)]
                    if g >= 3:
                        pe.wait_ge(exp_done, 2 * (g - 2))
                    if i == 0:
                        pe.wait_ge(q_lo, 3 * (h + 1))
                        pe.wait_ge(k_lo, 3 * kv_count(h))
                        if h == 0:
                            pe.wait_ge(consts, 6)
                        if h in (4, 5):
                            pe.wait_ge(consts, h + 3)
                        if h >= 4 and new_kv(h):
                            pe.wait_ge(k_hi_low, 3 * (kv_count(h) - 4))
                        if kind(h) == "B":
                            pe.wait_ge(table_lo, 2 * (h - 3))
                    if first:
                        pe.wait_ge(row_copied, 3 * h + block + 1)
                    ks, qs = slice(kt * P, kt * P + P), slice(q0, q0 + w)
                    if kind(h) == "A":
                        prods = [(k1[0:97, ks], q1[0:97, qs]), (k2[0:96, ks], q1[0:96, qs]), (k1[0:96, ks], q2[0:96, qs])]
                    else:
                        prods = [(k1[:, ks], q1[:, qs]), (k2[0:65, ks], q2[0:65, qs])]
                    if kind(h) == "B":
                        x0 = (q0 - kt * P) + 896
                        prods += [(c.ident_r[:], c.gh[h % 2][:, x0:x0 + w]), (c.ident_r[:], c.gl[h % 2][:, x0:x0 + w])]
                    for k, (a, b) in enumerate(prods):
                        mm = pe.matmul(out, a, b, start=(k == 0), stop=(k == len(prods) - 1))
                    mm.then_inc(scored, 1)

                def values(g):
                    h, i = divmod(g, NS)
                    block, q0, w, kt, first, last = STEPS[i]
                    if first and h >= 1:
                        pe.wait_ge(scaled, 3 * (h - 1) + block + 1)
                    if i == 0:
                        pe.wait_ge(v_lo, 2 * kv_count(h))
                    out = bank(c, OB + block, w)
                    pe.wait_ge(exp_done, 2 * g + 1)
                    pe.matmul(out, c.vh[kv(h)][:, kt, :], c.ph[g % RING][:, 0:w], start=first, stop=False)
                    pe.matmul(out, c.vl[kv(h)][:, kt, :], c.ph[g % RING][:, 0:w], start=False, stop=False)
                    who = pl_engine(g)
                    pe.wait_ge(lo_dve if who == "dve" else lo_pool, pl_count(g, who))
                    pe.matmul(out, c.vh[kv(h)][:, kt, :], c.pl[g % RING][:, 0:w], start=False, stop=last).then_inc(pv_done, 1)

                def max_scores(h, j, b):
                    qt, k0, w, kb = MAXES[j]
                    pe.wait_ge(q_hi, 3 * h + qt // 4 + 1)
                    if kind(h) == "A":
                        pe.wait_ge(k_hi, 3 * (kv_count(h) - 1) + kb + 1)
                    else:
                        pe.wait_ge(k_lo, 3 * (kv_count(h) - 1) + kb + 1)
                    if kind(h) == "B":
                        pe.wait_ge(table_hi, 2 * (h - 3))
                    r = 96 if kind(h) == "A" else P
                    out = bank(c, b, w)
                    mm = pe.matmul(out, c.q1[h % 3][0:r, qt * P:qt * P + P], c.k1[kv(h)][0:r, k0:k0 + w], start=True, stop=kind(h) != "B")
                    if kind(h) == "B":
                        for kk in range(w // P):
                            x0 = qt * P - (k0 + kk * P) + 896
                            mm = pe.matmul(out[:, kk * P:kk * P + P], c.gh[h % 2][:, x0:x0 + P], c.ident_r[:],
                                           start=False, stop=(kk == w // P - 1))
                    mm.then_inc(max_scored, 1)

                def turn_values(h, part, b):
                    pe.wait_ge(v_raw, 16 * kv_count(h))
                    for t in (range(8) if part == 0 else range(8, 10)):
                        mm = pe.transpose(bank(c, b, 64, off=(t % 8) * 64), c.vt[0:64, t * P:t * P + P], c.ident[0:64, 0:64])
                    mm.then_inc(v_turned, 1)

                def turn_row(h, r, b):
                    if r == 1:
                        pe.wait_ge(max_taken, NM * h + 10)
                    else:
                        pe.wait_ge(max_ready, 2 * h + r // 2 + 1)
                    for k, qt in enumerate(range(*ROW_TILES[r])):
                        mm = pe.matmul(bank(c, b, P, slice(0, 1), off=k * P), c.m[:, qt:qt + 1], c.ident[:], start=True, stop=True)
                    mm.then_inc(row_turned, 1)

                n = 0
                for g in range(-2 * NS, G_TOTAL + PV_LAG):
                    if 0 <= g < G_TOTAL:
                        scores(g)
                    for item in side_work(*divmod(g, NS)):
                        if n >= 2:
                            pe.wait_ge(*side_read(side_order[n - 2]))
                        what, h, j = item
                        if what == "max":
                            max_scores(h, j, side_bank[item])
                        elif what == "values":
                            turn_values(h, j, side_bank[item])
                        else:
                            turn_row(h, j, side_bank[item])
                        n += 1
                    if g >= PV_LAG:
                        values(g - PV_LAG)

            @block.scalar
            def _(act):
                act.preload_act_table_set(LOG_SET)

                def split_q(h, b):
                    t0, w = BLOCKS[b]
                    act.wait_ge(q_raw, 32 * (h + 1))
                    if h >= 3:
                        act.wait_ge(scored, NS * (h - 2))
                    r = 96 if kind(h) == "A" else P
                    act.activation(c.q1[h % 3][0:r, t0:t0 + w], c.rq[0:r, t0:t0 + w], ACT.Copy).then_inc(q_hi, 1)

                def split_k(h, b):
                    t0, w = BLOCKS[b]
                    act.wait_ge(k_raw, 32 * kv_count(h))
                    if h >= 2:
                        act.wait_ge(scored, NS * (h - 1))
                    if kind(h) == "A":
                        act.activation(c.k1[kv(h)][0:96, t0:t0 + w], c.rk[0:96, t0:t0 + w], ACT.Copy).then_inc(k_hi, 1)
                    else:
                        act.activation(c.k1[kv(h)][:, t0:t0 + w], c.rk[:, t0:t0 + w], ACT.Copy).then_inc(k_hi, 1)
                        act.activation(c.k2[kv(h)][0:64, t0:t0 + w], c.rk[0:64, t0:t0 + w], ACT.Copy).then_inc(k_hi_low, 1)

                def split_table(h, i):
                    act.wait_ge(table_raw, 32 * (h - 3))
                    act.activation(c.gh[h % 2][:, i * GW // 2:(i + 1) * GW // 2], c.graw[i][:], ACT.Copy).then_inc(table_hi, 1)

                def copy_row(h, r, b):
                    act.wait_ge(row_turned, 3 * h + r + 1)
                    t0, t1 = (x * P for x in ROW_TILES[r])
                    row = c.q1[h % 3][96:97, t0:t1] if kind(h) == "A" else c.q2[h % 3][64:65, t0:t1]
                    act.activation(row, bank(c, b, t1 - t0, slice(0, 1)), ACT.Copy).then_inc(row_copied, 1)

                def denominators(o):
                    q0, w, rows = out_block(o)
                    act.wait_ge(pv_done, o // 3 * NS + LAST[o % 3] + 1)
                    if o >= 1:
                        act.wait_ge(scaled, o)
                    act.activation(c.ln_den[0:64, 0:w], bank(c, OB + o % 3, w, slice(64, P)), ACT.Ln).then_inc(ln_done, 1)
                    act.wait_ge(ln_done, o + 1)
                    act.activation(c.rden[0:64, 0:w], c.ln_den[0:64, 0:w], ACT.Exp, scale=-1.0).then_inc(rden_done, 1)

                for g in range(-2 * NS, G_END):
                    h, i = divmod(g, NS)
                    if 0 <= g < G_TOTAL:
                        w = STEPS[i][2]
                        scores = bank(c, ST + g % 3, w)
                        act.wait_ge(scored, g + 1)
                        if g >= RING:
                            act.wait_ge(pv_done, g - RING + 1)
                        act.activation(c.ph[g % RING][:, 0:w], scores, ACT.Exp, scale=STEP_SCALE[kind(h)]).then_inc(exp_done, 1)
                        act.activation(c.p[g % RING][:, 0:w], scores, ACT.Exp, scale=STEP_SCALE[kind(h)]).then_inc(exp_done, 1)
                    if i in (9, 11, 13) and h + 2 < HEADS:
                        split_q(h + 2, (i - 9) // 2)
                    if i < 3 and new_kv(h + 1):
                        split_k(h + 1, i)
                    if i in (3, 4) and kind(h + 1) == "B":
                        split_table(h + 1, i - 3)
                    for what, head, j in side_work(h, i):
                        if what == "row":
                            copy_row(head, j, side_bank[what, head, j])
                    for o in ended(g, PV_LAG + 1):
                        denominators(o)

            @block.gpsimd
            def _(pool):
                before = [None, None, 0]

                def settle(rows, semaphore, count):
                    if before[0] is not None and before[0] != rows:
                        pool.wait_ge(before[1], before[2])
                    before[:] = [rows, semaphore, count]

                def lo_q(h, b):
                    t0, w = BLOCKS[b]
                    r = 96 if kind(h) == "A" else 64
                    pool.wait_ge(q_hi, 3 * h + b + 1)
                    settle((0, r), q_lo, 3 * h + b + 1)
                    pool.tensor_tensor(c.q2[h % 3][0:r, t0:t0 + w], c.rq[0:r, t0:t0 + w], c.q1[h % 3][0:r, t0:t0 + w].bitcast(F32),
                                       ALU.subtract).then_inc(q_lo, 1)

                def lo_k(h, b):
                    t0, w = BLOCKS[b]
                    n = 3 * (kv_count(h) - 1) + b + 1
                    pool.wait_ge(k_hi, n)
                    if kind(h) == "A":
                        rows, out = slice(0, 96), c.k2[kv(h)]
                    else:
                        rows, out = slice(64, P), c.k1[kv(h)]
                    settle((rows.start, rows.stop), k_lo, n)
                    pool.tensor_tensor(out[rows, t0:t0 + w], c.rk[rows, t0:t0 + w], c.k1[kv(h)][rows, t0:t0 + w].bitcast(F32),
                                       ALU.subtract).then_inc(k_lo, 1)

                def lo_table(h, i):
                    sl = slice(i * GW // 2, (i + 1) * GW // 2)
                    n = 2 * (h - 4) + i + 1
                    pool.wait_ge(table_hi, n)
                    settle((0, P), table_lo, n)
                    pool.tensor_tensor(c.gl[h % 2][:, sl], c.graw[i][:], c.gh[h % 2][:, sl].bitcast(F32), ALU.subtract).then_inc(table_lo, 1)

                def lo_output(o):
                    q0, w, rows = out_block(o)
                    pool.wait_ge(out_hi, o + 1)
                    settle((rows.start, rows.stop), out_lo, o + 1)
                    pool.tensor_tensor(c.hl[rows, o // 6, q0:q0 + w], c.ot[rows, 0:w], c.hh[rows, o // 6, q0:q0 + w].bitcast(F32),
                                       ALU.subtract).then_inc(out_lo, 1)

                for g in range(-2 * NS, G_END):
                    h, i = divmod(g, NS)
                    if 0 <= g < G_TOTAL and pl_engine(g) == "pool":
                        w = STEPS[i][2]
                        pool.wait_ge(exp_done, 2 * g + 2)
                        if g >= RING:
                            pool.wait_ge(pv_done, g - RING + 1)
                        settle((0, P), lo_pool, pl_count(g, "pool"))
                        pool.tensor_tensor(c.pl[g % RING][:, 0:w], c.p[g % RING][:, 0:w], c.ph[g % RING][:, 0:w].bitcast(F32),
                                           ALU.subtract).then_inc(lo_pool, 1)
                    if i in (9, 11, 13) and h + 2 < HEADS:
                        lo_q(h + 2, (i - 9) // 2)
                    if i < 3 and new_kv(h + 1):
                        lo_k(h + 1, i)
                    if i in (4, 5) and kind(h + 1) == "B":
                        lo_table(h + 1, i - 4)
                    for o in ended(g, PV_LAG + 3):
                        lo_output(o)

            @block.vector
            def _(dve):
                def take_max(h, j, b):
                    qt, k0, w, kb = MAXES[j]
                    if h >= 1 and j == 0:
                        dve.wait_ge(max_ready, 2 * h)
                    if h >= 1 and j == 8:
                        dve.wait_ge(row_turned, 3 * h - 1)
                    dve.wait_ge(max_scored, NM * h + j + 1)
                    if qt < 8:
                        dve.tensor_reduce(c.mx[:, qt, kb:kb + 1], bank(c, b, w), AX.X, ALU.max).then_inc(max_taken, 1)
                    else:
                        dve.tensor_reduce(c.m[:, qt:qt + 1], bank(c, b, w), AX.X, ALU.max, negate=True).then_inc(max_taken, 1)
                    if j in (7, 17):
                        r = j // 16
                        dve.wait_ge(max_taken, NM * h + j + 1)
                        if h >= 1:
                            dve.wait_ge(row_turned, 3 * (h - 1) + 2 * r + 1)
                        dve.tensor_reduce(c.m[:, 4 * r:4 * r + 4], c.mx[:, 4 * r:4 * r + 4, :], AX.X, ALU.max, negate=True).then_inc(max_ready, 1)

                def split_values(h, part, b):
                    n = kv_count(h) - 1
                    tiles, nt = (slice(0, 8), 8) if part == 0 else (slice(8, 10), 2)
                    src = bank(c, b, 64 * nt).rearrange("p (t v) -> p t v", v=64)
                    dve.wait_ge(v_turned, 2 * n + part + 1)
                    if h >= 2:
                        dve.wait_ge(pv_done, NS * (h - 1))
                    elif part == 0:
                        dve.wait_ge(consts, 6)
                    dve.tensor_copy(c.vh[kv(h)][:, tiles, 0:64], src).then_inc(v_hi, 1)
                    dve.wait_ge(v_hi, 2 * n + part + 1)
                    dve.tensor_tensor(c.vl[kv(h)][:, tiles, 0:64], src, c.vh[kv(h)][:, tiles, 0:64].bitcast(F32), ALU.subtract).then_inc(v_lo, 1)

                def scale_output(o):
                    q0, w, rows = out_block(o)
                    dve.wait_ge(rden_done, o + 1)
                    if o >= 1:
                        dve.wait_ge(out_lo, o)
                    dve.tensor_tensor(c.ot[rows, 0:w], bank(c, OB + o % 3, w, slice(0, 64)), c.rden[0:64, 0:w], ALU.mult).then_inc(scaled, 1)
                    dve.wait_ge(scaled, o + 1)
                    dve.tensor_copy(c.hh[rows, o // 6, q0:q0 + w], c.ot[rows, 0:w]).then_inc(out_hi, 1)

                for i in range(2):
                    dve.memset(c.k1[i][96:97, :].bitcast(F32), 1.0).then_inc(consts, 1)
                    dve.memset(c.vh[i][:, :, 64:P].bitcast(F32), 1.0).then_inc(consts, 1)
                    dve.memset(c.vl[i][:, :, 64:P].bitcast(F32), 0.0).then_inc(consts, 1)
                for g in range(-2 * NS, G_END):
                    h, i = divmod(g, NS)
                    if i == 1 and h + 1 in (4, 5):
                        dve.wait_ge(scored, NS * h)
                        dve.memset(c.k2[kv(h + 1)][64:65, :].bitcast(F32), 1.0).then_inc(consts, 1)
                    for what, head, j in side_work(h, i):
                        if what == "max":
                            take_max(head, j, side_bank[what, head, j])
                        elif what == "values":
                            split_values(head, j, side_bank[what, head, j])
                    if 0 <= g < G_TOTAL and pl_engine(g) == "dve":
                        w = STEPS[i][2]
                        dve.wait_ge(exp_done, 2 * g + 2)
                        if g >= RING:
                            dve.wait_ge(pv_done, g - RING + 1)
                        dve.tensor_tensor(c.pl[g % RING][:, 0:w], c.p[g % RING][:, 0:w], c.ph[g % RING][:, 0:w].bitcast(F32),
                                          ALU.subtract).then_inc(lo_dve, 1)
                    for o in ended(g, PV_LAG + 2):
                        scale_output(o)
        end_phase(nc, [q_raw, k_raw, v_raw, table_raw, consts, q_hi, k_hi, k_hi_low, q_lo, k_lo, table_hi, table_lo, v_turned, v_hi,
                       v_lo, max_scored, max_taken, max_ready, row_turned, row_copied, scored, exp_done, lo_pool, lo_dve,
                       pv_done, ln_done, rden_done, scaled, out_hi, out_lo])



def output_projection(nc, c, L):
    with ExitStack() as ex:
        def sem(name):
            return ex.enter_context(nc.semaphore(name))
        raw_arrived = [sem("raw_arrived0"), sem("raw_arrived1")]
        w_hi, w_lo, w_used, evacuated = sem("w_hi"), sem("w_lo"), sem("w_used"), sem("evacuated")
        with nc.Block() as block:
            @block.sync
            def _(sp):
                for n in range(KC):
                    load_weights(sp, c, n, c.raw[n % 2][:],
                                 c.w_out[bass.ds(L, 1), :, n * P:n * P + P].rearrange("a (k p) n -> p (a k) n", p=P), raw_arrived, w_lo)

            @block.tensor
            def _(pe):
                for n in range(KC):
                    pe.wait_ge(w_lo, n + 1)
                    if n >= 2:
                        pe.wait_ge(evacuated, n - 1)
                    project(pe, c, n % 2, n % 2).then_inc(w_used, 1)

            @block.scalar
            def _(act):
                split_hi(act, c, 0, raw_arrived, w_used, w_hi)
                split_hi(act, c, 1, raw_arrived, w_used, w_hi)
                for n in range(KC):
                    act.wait_ge(w_used, n + 1)
                    act.activation(c.y[:, n, :], unit_psum(c, n % 2), ACT.Copy).then_inc(evacuated, 1)
                    if n + 2 < KC:
                        split_hi(act, c, n + 2, raw_arrived, w_used, w_hi)

            @block.gpsimd
            def _(pool):
                for n in range(KC):
                    split_lo(pool, c, n, w_hi, w_lo)
        end_phase(nc, raw_arrived + [w_hi, w_lo, w_used, evacuated])



def gated_mlp(nc, c, L):
    def first(i):
        return 4 + 6 * (i - 1)

    with ExitStack() as ex:
        def sem(name):
            return ex.enter_context(nc.semaphore(name))
        raw_arrived = [sem("raw_arrived0"), sem("raw_arrived1")]
        w_hi, w_lo, w_used = sem("w_hi"), sem("w_lo"), sem("w_used")
        up_done, centred, shifted, gelu_done, gated, act_hi, act_lo = (sem("up_done"), sem("centred"), sem("shifted"),
            sem("gelu_done"), sem("gated"), sem("act_hi"), sem("act_lo"))
        down_done, down_added, cleared, left = sem("down_done"), sem("down_added"), sem("cleared"), sem("left")
        with nc.Block() as block:
            def up_src(i, unit):
                col = (i * 2 + unit // 2) * P + (unit % 2) * D_FF
                return c.w_up[bass.ds(L, 1), :, bass.ds(col, P)].rearrange("a (k p) n -> p (a k) n", p=P)

            def down_src(i, k):
                return c.w_down[bass.ds(L, 1), bass.ds((i * 2 + k) * P, P), :].rearrange("a p n -> p (a n)")

            @block.sync
            def _(sp):
                def load(n, parity, src, flat=False):
                    sp.wait_ge(w_lo, n - 1)
                    dst = c.raw[parity][:].rearrange("p k n -> p (k n)") if flat else c.raw[parity][:]
                    sp.dma_start(dst, src).then_inc(raw_arrived[parity], 16)

                sp.dma_start(c.raw[0][:], up_src(0, 0)).then_inc(raw_arrived[0], 16)
                sp.dma_start(c.raw[1][:], up_src(0, 1)).then_inc(raw_arrived[1], 16)
                load(2, 0, up_src(0, 2))
                load(3, 1, up_src(0, 3))
                with sp.Fori(1, FF_PAIRS) as i:
                    n = first(i)
                    load(n, 0, up_src(i, 0))
                    load(n + 1, 1, down_src(i - 1, 0), True)
                    load(n + 2, 0, down_src(i - 1, 1), True)
                    load(n + 3, 1, up_src(i, 1))
                    load(n + 4, 0, up_src(i, 2))
                    load(n + 5, 1, up_src(i, 3))
                n = first(FF_PAIRS)
                load(n, 0, down_src(FF_PAIRS - 1, 0), True)
                load(n + 1, 1, down_src(FF_PAIRS - 1, 1), True)

            @block.tensor
            def _(pe):
                def up(n, slot, m, half, wait=True):
                    pe.wait_ge(w_lo, n + 1)
                    if wait:
                        pe.wait_ge(shifted, m - 1)
                    project(pe, c, slot, half).then_inc(w_used, 1)

                def down(n, slots, it, wait=True):
                    pe.wait_ge(w_lo, n + 2)
                    pe.wait_ge(act_lo, it * 2)
                    for u in range(24):
                        o, (t0, w) = u // 3, BLOCKS[u % 3]
                        if u >= 2:
                            pe.wait_ge(down_added, (it - 1) * 24 + u - 1)
                        elif wait:
                            pe.wait_ge(down_added, (it - 1) * 24 + u - 1)
                        last = product(pe, c, bank(c, 6 + u % 2, w), 0,
                                       [(c.wh[s][:, o, :], c.wl[s][:, o, :], c.ah[:, k, t0:t0 + w], c.al[:, k, t0:t0 + w])
                                        for k, s in enumerate(slots)])
                        if u == 23:
                            last.then_inc(w_used, 2)
                        else:
                            last.then_inc(down_done, 1)

                up(0, 0, 0, 0, False)
                up(1, 1, 1, 1, False)
                up(2, 2, 2, 0)
                up(3, 0, 3, 1)
                n = first(1)
                up(n, 1, 4, 0)
                down(n + 1, (2, 0), 1, False)
                up(n + 3, 1, 5, 1)
                up(n + 4, 2, 6, 0)
                up(n + 5, 0, 7, 1)
                with pe.Fori(2, FF_PAIRS) as i:
                    n = first(i)
                    up(n, 1, 4 * i, 0)
                    down(n + 1, (2, 0), i)
                    up(n + 3, 1, 4 * i + 1, 1)
                    up(n + 4, 2, 4 * i + 2, 0)
                    up(n + 5, 0, 4 * i + 3, 1)
                down(first(FF_PAIRS), (1, 2), FF_PAIRS)

            def split(act, n, slot, parity, raws, wait=True):
                act.wait_ge(raw_arrived[parity], 16 * raws)
                if wait:
                    act.wait_ge(w_used, n - 2)
                act.activation(c.wh[slot][:], c.raw[parity][:], ACT.Copy).then_inc(w_hi, 1)

            @block.scalar
            def _(act):
                def centre(i, unit, used):
                    act.wait_ge(w_used, used)
                    j = i * 2 + unit // 2 + (unit % 2) * (D_FF // P)
                    act.activation(c.cb[unit][:], unit_psum(c, unit % 2), ACT.Identity, scale=c.conv[:, 1, bass.ds(j, 1)],
                                   bias=c.conv[:, 3, bass.ds(j, 1)]).then_inc(centred, 1)

                def gelu(i, k):
                    act.wait_ge(shifted, i * 4 + 2 * k + 1)
                    act.activation(c.cb[2 * k][:], c.cb[2 * k][:], ACT.Gelu_apprx_tanh).then_inc(gelu_done, 1)

                def hi(i, k):
                    act.wait_ge(gated, i * 2 + k + 1)
                    act.activation(c.ah[:, k, :], c.cb[2 * k][:], ACT.Copy).then_inc(act_hi, 1)

                split(act, 0, 0, 0, 1, False)
                split(act, 1, 1, 1, 1, False)
                split(act, 2, 2, 0, 2, False)
                centre(0, 0, 1)
                split(act, 3, 0, 1, 2)
                gelu(0, 0)
                centre(0, 1, 2)
                split(act, 4, 1, 0, 3)
                hi(0, 0)
                centre(0, 2, 3)
                split(act, 5, 2, 1, 3)
                gelu(0, 1)
                centre(0, 3, 4)
                hi(0, 1)
                with act.Fori(1, FF_PAIRS) as i:
                    n = first(i)
                    half = 2 + 3 * (i - 1)
                    split(act, n + 2, 0, 0, half + 2)
                    act.wait_ge(act_lo, i * 2)
                    centre(i, 0, n + 1)
                    split(act, n + 3, 1, 1, half + 2)
                    gelu(i, 0)
                    split(act, n + 4, 2, 0, half + 3)
                    split(act, n + 5, 0, 1, half + 3)
                    centre(i, 1, n + 4)
                    split(act, n + 6, 1, 0, half + 4)
                    hi(i, 0)
                    centre(i, 2, n + 5)
                    split(act, n + 7, 2, 1, half + 4)
                    gelu(i, 1)
                    centre(i, 3, n + 6)
                    hi(i, 1)

            @block.gpsimd
            def _(pool):
                def lo(n, slot, parity):
                    pool.wait_ge(w_hi, n + 1)
                    pool.tensor_tensor(c.wl[slot][:], c.raw[parity][:], c.wh[slot][:].bitcast(F32), ALU.subtract).then_inc(w_lo, 1)

                def act_low(i, k):
                    pool.wait_ge(act_hi, i * 2 + k + 1)
                    pool.tensor_tensor(c.al[:, k, :], c.cb[2 * k][:], c.ah[:, k, :].bitcast(F32), ALU.subtract).then_inc(act_lo, 1)

                lo(0, 0, 0)
                lo(1, 1, 1)
                pool.memset(c.y[:], 0.0).then_inc(cleared, 1)
                lo(2, 2, 0)
                lo(3, 0, 1)
                lo(4, 1, 0)
                act_low(0, 0)
                lo(5, 2, 1)
                act_low(0, 1)
                with pool.Fori(1, FF_PAIRS) as i:
                    n = first(i)
                    lo(n + 2, 0, 0)
                    lo(n + 3, 1, 1)
                    lo(n + 4, 2, 0)
                    lo(n + 5, 0, 1)
                    lo(n + 6, 1, 0)
                    act_low(i, 0)
                    lo(n + 7, 2, 1)
                    act_low(i, 1)

            @block.vector
            def _(dve):
                def shift(i, unit):
                    m = i * 4 + unit
                    j = i * 2 + unit // 2 + (unit % 2) * (D_FF // P)
                    dve.wait_ge(centred, m + 1)
                    for seg, (t0, s) in enumerate(SEGS):
                        dve.scalar_tensor_tensor(out=c.cb[unit][:, t0 + 1:t0 + s], in0=unit_psum(c, unit % 2, t0, t0 + s - 1),
                                                 scalar=c.conv[:, 0, bass.ds(j, 1)], in1=c.cb[unit][:, t0 + 1:t0 + s],
                                                 op0=ALU.mult, op1=ALU.add).then_inc(left, 1)
                    dve.wait_ge(left, m * 2 + 2)
                    for seg, (t0, s) in enumerate(SEGS):
                        mm = dve.scalar_tensor_tensor(out=c.cb[unit][:, t0:t0 + s - 1], in0=unit_psum(c, unit % 2, t0 + 1, t0 + s),
                                                      scalar=c.conv[:, 2, bass.ds(j, 1)], in1=c.cb[unit][:, t0:t0 + s - 1],
                                                      op0=ALU.mult, op1=ALU.add)
                    mm.then_inc(shifted, 1)

                def gate(i, k):
                    dve.wait_ge(gelu_done, i * 2 + k + 1)
                    dve.wait_ge(shifted, i * 4 + 2 * k + 2)
                    dve.tensor_tensor(c.cb[2 * k][:], c.cb[2 * k][:], c.cb[2 * k + 1][:], ALU.mult).then_inc(gated, 1)

                def add_down(it):
                    for u in range(24):
                        o, (t0, w) = u // 3, BLOCKS[u % 3]
                        if u == 23:
                            dve.wait_ge(w_used, first(it) + 3)
                        else:
                            dve.wait_ge(down_done, (it - 1) * 23 + u + 1)
                        dve.tensor_tensor(c.y[:, o, t0:t0 + w], bank(c, 6 + u % 2, w), c.y[:, o, t0:t0 + w], ALU.add).then_inc(down_added, 1)

                for unit in range(4):
                    shift(0, unit)
                    if unit % 2:
                        gate(0, unit // 2)
                dve.wait_ge(cleared, 1)
                with dve.Fori(1, FF_PAIRS) as i:
                    shift(i, 0)
                    add_down(i)
                    for unit in range(1, 4):
                        shift(i, unit)
                        if unit % 2:
                            gate(i, unit // 2)
                for u in range(24):
                    o, (t0, w) = u // 3, BLOCKS[u % 3]
                    if u == 23:
                        dve.wait_ge(w_used, first(FF_PAIRS) + 2)
                    else:
                        dve.wait_ge(down_done, (FF_PAIRS - 1) * 23 + u + 1)
                    dve.tensor_tensor(c.y[:, o, t0:t0 + w], bank(c, 6 + u % 2, w), c.y[:, o, t0:t0 + w], ALU.add).then_inc(down_added, 1)
        end_phase(nc, raw_arrived + [w_hi, w_lo, w_used, up_done, centred, shifted, gelu_done, gated, act_hi, act_lo,
                                     down_done, down_added, cleared, left])


def encoder(nc, c):
    c.s_x = nc.dram_tensor("residual", (P, KC, T), F32, kind="Internal").ap()
    c.s_z = nc.dram_tensor("heads", (Z_ROWS, T), F32, kind="Internal").ap()
    c.s_line = nc.dram_tensor("distance_lines", (H_B, N_DIST), F32, kind="Internal").ap()
    c.s_lines = nc.dram_tensor("distance_tables", (H_B, P, N_DIST), F32, kind="Internal").ap()
    place_buffers(nc, c)
    build_tables(nc, c)
    turn_input(nc, c)
    with nc.Fori(0, DEPTH) as L:
        load_params(nc, c, L)
        norm(nc, c, G_MIX_PRE, False)
        latent_projections(nc, c, L)
        head_projections(nc, c, L)
        attention(nc, c)
        output_projection(nc, c, L)
        norm(nc, c, G_MIX_POST, True)
        norm(nc, c, G_FFN_PRE, False)
        gated_mlp(nc, c, L)
        norm(nc, c, G_FFN_POST, True)
    turn_output(nc, c)



def rope_tables(positions, n_freq):
    inv = np.float32(10000.0) ** (-np.arange(n_freq, dtype=np.float32) / np.float32(n_freq))
    ang = positions.astype(np.float32)[None, :] * inv.astype(np.float32)[:, None]
    return np.cos(ang).astype(np.float32), np.sin(ang).astype(np.float32)


def swap_halves(n, width):
    m = np.zeros((n, n), np.float32)
    h = width // 2
    for g in range(0, n, width):
        for i in range(h):
            m[g + h + i, g + i] = -1.0
            m[g + i, g + h + i] = 1.0
    return m


def distance_constants():
    dist = 1023 - np.arange(N_DIST)
    half, exact = 16, 8
    n = np.abs(dist)
    large = exact + (np.log(np.maximum(n, 1) / exact) / math.log(1024 / exact) * (half - exact)).astype(np.int32)
    bucket = np.where(dist > 0, half, 0) + np.where(n < exact, n, np.minimum(large, half - 1))
    onehot = (bucket[None, :] == np.arange(32)[:, None]).astype(np.float32)
    count = np.zeros(N_DIST, np.int64)
    for window, dilation in ((128, 1), (512, 4), (2048, 16)):
        count += (n % dilation == 0) & (n // dilation <= window // (2 * dilation))
    logc = np.where(count > 0, np.log(np.maximum(count, 1)), MASKED).astype(np.float32)
    return onehot, np.ascontiguousarray(np.broadcast_to(logc, (H_B, N_DIST)))


def shape_constants():
    pos = np.concatenate([np.arange(s) for _, s in SEGS])
    cos_a, sin_a = rope_tables(pos, 16)
    cos_r, sin_r = rope_tables(pos // 64, 16)
    cos_l, sin_l = rope_tables(pos % 64, 16)
    onehot, logc = distance_constants()
    return {
        "cos_a": np.tile(cos_a, (8, 1)), "sin_a": np.tile(sin_a, (8, 1)),
        "cos_c": np.tile(np.concatenate([cos_r, cos_r, cos_l, cos_l]), (2, 1)),
        "sin_c": np.tile(np.concatenate([sin_r, sin_r, sin_l, sin_l]), (2, 1)),
        "onehot": onehot, "logc": logc, "ident": np.eye(P, dtype=np.float32), "ones": np.ones((P, P), np.float32),
        "block_ones": np.kron(np.eye(2, dtype=np.float32), np.ones((64, 64), np.float32)),
        "perm_c": swap_halves(P, 32), "perm_a": swap_halves(P, 32),
    }


INPUTS = ("x_prompt", "x_sample", "rel_bias", "norm_mix_pre", "norm_mix_post", "w_in", "q_lora_norm", "w_uq", "kv_norm",
          "w_ukv", "c_q_norm", "c_k_norm", "w_out", "norm_ffn_pre", "norm_ffn_post", "w_up", "conv_w", "conv_b", "w_down")


def kernel(**inputs):
    from concourse import bacc
    from concourse.bass_utils import run_bass_kernel_spmd

    nc = bacc.Bacc("TRN2", target_bir_lowering=False, num_devices=1)
    c = Ctx()
    arrays = {}

    def declare(name, a):
        a = np.ascontiguousarray(a)
        arrays[name] = a
        return nc.dram_tensor(name, a.shape, mybir.dt.from_np(a.dtype), kind="ExternalInput").ap()

    (c.x_prompt, c.x_sample, c.rel_bias, c.norm_mix_pre, c.norm_mix_post, c.w_in, c.q_lora_norm, c.w_uq, c.kv_norm, c.w_ukv,
     c.c_q_norm, c.c_k_norm, c.w_out, c.norm_ffn_pre, c.norm_ffn_post, c.w_up, c.conv_w, c.conv_b, c.w_down) = [
        declare(f"in_{name}", inputs[name]) for name in INPUTS]
    k = {name: declare(f"const_{name}", a) for name, a in shape_constants().items()}
    c.d_cos_a, c.d_sin_a, c.d_cos_c, c.d_sin_c, c.d_onehot, c.d_logc = (k["cos_a"], k["sin_a"], k["cos_c"], k["sin_c"],
                                                                        k["onehot"], k["logc"])
    c.d_ident, c.d_ones, c.d_block_ones, c.d_perm_c, c.d_perm_a = (k["ident"], k["ones"], k["block_ones"], k["perm_c"], k["perm_a"])
    c.y_prompt = nc.dram_tensor("y_prompt", (1, 1024, D), F32, kind="ExternalOutput").ap()
    c.y_sample = nc.dram_tensor("y_sample", (1, 256, D), F32, kind="ExternalOutput").ap()
    encoder(nc, c)
    r = run_bass_kernel_spmd(nc, [arrays], core_ids=[0])
    return r.results[0]["y_prompt"], r.results[0]["y_sample"]
```

```python
import math
from contextlib import ExitStack

import numpy as np

import concourse.bass as bass
from concourse import mybir
from concourse.alu_op_type import AluOpType as ALU

F32 = mybir.dt.float32
F32R = mybir.dt.float32r
ACT = mybir.ActivationFunctionType
AX = mybir.AxisListType

P = 128
D = 1024
DEPTH = 2
SEGS = ((0, 1024), (1024, 256))
T = 1280
BLOCKS = ((0, 512), (512, 512), (1024, 256))
KC = D // P
NT = T // P
H_A, H_B, H_C = 4, 4, 8
HEADS = H_A + H_B + H_C
D_FF = 2816
FF_PAIRS = D_FF // (2 * P)
EPS = 1e-6
MASKED = -1e30
N_DIST = 2048
XO_EARLY = 5
GW = 1920
LOG_SET = "natural_log_exp_and_others"

QAN, QAR, KAN, KAR, VA = 0, 256, 384, 640, 672
QB, KB, VB = 928, 1184, 1440
QC, KC_ROW, VC = 1696, 2208, 2336
Z_ROWS = 2464

G_MIX_PRE, G_MIX_POST, G_FFN_PRE, G_FFN_POST, G_QL, G_KV, G_CQ, G_CK, N_GAINS = 0, 8, 16, 24, 32, 34, 35, 36, 37


N_PARAMS = N_GAINS + 4 * (2 * D_FF // P)


class Ctx:
    pass


def place_buffers(nc, c):
    at = [(nc.sbuf_base + 31) // 32 * 32]

    def take(name, shape, dt=F32):
        t = nc.alloc_sbuf_tensor_at(name, shape, dt, offset=at[0])
        at[0] += 4 * int(np.prod(shape[1:]))
        at[0] = (at[0] + 31) // 32 * 32
        return t

    c.ident = take("ident", [P, P])
    c.ident_r = take("ident_r", [P, P], F32R)
    c.ones = take("ones", [P, P])
    c.block_ones = take("block_ones", [P, P])
    c.perm_c = take("perm_c", [P, P])
    c.perm_a = take("perm_a", [P, P])
    c.params = take("params", [P, N_PARAMS])
    c.gain = c.params[:, 0:N_GAINS]
    c.conv = c.params[:, N_GAINS:].rearrange("p (t j) -> p t j", t=4)
    c.all_params = take("all_params", [P, DEPTH * N_PARAMS])
    c.eps = take("eps", [P, 1])
    h_at = at[0]
    c.hh = take("hh", [P, KC, T], F32R)
    c.hl = take("hl", [P, KC, T], F32R)
    raw_at = at[0]
    c.raw = [take(f"raw{i}", [P, KC, P]) for i in range(2)]
    wh_at = at[0]
    c.wh = [take(f"wh{i}", [P, KC, P], F32R) for i in range(2)]
    c.wl = [take(f"wl{i}", [P, KC, P], F32R) for i in range(2)]
    arena = at[0]
    end = nc.sbuf_usable_end

    c.y = take("y", [P, KC, T])
    after_y = at[0]
    c.ah = take("ah", [P, 2, T], F32R)
    c.al = take("al", [P, 2, T], F32R)
    c.wh.append(take("wh2", [P, KC, P], F32R))
    c.wl.append(take("wl2", [P, KC, P], F32R))
    cb_at = at[0]
    c.cb = [take(f"cb{i}", [P, T]) for i in range(4)]
    at[0] = cb_at
    c.xo = [take(f"xo{i}", [P, T]) for i in range(XO_EARLY)]
    c.acc = take("acc", [P, T])
    assert at[0] <= end, (at[0], end)
    at[0] = wh_at
    c.mlp_sq = [take(f"mlp_sq{i}", [P, 512]) for i in range(2)]
    at[0] = after_y
    c.out_sq = [take(f"out_sq{i}", [P, 512]) for i in range(2)]
    at[0] = after_y
    c.xo += [take(f"xo{i}", [P, T]) for i in range(XO_EARLY, KC)]
    c.r = take("r", [P, T])
    c.block_sq = [take(f"block_sq{i}", [P, 512]) for i in range(3)]
    c.block_ln = take("block_ln", [P, 512])
    assert at[0] <= cb_at
    at[0] = wh_at
    c.xsq = [take(f"xsq{i}", [P, T]) for i in range(2)]
    c.lnt = take("lnt", [P, T])
    assert at[0] <= arena
    at[0] = cb_at
    c.tok = [take(f"tok{i}", [P, D]) for i in range(4)]
    at[0] = arena
    c.gain_rows = take("gain_rows", [N_GAINS * DEPTH, P])
    c.conv_rows = take("conv_rows", [2 * D_FF // P * DEPTH, 4, P])
    c.onehot = take("onehot", [32, N_DIST])
    c.logc = take("logc", [4, N_DIST])
    c.line = take("line", [4, N_DIST])
    c.rel = take("rel", [32, H_B])
    assert at[0] <= after_y
    at[0] = arena
    c.stage = [take(f"stage{i}", [P, T]) for i in range(3)]
    c.pr = take("pr", [P, T])
    c.cos = take("cos", [P, T])
    c.sin = take("sin", [P, T])
    c.psq = [take(f"psq{i}", [P, T]) for i in range(2)]
    c.pln = take("pln", [P, T])
    after_common = at[0]
    c.lat = [take(f"lat{i}", [P, T]) for i in range(3)]
    c.lath = take("lath", [P, 3, T], F32R)
    c.latl = take("latl", [P, 3, T], F32R)
    assert at[0] <= end
    at[0] = after_common
    c.rot = [take(f"rot{i}", [P, T]) for i in range(2)]
    c.st2 = [take(f"st2_{i}", [P, T]) for i in range(2)]
    projections_end = at[0]
    at[0] = raw_at
    q1_1, q2_1 = take("q1_1", [P, T], F32R), take("q2_1", [P, T], F32R)
    assert at[0] >= wh_at
    c.p = [take(f"p{i}", [P, 512]) for i in range(4)]
    c.ln_den = take("ln_den", [P, 512])
    c.rden = take("rden", [P, 512])
    c.ot = take("ot", [P, 512])
    assert at[0] <= arena
    at[0] = arena
    k1_1, k2_1, q1_2 = take("k1_1", [P, T], F32R), take("k2_1", [P, T], F32R), take("q1_2", [P, T], F32R)
    c.q1 = [take("q1_0", [P, T], F32R), q1_1, q1_2]
    c.q2 = [take("q2_0", [P, T], F32R), q2_1, take("q2_2", [P, T], F32R)]
    c.k1 = [take("k1_0", [P, T], F32R), k1_1]
    c.k2 = [take("k2_0", [P, T], F32R), k2_1]
    c.vh = [take(f"vh{i}", [P, NT, P], F32R) for i in range(2)]
    c.vl = [take(f"vl{i}", [P, NT, P], F32R) for i in range(2)]
    at[0] = max(at[0], projections_end)
    c.rq = take("rq", [P, T])
    c.rk = take("rk", [P, T])
    c.vt = take("vt", [P, T])
    c.ph = [take(f"ph{i}", [P, 512], F32R) for i in range(4)]
    c.pl = [take(f"pl{i}", [P, 512], F32R) for i in range(4)]
    c.mx = take("mx", [P, 8, 2])
    c.m = take("m", [P, NT])
    assert at[0] <= end, (at[0], end)
    chunk = 4 * T
    c.graw = [nc.alloc_sbuf_tensor_at(f"graw{i}", [P, GW // 2], F32, offset=h_at + (8 * i + 4) * chunk) for i in range(2)]
    c.gh = [nc.alloc_sbuf_tensor_at(f"gh{i}", [P, GW], F32R, offset=h_at + (8 * i + 5) * chunk) for i in range(2)]
    c.gl = [nc.alloc_sbuf_tensor_at(f"gl{i}", [P, GW], F32R, offset=h_at + (8 * i + 5) * chunk + 4 * GW) for i in range(2)]
    c.ps = nc.alloc_psum_tensor("ps", [P, 8 * 512], F32)


def bank(c, b, w=512, rows=slice(0, P), off=0):
    return c.ps[rows, b * 512 + off:b * 512 + off + w]


def end_phase(nc, sems):
    nums = [s.num for s in sems]
    nc.multi_engine_barrier(list(nc.engines), sems_to_clear=range(min(nums), max(nums) + 1))


def product(pe, out, pairs):
    for k, (wh, wl, xh, xl) in enumerate(pairs):
        pe.matmul(out, wh, xh, start=(k == 0), stop=False)
        pe.matmul(out, wh, xl, start=False, stop=False)
        last = pe.matmul(out, wl, xh, start=False, stop=(k == len(pairs) - 1))
    return last


def project(pe, c, slot, half, after_block=None):
    for b, (t0, w) in enumerate(BLOCKS):
        last = product(pe, bank(c, 3 * half + b, w),
                       [(c.wh[slot][:, k, :], c.wl[slot][:, k, :], c.hh[:, k, t0:t0 + w], c.hl[:, k, t0:t0 + w])
                        for k in range(KC)])
        if after_block and b < 2:
            after_block(b)
    return last


def unit_psum(c, half, t0=0, t1=T, rows=slice(0, P)):
    return c.ps[rows, half * 1536 + t0:half * 1536 + t1]



GAIN_ROWS = [("norm_mix_pre", 0, 8, G_MIX_PRE), ("norm_mix_post", 8 * DEPTH, 8, G_MIX_POST),
             ("norm_ffn_pre", 16 * DEPTH, 8, G_FFN_PRE), ("norm_ffn_post", 24 * DEPTH, 8, G_FFN_POST),
             ("q_lora_norm", 32 * DEPTH, 2, G_QL), ("kv_norm", 34 * DEPTH, 1, G_KV),
             ("c_q_norm", 35 * DEPTH, 1, G_CQ), ("c_k_norm", 36 * DEPTH, 1, G_CK)]


def load_constants(nc, c):
    nj = 2 * D_FF // P
    gain_src = {"norm_mix_pre": c.norm_mix_pre, "norm_mix_post": c.norm_mix_post, "norm_ffn_pre": c.norm_ffn_pre,
                "norm_ffn_post": c.norm_ffn_post, "q_lora_norm": c.q_lora_norm, "kv_norm": c.kv_norm,
                "c_q_norm": c.c_q_norm, "c_k_norm": c.c_k_norm}
    with ExitStack() as ex:
        def sem(name):
            return ex.enter_context(nc.semaphore(name))
        table_in, consts_in, params_in, tiles_in, stored = (sem("table_in"), sem("consts_in"), sem("params_in"), sem("tiles_in"),
                                                            sem("stored"))
        products, added, turned, copied, const = sem("products"), sem("added"), sem("turned"), sem("copied"), sem("const")
        with nc.Block() as block:
            @block.sync
            def _(sp):
                for dst, src in ((c.onehot[:], c.d_onehot), (c.rel[:], c.rel_bias), (c.logc[:], c.d_logc)):
                    sp.dma_start(dst, src).then_inc(table_in, 16)
                sp.dma_start(c.ident[:], c.d_ident).then_inc(consts_in, 16)
                for name, row, n, _ in GAIN_ROWS[:6]:
                    sp.dma_start(c.gain_rows[row:row + n * DEPTH, :],
                                 gain_src[name].rearrange("l (r p) -> (l r) p", p=P)).then_inc(params_in, 16)
                for name, row, n, _ in GAIN_ROWS[6:]:
                    for half in range(2):
                        sp.dma_start(c.gain_rows[row:row + DEPTH, 64 * half:64 * half + 64], gain_src[name]).then_inc(params_in, 16)
                for i in range(DEPTH):
                    sp.dma_start(c.conv_rows[i * nj:(i + 1) * nj, 0:3, :],
                                 c.conv_w[i].rearrange("t (j p) -> j t p", p=P)).then_inc(params_in, 16)
                sp.dma_start(c.conv_rows[:, 3, :], c.conv_b.rearrange("l (j p) -> (l j) p", p=P)).then_inc(params_in, 16)
                for dst, src in ((c.ones[:], c.d_ones), (c.block_ones[:], c.d_block_ones), (c.perm_c[:], c.d_perm_c),
                                 (c.perm_a[:], c.d_perm_a)):
                    sp.dma_start(dst, src).then_inc(tiles_in, 16)
                for t in range(4):
                    sp.dma_start(c.tok[t][:], c.x_prompt[0, t * P:(t + 1) * P, :]).then_inc(tiles_in, 16)
                sp.wait_ge(added, 4)
                sp.dma_start(c.s_line, c.line[:]).then_inc(stored, 16)
                sp.wait_ge(tiles_in, 16 * 8)
                sp.wait_ge(stored, 16)

            @block.tensor
            def _(pe):
                pe.wait_ge(table_in, 16 * 3)
                for j in range(4):
                    pe.matmul(bank(c, j, rows=slice(0, H_B)), c.rel[:], c.onehot[:, 512 * j:512 * j + 512],
                              start=True, stop=True).then_inc(products, 1)
                pe.wait_ge(consts_in, 16)
                pe.wait_ge(params_in, 16 * (6 + 4 + DEPTH + 1))
                n = 37 * DEPTH
                pe.transpose(bank(c, 4, n), c.gain_rows[:], c.ident[0:n, 0:n]).then_inc(turned, 1)
                n = nj * DEPTH
                for t in range(4):
                    last = pe.transpose(bank(c, 5, n, off=t * n), c.conv_rows[:, t, :], c.ident[0:n, 0:n])
                last.then_inc(turned, 1)

            @block.vector
            def _(dve):
                dve.memset(c.eps[:], EPS).then_inc(const, 1)
                for j in range(4):
                    dve.wait_ge(products, j + 1)
                    sl = slice(512 * j, 512 * j + 512)
                    dve.tensor_tensor(c.line[:, sl], bank(c, j, rows=slice(0, H_B)), c.logc[:, sl], ALU.add).then_inc(added, 1)
                dve.wait_ge(consts_in, 16)
                dve.tensor_copy(c.ident_r[:], c.ident[:]).then_inc(const, 1)
                dve.wait_ge(turned, 1)
                for i in range(DEPTH):
                    for _, row, n, column in GAIN_ROWS:
                        dve.tensor_copy(c.all_params[:, i * N_PARAMS + column:i * N_PARAMS + column + n],
                                        bank(c, 4, n, off=row + i * n)).then_inc(copied, 1)
                dve.wait_ge(turned, 2)
                for i in range(DEPTH):
                    dve.tensor_copy(c.all_params[:, i * N_PARAMS + N_GAINS:(i + 1) * N_PARAMS].rearrange("p (t j) -> p t j", t=4),
                                    bank(c, 5, 4 * nj * DEPTH).rearrange("p (t i j) -> p t i j", t=4, i=DEPTH)[:, :, i, :]).then_inc(copied, 1)
        end_phase(nc, [table_in, consts_in, params_in, tiles_in, stored, products, added, turned, copied, const])



def turn_input(nc, c):
    TB = 5
    with ExitStack() as ex:
        def sem(name):
            return ex.enter_context(nc.semaphore(name))
        arrived = [sem(f"arrived{i}") for i in range(4)]
        turned, copied, stored = sem("turned"), sem("copied"), sem("stored")
        squared, summed, logged, root = sem("squared"), sem("summed"), sem("logged"), sem("root")
        xsq = [t[:, 0:D].rearrange("p (k t) -> p k t", k=KC) for t in c.xsq]
        with nc.Block() as block:
            @block.sync
            def _(sp):
                for t in range(4, NT):
                    sp.wait_ge(turned, 2 * (t - 3))
                    src = c.x_prompt[0, t * P:(t + 1) * P, :] if t < 8 else c.x_sample[0, (t - 8) * P:(t - 7) * P, :]
                    sp.dma_start(c.tok[t % 4][:], src).then_inc(arrived[t % 4], 16)
                for h in range(H_B):
                    sp.dma_start(c.s_lines[h], bass.AP(tensor=c.s_line.tensor, offset=h * N_DIST, ap=[[0, P], [1, N_DIST]])).then_inc(stored, 16)
                for t0, w in BLOCKS:
                    sp.wait_ge(copied, 2 * (t0 + w) // P)
                    sp.dma_start(c.s_x[:, 0:KC // 2, t0:t0 + w], c.y[:, 0:KC // 2, t0:t0 + w]).then_inc(stored, 16)
                sp.wait_ge(stored, 16 * (H_B + 3))

            @block.tensor
            def _(pe):
                def sums(t):
                    b = (0, 0, 0, 0, 1, 1, 1, 1, 2, 2)[t]
                    pe.wait_ge(squared, t + 1)
                    for k in range(KC):
                        last = pe.matmul(bank(c, TB + b, P, off=t * P - BLOCKS[b][0]), c.ones[:], xsq[t % 2][:, k, :],
                                         start=(k == 0), stop=(k == KC - 1))
                    last.then_inc(summed, 1)

                for t in range(NT):
                    if t >= 4:
                        pe.wait_ge(arrived[t % 4], 16 * (t // 4))
                    for g in range(2):
                        n = 2 * t + g
                        if n >= TB:
                            pe.wait_ge(copied, n - TB + 1)
                        for j in range(4):
                            last = pe.transpose(bank(c, n % TB, P, off=j * P), c.tok[t % 4][:, (4 * g + j) * P:(4 * g + j + 1) * P],
                                                c.ident[:])
                        last.then_inc(turned, 1)
                    if t >= 1:
                        sums(t - 1)
                sums(NT - 1)

            @block.vector
            def _(dve):
                for n in range(2 * NT):
                    t, g = n // 2, n % 2
                    dve.wait_ge(turned, n + 1)
                    dve.tensor_copy(c.y[:, 4 * g:4 * g + 4, t * P:(t + 1) * P],
                                    bank(c, n % TB).rearrange("p (k t) -> p k t", k=4)).then_inc(copied, 1)

            @block.scalar
            def _(act):
                act.preload_act_table_set(LOG_SET)
                for t in range(NT):
                    act.wait_ge(copied, 2 * t + 2)
                    if t >= 2:
                        act.wait_ge(summed, t - 1)
                    act.activation(xsq[t % 2], c.y[:, :, t * P:(t + 1) * P], ACT.Square).then_inc(squared, 1)
                for b, (t0, w) in enumerate(BLOCKS):
                    act.wait_ge(summed, (t0 + w) // P)
                    act.activation(c.lnt[:, t0:t0 + w], bank(c, TB + b, w), ACT.Ln, scale=1.0 / D, bias=c.eps[:]).then_inc(logged, 1)
                    act.wait_ge(logged, b + 1)
                    act.activation(c.r[:, t0:t0 + w], c.lnt[:, t0:t0 + w], ACT.Exp, scale=-0.5).then_inc(root, 1)
        end_phase(nc, arrived + [turned, copied, stored, squared, summed, logged, root])


def turn_output(nc, c):
    with ExitStack() as ex:
        def sem(name):
            return ex.enter_context(nc.semaphore(name))
        stored = [sem(f"stored{i}") for i in range(4)]
        turned, copied = sem("turned"), sem("copied")
        with nc.Block() as block:
            @block.tensor
            def _(pe):
                for n in range(2 * NT):
                    t, g = n // 2, n % 2
                    if n >= 8:
                        pe.wait_ge(copied, n - 7)
                    for j in range(4):
                        last = pe.transpose(bank(c, n % 8, P, off=j * P), c.y[:, 4 * g + j, t * P:(t + 1) * P], c.ident[:])
                    last.then_inc(turned, 1)

            @block.vector
            def _(dve):
                for n in range(2 * NT):
                    t, g = n // 2, n % 2
                    if t >= 4 and g == 0:
                        dve.wait_ge(stored[t % 4], 16 * (t // 4))
                    dve.wait_ge(turned, n + 1)
                    dve.tensor_copy(c.tok[t % 4][:, 512 * g:512 * g + 512], bank(c, n % 8)).then_inc(copied, 1)

            @block.sync
            def _(sp):
                for t in range(NT):
                    sp.wait_ge(copied, 2 * t + 2)
                    dst = c.y_prompt[0, t * P:(t + 1) * P, :] if t < 8 else c.y_sample[0, (t - 8) * P:(t - 7) * P, :]
                    sp.dma_start(dst, c.tok[t % 4][:]).then_inc(stored[t % 4], 16)
                for i in range(4):
                    sp.wait_ge(stored[i], 16 * ((NT - 1 - i) // 4 + 1))
        end_phase(nc, stored + [turned, copied])



def before(k, chunks):
    return sum(j < k for j in chunks)


LOW_ON_DVE = (1, 4, 6)


def wait_low(pe, lo_pool, lo_dve, b):
    pe.wait_ge(lo_dve, (b + 1) * len(LOW_ON_DVE))
    pe.wait_ge(lo_pool, (b + 1) * (KC - len(LOW_ON_DVE)))


def split_normed(nc, c, L, gain, next_unit):
    with ExitStack() as ex:
        def sem(name):
            return ex.enter_context(nc.semaphore(name))
        normed, hi_done, lo_pool, lo_dve, stored = sem("normed"), sem("hi_done"), sem("lo_pool"), sem("lo_dve"), sem("stored")
        raw_arrived, w_hi, w_lo, params, unit_done = sem("raw_arrived"), sem("w_hi"), sem("w_lo"), sem("params"), sem("unit_done")
        with nc.Block() as block:
            @block.sync
            def _(sp):
                for i in range(2):
                    sp.dma_start(c.raw[i][:], next_unit(i)).then_inc(raw_arrived, 16)
                for k in range(KC // 2, KC):
                    sp.dma_start(c.s_x[:, k, :], c.y[:, k, :]).then_inc(stored, 16)
                for i in range(2):
                    sp.wait_ge(w_lo, i + 1)
                    sp.dma_start(c.raw[i][:], next_unit(2 + i)).then_inc(raw_arrived, 16)
                sp.wait_ge(raw_arrived, 16 * 4)
                sp.wait_ge(stored, 16 * (KC // 2))

            @block.tensor
            def _(pe):
                for b in range(3):
                    wait_low(pe, lo_pool, lo_dve, b)
                    for unit in range(2):
                        if b == 0:
                            pe.wait_ge(w_lo, unit + 1)
                        first_units(pe, c, (b,), unit).then_inc(unit_done, 1)

            @block.scalar
            def _(act):
                for b, (t0, w) in enumerate(BLOCKS):
                    for k in range(KC):
                        act.wait_ge(normed, KC * b + k + 1)
                        act.activation(c.hh[:, k, t0:t0 + w], c.xo[k][:, t0:t0 + w], ACT.Copy).then_inc(hi_done, 1)
                    if b == 0:
                        for i in range(2):
                            act.wait_ge(raw_arrived, 32)
                            act.activation(c.wh[i][:], c.raw[i][:], ACT.Copy).then_inc(w_hi, 1)

            @block.vector
            def _(dve):
                if gain == G_MIX_PRE:
                    dve.tensor_copy(c.params[:], c.all_params[:, bass.ds(L * N_PARAMS, N_PARAMS)]).then_inc(params, 1)
                    dve.wait_ge(params, 1)
                for b, (t0, w) in enumerate(BLOCKS):
                    for k in range(KC):
                        dve.scalar_tensor_tensor(out=c.xo[k][:, t0:t0 + w], in0=c.y[:, k, t0:t0 + w],
                                                 scalar=c.gain[:, gain + k:gain + k + 1], in1=c.r[:, t0:t0 + w],
                                                 op0=ALU.mult, op1=ALU.mult).then_inc(normed, 1)
                        if k - 1 in LOW_ON_DVE:
                            dve.wait_ge(hi_done, KC * b + k)
                            dve.tensor_tensor(c.hl[:, k - 1, t0:t0 + w], c.xo[k - 1][:, t0:t0 + w],
                                              c.hh[:, k - 1, t0:t0 + w].bitcast(F32), ALU.subtract).then_inc(lo_dve, 1)
                    if b == 0:
                        for i in range(2):
                            dve.wait_ge(w_hi, i + 1)
                            dve.tensor_tensor(c.wl[i][:], c.raw[i][:], c.wh[i][:].bitcast(F32), ALU.subtract).then_inc(w_lo, 1)

            @block.gpsimd
            def _(pool):
                for b, (t0, w) in enumerate(BLOCKS):
                    for k in range(KC):
                        if k not in LOW_ON_DVE:
                            pool.wait_ge(hi_done, KC * b + k + 1)
                            pool.tensor_tensor(c.hl[:, k, t0:t0 + w], c.xo[k][:, t0:t0 + w], c.hh[:, k, t0:t0 + w].bitcast(F32),
                                               ALU.subtract).then_inc(lo_pool, 1)
        end_phase(nc, [normed, hi_done, lo_pool, lo_dve, stored, raw_arrived, w_hi, w_lo, params, unit_done])


def add_normed(nc, c, L, post_gain, pre_gain=None, next_unit=None):
    ADD_ON_DVE = (2, 4, 6)

    def square_slot(b, k):
        w = BLOCKS[b][1]
        if b == 2 and k >= 3:
            return c.acc[:, (k - 3) * w:(k - 2) * w]
        return c.block_sq[(KC * b + k) % 3 if b < 2 else k][:, 0:w]

    with ExitStack() as ex:
        def sem(name):
            return ex.enter_context(nc.semaphore(name))
        late, summed, logged, root = sem("late"), sem("summed"), sem("logged"), sem("root")
        scaled, added_pool, added_dve = sem("scaled"), sem("added_pool"), sem("added_dve")
        squared, new_summed, new_logged, new_root = sem("squared"), sem("new_summed"), sem("new_logged"), sem("new_root")
        normed, hi_done, lo_pool, lo_dve, stored = sem("normed"), sem("hi_done"), sem("lo_pool"), sem("lo_dve"), sem("stored")
        raw_arrived, w_hi, w_lo, unit_done = sem("raw_arrived"), sem("w_hi"), sem("w_lo"), sem("unit_done")

        def wait_added(engine, b, k):
            if k in ADD_ON_DVE:
                engine.wait_ge(added_dve, b * len(ADD_ON_DVE) + before(k, ADD_ON_DVE) + 1)
            else:
                engine.wait_ge(added_pool, b * (KC - len(ADD_ON_DVE)) + k - before(k, ADD_ON_DVE) + 1)

        with nc.Block() as block:
            @block.sync
            def _(sp):
                for k in range(XO_EARLY, KC):
                    sp.dma_start(c.xo[k][:], c.s_x[:, k, :]).then_inc(late, 16)
                if next_unit:
                    for i in range(2):
                        sp.dma_start(c.raw[i][:], next_unit(i)).then_inc(raw_arrived, 16)
                chunks = KC if next_unit else KC // 2
                for b, (t0, w) in enumerate(BLOCKS):
                    for k in range(chunks):
                        wait_added(sp, b, k)
                    sp.dma_start(c.s_x[:, 0:chunks, t0:t0 + w], c.y[:, 0:chunks, t0:t0 + w]).then_inc(stored, 16)
                if next_unit:
                    for i in range(2):
                        sp.wait_ge(w_lo, i + 1)
                        sp.dma_start(c.raw[i][:], next_unit(2 + i)).then_inc(raw_arrived, 16)
                    sp.wait_ge(raw_arrived, 16 * 4)
                sp.wait_ge(stored, 16 * 3)

            @block.tensor
            def _(pe):
                for b, (t0, w) in enumerate(BLOCKS):
                    pe.matmul(bank(c, b, w), c.ones[:], c.acc[:, t0:t0 + w], start=True, stop=True).then_inc(summed, 1)
                def sums(b):
                    w = BLOCKS[b][1]
                    if b == 2:
                        pe.wait_ge(new_logged, 1)
                    for k in range(KC):
                        pe.wait_ge(squared, KC * b + k + 1)
                        pe.matmul(bank(c, 6 + b % 2, w), c.ones[:], square_slot(b, k), start=(k == 0),
                                  stop=(k == KC - 1)).then_inc(new_summed, 1)

                def unit(n, b):
                    first_units(pe, c, (b,), n).then_inc(unit_done, 1)

                sums(0)
                sums(1)
                if pre_gain is None:
                    sums(2)
                    return
                pe.wait_ge(root, 3)
                wait_low(pe, lo_pool, lo_dve, 0)
                pe.wait_ge(w_lo, 1)
                unit(0, 0)
                sums(2)
                pe.wait_ge(w_lo, 2)
                unit(1, 0)
                for b in (1, 2):
                    wait_low(pe, lo_pool, lo_dve, b)
                    unit(0, b)
                    unit(1, b)

            @block.scalar
            def _(act):
                act.preload_act_table_set(LOG_SET)

                def squares(b, chunks):
                    t0, w = BLOCKS[b]
                    for k in chunks:
                        n = KC * b + k
                        wait_added(act, b, k)
                        if b == 2 and k == 0:
                            act.wait_ge(new_summed, n)
                        elif b < 2 and n >= 3:
                            act.wait_ge(new_summed, n - 2)
                        act.activation(square_slot(b, k), c.y[:, k, t0:t0 + w], ACT.Square).then_inc(squared, 1)

                def new_roots(b):
                    t0, w = BLOCKS[b]
                    act.wait_ge(new_summed, KC * (b + 1))
                    if b >= 1:
                        act.wait_ge(new_root, b)
                    act.activation(c.block_ln[:, 0:w], bank(c, 6 + b % 2, w), ACT.Ln, scale=1.0 / D, bias=c.eps[:]).then_inc(new_logged, 1)
                    act.wait_ge(new_logged, b + 1)
                    act.activation(c.r[:, t0:t0 + w], c.block_ln[:, 0:w], ACT.Exp, scale=-0.5).then_inc(new_root, 1)

                def high(b, chunks):
                    t0, w = BLOCKS[b]
                    for k in chunks:
                        act.wait_ge(normed, KC * b + k + 1)
                        act.activation(c.hh[:, k, t0:t0 + w], c.xo[k][:, t0:t0 + w], ACT.Copy).then_inc(hi_done, 1)

                for b, (t0, w) in enumerate(BLOCKS):
                    act.wait_ge(summed, b + 1)
                    if b >= 1:
                        act.wait_ge(root, b)
                    act.activation(c.block_ln[:, 0:w], bank(c, b, w), ACT.Ln, scale=1.0 / D, bias=c.eps[:]).then_inc(logged, 1)
                    act.wait_ge(logged, b + 1)
                    act.activation(c.r[:, t0:t0 + w], c.block_ln[:, 0:w], ACT.Exp, scale=-0.5).then_inc(root, 1)
                act.wait_ge(root, 3)
                squares(0, range(KC))
                squares(1, range(2))
                if pre_gain is None:
                    new_roots(0)
                    squares(1, range(2, KC))
                    squares(2, range(2))
                    new_roots(1)
                    squares(2, range(2, KC))
                    new_roots(2)
                    return
                new_roots(0)
                squares(1, range(2, 6))
                high(0, (0,))
                squares(1, (6,))
                high(0, (1,))
                squares(1, (7,))
                high(0, range(2, 6))
                for i in range(2):
                    act.wait_ge(raw_arrived, 32)
                    act.activation(c.wh[i][:], c.raw[i][:], ACT.Copy).then_inc(w_hi, 1)
                    high(0, (6 + i,))
                new_roots(1)
                squares(2, range(3))
                for k in range(3, KC):
                    high(1, (k - 3,))
                    squares(2, (k,))
                new_roots(2)
                high(1, range(5, KC))
                high(2, range(KC))

            @block.vector
            def _(dve):
                def first_norm(b):
                    t0, w = BLOCKS[b]
                    dve.wait_ge(root, b + 1)
                    for k in range(KC):
                        y = c.y[:, k, t0:t0 + w]
                        dve.scalar_tensor_tensor(out=y, in0=y, scalar=c.gain[:, post_gain + k:post_gain + k + 1],
                                                 in1=c.r[:, t0:t0 + w], op0=ALU.mult, op1=ALU.mult).then_inc(scaled, 1)
                        if k - 1 in ADD_ON_DVE:
                            y = c.y[:, k - 1, t0:t0 + w]
                            dve.wait_ge(scaled, KC * b + k)
                            if k - 1 >= XO_EARLY:
                                dve.wait_ge(late, 16 * (KC - XO_EARLY))
                            dve.tensor_tensor(y, y, c.xo[k - 1][:, t0:t0 + w], ALU.add).then_inc(added_dve, 1)

                def second_norm(b):
                    t0, w = BLOCKS[b]
                    dve.wait_ge(new_root, b + 1)
                    for k in range(KC):
                        wait_added(dve, b, k)
                        dve.scalar_tensor_tensor(out=c.xo[k][:, t0:t0 + w], in0=c.y[:, k, t0:t0 + w],
                                                 scalar=c.gain[:, pre_gain + k:pre_gain + k + 1], in1=c.r[:, t0:t0 + w],
                                                 op0=ALU.mult, op1=ALU.mult).then_inc(normed, 1)
                        if k - 1 in LOW_ON_DVE:
                            dve.wait_ge(hi_done, KC * b + k)
                            dve.tensor_tensor(c.hl[:, k - 1, t0:t0 + w], c.xo[k - 1][:, t0:t0 + w],
                                              c.hh[:, k - 1, t0:t0 + w].bitcast(F32), ALU.subtract).then_inc(lo_dve, 1)

                first_norm(0)
                first_norm(1)
                if pre_gain is None:
                    first_norm(2)
                    return
                second_norm(0)
                for i in range(2):
                    dve.wait_ge(w_hi, i + 1)
                    dve.tensor_tensor(c.wl[i][:], c.raw[i][:], c.wh[i][:].bitcast(F32), ALU.subtract).then_inc(w_lo, 1)
                first_norm(2)
                second_norm(1)
                second_norm(2)

            @block.gpsimd
            def _(pool):
                def add(b):
                    t0, w = BLOCKS[b]
                    for k in range(KC):
                        if k not in ADD_ON_DVE:
                            y = c.y[:, k, t0:t0 + w]
                            pool.wait_ge(scaled, KC * b + k + 1)
                            if k >= XO_EARLY:
                                pool.wait_ge(late, 16 * (KC - XO_EARLY))
                            pool.tensor_tensor(y, y, c.xo[k][:, t0:t0 + w], ALU.add).then_inc(added_pool, 1)

                def low(b):
                    t0, w = BLOCKS[b]
                    for k in range(KC):
                        if k not in LOW_ON_DVE:
                            pool.wait_ge(hi_done, KC * b + k + 1)
                            pool.tensor_tensor(c.hl[:, k, t0:t0 + w], c.xo[k][:, t0:t0 + w], c.hh[:, k, t0:t0 + w].bitcast(F32),
                                               ALU.subtract).then_inc(lo_pool, 1)

                add(0)
                add(1)
                if pre_gain is None:
                    add(2)
                    return
                low(0)
                add(2)
                low(1)
                low(2)
        end_phase(nc, [late, summed, logged, root, scaled, added_pool, added_dve, squared, new_summed, new_logged, new_root,
                       normed, hi_done, lo_pool, lo_dve, stored, raw_arrived, w_hi, w_lo, unit_done])



def w_in_chunk(c, L, col):
    return c.w_in[bass.ds(L, 1), :, col:col + P].rearrange("a (k p) n -> p (a k) n", p=P)


HEAD_UNITS = [(QB, 416), (QB + P, 544), (KB, 672), (KB + P, 800), (VB, 928), (QC, 1184), (QC + P, 1312), (QC + 2 * P, 1440),
              (QC + 3 * P, 1568), (KC_ROW, 1696), (VC, 1824), (VB + P, 1056)]


def head_unit(c, L, n):
    return w_in_chunk(c, L, HEAD_UNITS[n][1])


def out_unit(c, L, n):
    return c.w_out[bass.ds(L, 1), :, n * P:n * P + P].rearrange("a (k p) n -> p (a k) n", p=P)


def up_unit(c, L, i, unit):
    col = (i * 2 + unit // 2) * P + (unit % 2) * D_FF
    return c.w_up[bass.ds(L, 1), :, bass.ds(col, P)].rearrange("a (k p) n -> p (a k) n", p=P)


def first_units(pe, c, blocks, unit):
    for b in blocks:
        t0, w = BLOCKS[b]
        last = product(pe, bank(c, 3 * unit + b, w),
                       [(c.wh[unit][:, k, :], c.wl[unit][:, k, :], c.hh[:, k, t0:t0 + w], c.hl[:, k, t0:t0 + w]) for k in range(KC)])
    return last


def load_weights(sp, c, n, dst, src, raw_arrived, w_lo, ready=0):
    if n >= 2 + ready:
        sp.wait_ge(w_lo, n - 1 - ready)
    sp.dma_start(dst, src).then_inc(raw_arrived[n % 2], 16)


def split_hi(act, c, n, raw_arrived, w_used, w_hi, part=lambda t: t[:], arrivals=None, ready=0, done=0):
    if (arrivals or n // 2 + 1) > ready // 2:
        act.wait_ge(raw_arrived[n % 2], 16 * ((arrivals or n // 2 + 1) - ready // 2))
    if n >= 2 + done:
        act.wait_ge(w_used, n - 1 - done)
    act.activation(part(c.wh[n % 2]), part(c.raw[n % 2]), ACT.Copy).then_inc(w_hi, 1)


def split_lo(pool, c, n, w_hi, w_lo, part=lambda t: t[:], ready=0):
    pool.wait_ge(w_hi, n + 1 - ready)
    pool.tensor_tensor(part(c.wl[n % 2]), part(c.raw[n % 2]), part(c.wh[n % 2]).bitcast(F32), ALU.subtract).then_inc(w_lo, 1)


def latent_projections(nc, c, L):
    HQ, HV = 96, 128
    wide = {4: lambda t: t[:].rearrange("p k n -> p (k n)")[:, 0:2 * H_A * HQ],
            5: lambda t: t[:].rearrange("p k n -> p (k n)")[:, 0:H_A * HV]}
    outs = [(4, 0, (0, 1), QAR), (4, P, (0, 1), QAN), (4, 2 * P, (0, 1), QAN + P),
            (5, 0, (2,), KAN), (5, P, (2,), KAN + P), (5, 2 * P, (2,), VA), (5, 3 * P, (2,), VA + P)]
    with ExitStack() as ex:
        def sem(name):
            return ex.enter_context(nc.semaphore(name))
        raw_arrived = [sem("raw_arrived0"), sem("raw_arrived1")]
        w_hi, w_lo, w_used = sem("w_hi"), sem("w_lo"), sem("w_used")
        tables, unit_done, evacuated, squared = sem("tables"), sem("unit_done"), sem("evacuated"), sem("squared")
        aux_done, aux_read_act, aux_read_dve = sem("aux_done"), sem("aux_read_act"), sem("aux_read_dve")
        root, normed, lat_hi, lat_lo = sem("root"), sem("normed"), sem("lat_hi"), sem("lat_lo")
        cos_done, roped = sem("cos_done"), sem("roped")
        stored = [sem(f"stored{i}") for i in range(3)]
        with nc.Block() as block:
            @block.sync
            def _(sp):
                sp.dma_start(c.cos[:], c.d_cos_a).then_inc(tables, 16)
                sp.dma_start(c.sin[:], c.d_sin_a).then_inc(tables, 16)
                sp.wait_ge(w_lo, 1)
                for k in range(2):
                    src = c.w_uq[bass.ds(L, 1), k * P:k * P + P, :].rearrange("a p (h n) -> (a p) h n", h=H_A)
                    dst = wide[4](c.raw[0]).rearrange("p (k n) -> p k n", k=2)[:, k, :]
                    sp.dma_start(dst[:, 0:P].rearrange("p (h n) -> p h n", h=H_A), src[:, :, 64:96]).then_inc(raw_arrived[0], 16)
                    sp.dma_start(dst[:, P:3 * P].rearrange("p (h n) -> p h n", h=H_A), src[:, :, 0:64]).then_inc(raw_arrived[0], 16)
                sp.wait_ge(w_lo, 2)
                src = c.w_ukv[bass.ds(L, 1), :, :].rearrange("a p (h n) -> (a p) h n", h=H_A)
                for part in range(2):
                    dst = wide[5](c.raw[1])[:, 256 * part:256 * part + 256].rearrange("p (h n) -> p h n", h=H_A)
                    sp.dma_start(dst, src[:, :, 64 * part:64 * part + 64]).then_inc(raw_arrived[1], 16)
                for i in range(2):
                    sp.wait_ge(w_lo, 3 + i)
                    sp.dma_start(c.raw[i][:], head_unit(c, L, i)).then_inc(raw_arrived[i], 16)
                sp.wait_ge(roped, 1)
                sp.dma_start(c.s_z[KAR:KAR + 32, :], c.stage[0][0:32, :]).then_inc(stored[0], 16)
                sp.wait_ge(roped, 2)
                sp.dma_start(c.s_z[QAR:QAR + P, :], c.stage[1][:]).then_inc(stored[1], 16)
                for j in range(2, 8):
                    sp.wait_ge(evacuated, 4 + j)
                    row = outs[j - 1][3]
                    done = stored[j % 3] if j < 5 else c.latents_stored
                    sp.dma_start(c.s_z[row:row + P, :], c.stage[j % 3][:]).then_inc(done, 16)
                for i, count in enumerate((2, 2, 1)):
                    sp.wait_ge(stored[i], 16 * count)

            @block.tensor
            def _(pe):
                def aux(x, lhs_rhs, rows, w):
                    if 2 <= x < 8:
                        pe.wait_ge(aux_read_act, x - 1)
                    elif x >= 8:
                        pe.wait_ge(aux_read_dve, x - 7)
                    for k, (lhs, rhs) in enumerate(lhs_rhs):
                        last = pe.matmul(bank(c, 6 + x % 2, w, rows), lhs, rhs, start=(k == 0), stop=(k == len(lhs_rhs) - 1))
                    last.then_inc(aux_done, 1)

                pe.wait_ge(w_lo, 1)
                pe.wait_ge(evacuated, 1)
                project(pe, c, 0, 0).then_inc(w_used, 1)
                pe.wait_ge(squared, 2)
                for b, (t0, w) in enumerate(BLOCKS):
                    aux(b, [(c.ones[:], c.psq[i][:, t0:t0 + w]) for i in range(2)], slice(0, P), w)
                pe.wait_ge(w_lo, 2)
                pe.wait_ge(evacuated, 2)

                def kv_sums(b):
                    t0, w = BLOCKS[b]
                    pe.wait_ge(squared, 3)
                    aux(3 + b, [(c.ones[:], c.psq[0][:, t0:t0 + w])], slice(0, P), w)

                project(pe, c, 1, 1, kv_sums).then_inc(w_used, 1)
                kv_sums(2)
                pe.wait_ge(evacuated, 4)
                for b, (t0, w) in enumerate(BLOCKS):
                    aux(6 + b, [(c.perm_a[0:32, 0:32], c.stage[0][0:32, t0:t0 + w])], slice(0, 32), w)
                for j, (unit, col, chunks, row) in enumerate(outs):
                    m = 4 + j
                    pe.wait_ge(w_lo, unit - 1)
                    pe.wait_ge(lat_lo, 1 + max(chunks))
                    pe.wait_ge(evacuated, m - 1)
                    row_len = H_A * (HQ if unit == 4 else HV)
                    pairs = [tuple(wide[unit](t[unit % 2])[:, i * row_len + col:i * row_len + col + P] for t in (c.wh, c.wl)) + (k,)
                             for i, k in enumerate(chunks)]
                    for b, (t0, w) in enumerate(BLOCKS):
                        last = product(pe, bank(c, 3 * (m % 2) + b, w),
                                       [(wh, wl, c.lath[:, k, t0:t0 + w], c.latl[:, k, t0:t0 + w]) for wh, wl, k in pairs])
                    last.then_inc(unit_done, 1)
                    if j == 0:
                        continue
                    if j == 1:
                        pe.wait_ge(evacuated, 5)
                        for b, (t0, w) in enumerate(BLOCKS):
                            aux(9 + b, [(c.perm_a[:], c.stage[1][:, t0:t0 + w])], slice(0, P), w)

            @block.scalar
            def _(act):
                act.preload_act_table_set(LOG_SET)
                def sums(x, b, width):
                    t0, w = BLOCKS[b]
                    act.wait_ge(aux_done, x + 1)
                    if x == 3:
                        act.wait_ge(normed, 2)
                    act.activation(c.pln[:, t0:t0 + w], bank(c, 6 + x % 2, w), ACT.Ln, scale=1.0 / width, bias=c.eps[:]).then_inc(aux_read_act, 1)
                    act.wait_ge(aux_read_act, x + 1)
                    act.activation(c.pr[:, t0:t0 + w], c.pln[:, t0:t0 + w], ACT.Exp, scale=-0.5).then_inc(root, 1)

                split_hi(act, c, 2, raw_arrived, w_used, w_hi, ready=4, done=2)
                for n in range(3):
                    if n == 2:
                        for b in range(3):
                            sums(b, b, 256)
                    if n == 2:
                        act.wait_ge(w_used, 1)
                    if n == 2:
                        act.wait_ge(aux_done, 3)
                    act.activation(c.psq[n % 2][:], unit_psum(c, n % 2), ACT.Square).then_inc(squared, 1)
                    act.activation(c.lat[n][:], unit_psum(c, n % 2), ACT.Copy).then_inc(evacuated, 1)
                    if n == 0:
                        split_hi(act, c, 3, raw_arrived, w_used, w_hi, ready=4, done=2)
                split_hi(act, c, 4, raw_arrived, w_used, w_hi, wide[4], 6, 4, 2)
                for i in range(2):
                    act.wait_ge(normed, i + 1)
                    act.activation(c.lath[:, i, :], c.lat[i][:], ACT.Copy).then_inc(lat_hi, 1)
                for b in range(2):
                    sums(3 + b, b, 128)
                act.wait_ge(w_used, 2)
                act.activation(c.stage[0][0:32, :], unit_psum(c, 1, rows=slice(0, 32)), ACT.Copy).then_inc(evacuated, 1)
                split_hi(act, c, 5, raw_arrived, w_used, w_hi, wide[5], 4, 4, 2)
                sums(5, 2, 128)
                act.wait_ge(normed, 3)
                act.activation(c.lath[:, 2, :], c.lat[2][:], ACT.Copy).then_inc(lat_hi, 1)
                for j in range(1, 8):
                    m = 3 + j
                    act.wait_ge(unit_done, j)
                    if j >= 3:
                        act.wait_ge(stored[j % 3], 16 * (j // 3))
                    act.activation(c.stage[j % 3][:], unit_psum(c, m % 2), ACT.Copy).then_inc(evacuated, 1)
                    if j in (3, 7):
                        i = j // 4
                        act.wait_ge(raw_arrived[i], 16 * (5, 3)[i])
                        act.activation(c.wh[i][:], c.raw[i][:], ACT.Copy).then_inc(w_hi, 1)

            @block.gpsimd
            def _(pool):
                for n in (2, 3):
                    split_lo(pool, c, n, w_hi, w_lo, ready=2)
                split_lo(pool, c, 4, w_hi, w_lo, wide[4], 2)
                split_lo(pool, c, 5, w_hi, w_lo, wide[5], 2)
                pool.wait_ge(tables, 32)
                pool.wait_ge(evacuated, 4)
                pool.wait_ge(aux_done, 3)
                pool.tensor_tensor(c.psq[1][0:32, :], c.stage[0][0:32, :], c.cos[0:32, :], ALU.mult).then_inc(cos_done, 1)
                pool.wait_ge(evacuated, 5)
                pool.wait_ge(roped, 1)
                pool.tensor_tensor(c.psq[1][:], c.stage[1][:], c.cos[:], ALU.mult).then_inc(cos_done, 1)
                for i in range(2):
                    pool.wait_ge(w_hi, 5 + i)
                    pool.tensor_tensor(c.wl[i][:], c.raw[i][:], c.wh[i][:].bitcast(F32), ALU.subtract).then_inc(w_lo, 1)

            @block.vector
            def _(dve):
                def scale_latent(i, gain):
                    dve.scalar_tensor_tensor(out=c.lat[i][:], in0=c.lat[i][:], scalar=c.gain[:, gain:gain + 1], in1=c.pr[:],
                                             op0=ALU.mult, op1=ALU.mult).then_inc(normed, 1)

                def low_latent(i):
                    dve.wait_ge(lat_hi, i + 1)
                    dve.tensor_tensor(c.latl[:, i, :], c.lat[i][:], c.lath[:, i, :].bitcast(F32), ALU.subtract).then_inc(lat_lo, 1)

                def rope(x0, rows, r, j):
                    for b, (t0, w) in enumerate(BLOCKS):
                        dve.wait_ge(aux_done, x0 + b + 1)
                        dve.tensor_tensor(c.psq[0][rows, t0:t0 + w], bank(c, 6 + (x0 + b) % 2, w, rows), c.sin[rows, t0:t0 + w],
                                          ALU.mult).then_inc(aux_read_dve, 1)
                    dve.wait_ge(aux_read_dve, x0 + 3 - 6)
                    dve.wait_ge(cos_done, r + 1)
                    dve.tensor_tensor(c.stage[j][rows, :], c.psq[0][rows, :], c.psq[1][rows, :], ALU.add).then_inc(roped, 1)

                dve.wait_ge(root, 3)
                dve.wait_ge(evacuated, 2)
                scale_latent(0, G_QL)
                scale_latent(1, G_QL + 1)
                low_latent(0)
                low_latent(1)
                dve.wait_ge(root, 6)
                dve.wait_ge(evacuated, 3)
                scale_latent(2, G_KV)
                dve.wait_ge(tables, 32)
                rope(6, slice(0, 32), 0, 0)
                low_latent(2)
                dve.wait_ge(roped, 1)
                rope(9, slice(0, P), 1, 1)
        end_phase(nc, raw_arrived + [w_hi, w_lo, w_used, tables, unit_done, evacuated, squared, aux_done, aux_read_act,
                                     aux_read_dve, root, normed, lat_hi, lat_lo, cos_done, roped] + stored)


def head_projections(nc, c, L):
    UNITS = 12
    rows = [row for row, _ in HEAD_UNITS]
    ROPED = range(5, 10)
    with ExitStack() as ex:
        def sem(name):
            return ex.enter_context(nc.semaphore(name))
        raw_arrived = [sem("raw_arrived0"), sem("raw_arrived1")]
        w_hi, w_lo, w_used = sem("w_hi"), sem("w_lo"), sem("w_used")
        tables, evacuated, squared, unit_sum, turned = sem("tables"), sem("evacuated"), sem("squared"), sem("unit_sum"), sem("turned")
        sum_read, turn_read, root, cos_done, added, roped = (sem("sum_read"), sem("turn_read"), sem("root"), sem("cos_done"),
                                                             sem("added"), sem("roped"))
        stored, head0 = [sem(f"stored{i}") for i in range(3)], sem("head0")
        with nc.Block() as block:
            @block.sync
            def _(sp):
                sp.wait_ge(c.latents_stored, 16 * 3)
                for dst, row, n in ((c.rq[0:64, :], QAN, 64), (c.rq[64:96, :], QAR, 32), (c.rk[0:64, :], KAN, 64),
                                    (c.rk[64:96, :], KAR, 32), (c.vt[0:64, :], VA, 64)):
                    sp.dma_start(dst, c.s_z[row:row + n, :]).then_inc(head0, 16)
                sp.dma_start(c.cos[:], c.d_cos_c).then_inc(tables, 16)
                sp.dma_start(c.sin[:], c.d_sin_c).then_inc(tables, 16)

                def store(n):
                    if n in ROPED:
                        sp.wait_ge(roped, n - ROPED[0] + 1)
                    else:
                        sp.wait_ge(evacuated, n + 1)
                    done = stored[n % 3] if n < UNITS - 3 else c.heads_stored
                    sp.dma_start(c.s_z[rows[n]:rows[n] + P, :], c.stage[n % 3][:]).then_inc(done, 16)

                for n in range(2, UNITS):
                    load_weights(sp, c, n, c.raw[n % 2][:], head_unit(c, L, n), raw_arrived, w_lo, 2)
                    if n >= 4:
                        store(n - 4)
                for n in range(UNITS - 4, UNITS):
                    store(n)
                for i in range(3):
                    sp.wait_ge(stored[i], 16 * 3)
                sp.wait_ge(head0, 16 * 5)

            @block.tensor
            def _(pe):
                def norm_and_turn(n, b):
                    r = n - ROPED[0]
                    t0, w = BLOCKS[b]
                    pe.wait_ge(evacuated, n + 1)
                    if 3 * r + b >= 1:
                        pe.wait_ge(sum_read, 3 * r + b)
                    pe.matmul(bank(c, 6, w), c.block_ones[:], c.psq[n % 2][:, t0:t0 + w], start=True, stop=True).then_inc(unit_sum, 1)
                    if 3 * r + b >= 1:
                        pe.wait_ge(turn_read, 3 * r + b)
                    pe.matmul(bank(c, 7, w), c.perm_c[:], c.stage[n % 3][:, t0:t0 + w], start=True, stop=True).then_inc(turned, 1)

                for n in range(UNITS):
                    if n >= 2:
                        pe.wait_ge(w_lo, n - 1)
                        pe.wait_ge(evacuated, n - 1)
                    if n - 1 in ROPED:
                        project(pe, c, n % 2, n % 2, lambda b: norm_and_turn(n - 1, b)).then_inc(w_used, 1)
                        norm_and_turn(n - 1, 2)
                    else:
                        project(pe, c, n % 2, n % 2).then_inc(w_used, 1)

            @block.scalar
            def _(act):
                act.preload_act_table_set(LOG_SET)
                def roots(n, blocks):
                    r = n - ROPED[0]
                    for b in blocks:
                        t0, w = BLOCKS[b]
                        x = 3 * r + b
                        act.wait_ge(unit_sum, x + 1)
                        if r >= 1:
                            act.wait_ge(roped, r)
                        act.activation(c.pln[:, t0:t0 + w], bank(c, 6, w), ACT.Ln, scale=1.0 / 64, bias=c.eps[:]).then_inc(sum_read, 1)
                        act.wait_ge(sum_read, x + 1)
                        act.activation(c.pr[:, t0:t0 + w], c.pln[:, t0:t0 + w], ACT.Exp, scale=-0.5).then_inc(root, 1)

                for n in range(UNITS):
                    if n - 1 in ROPED:
                        roots(n - 1, (0, 1))
                    act.wait_ge(w_used, n + 1)
                    if n >= 3:
                        act.wait_ge(stored[n % 3], 16 * (n // 3))
                    elif n == 0:
                        act.wait_ge(c.latents_stored, 16 * 3)
                    if n in ROPED:
                        if n >= ROPED[2]:
                            act.wait_ge(unit_sum, 3 * (n - ROPED[1]))
                        act.activation(c.psq[n % 2][:], unit_psum(c, n % 2), ACT.Square).then_inc(squared, 1)
                        g = G_CK if rows[n] == KC_ROW else G_CQ
                        act.activation(c.stage[n % 3][:], unit_psum(c, n % 2), ACT.Identity, scale=c.gain[:, g:g + 1]).then_inc(evacuated, 1)
                    else:
                        act.activation(c.stage[n % 3][:], unit_psum(c, n % 2), ACT.Copy, scale=0.125 if n < 2 else 1.0).then_inc(evacuated, 1)
                    if n + 2 < UNITS:
                        split_hi(act, c, n + 2, raw_arrived, w_used, w_hi, ready=2)
                    if n - 1 in ROPED:
                        roots(n - 1, (2,))

            @block.gpsimd
            def _(pool):
                pool.wait_ge(tables, 32)
                for n in range(UNITS):
                    if n + 2 < UNITS:
                        split_lo(pool, c, n + 2, w_hi, w_lo, ready=2)
                    if n in ROPED:
                        pool.wait_ge(evacuated, n + 1)
                        if n >= ROPED[2]:
                            pool.wait_ge(roped, n - ROPED[1])
                        pool.tensor_tensor(c.st2[n % 2][:], c.stage[n % 3][:], c.cos[:], ALU.mult).then_inc(cos_done, 1)

            @block.vector
            def _(dve):
                dve.wait_ge(tables, 32)
                for n in ROPED:
                    r = n - ROPED[0]
                    rot = c.rot[n % 2]
                    for b, (t0, w) in enumerate(BLOCKS):
                        dve.wait_ge(turned, 3 * r + b + 1)
                        dve.tensor_tensor(rot[:, t0:t0 + w], bank(c, 7, w), c.sin[:, t0:t0 + w], ALU.mult).then_inc(turn_read, 1)
                    dve.wait_ge(turn_read, 3 * r + 3)
                    dve.wait_ge(cos_done, r + 1)
                    dve.tensor_tensor(rot[:], rot[:], c.st2[n % 2][:], ALU.add).then_inc(added, 1)
                    dve.wait_ge(added, r + 1)
                    dve.wait_ge(root, 3 * r + 3)
                    dve.tensor_tensor(c.stage[n % 3][:], rot[:], c.pr[:], ALU.mult).then_inc(roped, 1)
        end_phase(nc, raw_arrived + [w_hi, w_lo, w_used, tables, evacuated, squared, unit_sum, turned, sum_read, turn_read,
                                     root, cos_done, added, roped, head0] + stored)



def attention(nc, c, L):
    STEPS = []
    for half in range(2):
        block = [(2 * half, 512 * half, 512, kt, kt == 0, kt == 7) for kt in range(8)]
        STEPS += block[0:4] + [(1, 1024, 256, 8 + half, half == 0, half == 1)] + block[4:8]
    NS = len(STEPS)
    FIRST = [i for i, step in enumerate(STEPS) if step[4]]
    LAST = [8, 13, 17]
    assert all(STEPS[i][0] == block and STEPS[i][5] for block, i in enumerate(LAST))
    MAXES = [(qt, 512 * kb, 512, kb) for qt in range(8) for kb in range(2)]
    MAXES[8:8] = [(8, 1024, 256, 2), (9, 1024, 256, 2)]
    NM = len(MAXES)
    assert NM == NS
    ROW_TILES = ((0, 4), (8, 10), (4, 8))
    MAX_LEAD = 13
    SIDE, ST, OB = 0, 2, 5
    RING = 4
    PV_LAG = 3
    G_TOTAL = HEADS * NS
    G_END = G_TOTAL + PV_LAG + 4
    STEP_SCALE = {"A": 96 ** -0.5, "B": 1.0, "C": 0.125}

    def kind(h):
        return "A" if h < 4 else "B" if h < 8 else "C"

    def kv(h):
        return h % 2 if h < 8 else (h - 8) // 4

    def new_kv(h):
        return 0 <= h <= 8 or h == 12

    def kv_count(h):
        return sum(new_kv(i) for i in range(h + 1))

    def pl_engine(g):
        h, i = divmod(g, NS)
        start = 0 if not new_kv(h + 1) else 7 if kind(h + 1) == "B" else 4
        return "pool" if i >= start and i % 2 else "dve"

    def pl_count(g, who):
        return sum(pl_engine(x) == who for x in range(g + 1))

    def side_work(h, i):
        work = []
        if i < NM - MAX_LEAD and 0 <= h < HEADS:
            work.append(("max", h, MAX_LEAD + i))
        if i >= NS - MAX_LEAD and 0 <= h + 1 < HEADS:
            work.append(("max", h + 1, i - (NS - MAX_LEAD)))
        if i in (3, 11) and new_kv(h + 1):
            work.append(("values", h + 1, (i - 3) // 8))
        if i == 7 and 0 <= h < HEADS:
            work.append(("row", h, 2))
        if i in (15, 17) and 0 <= h + 1 < HEADS:
            work.append(("row", h + 1, (i - 15) // 2))
        return work

    side_order = [item for g in range(-2 * NS, G_TOTAL) for item in side_work(*divmod(g, NS))]
    side_bank = {item: SIDE + n % 2 for n, item in enumerate(side_order)}

    def ended(g, lag):
        h, i = divmod(g - lag, NS)
        return [3 * h + LAST.index(i)] if 0 <= h < HEADS and i in LAST else []

    def out_block(o):
        q0, w = STEPS[LAST[o % 3]][1:3]
        r0 = 64 * (o // 3 % 2)
        return q0, w, slice(r0, r0 + 64)

    with ExitStack() as ex:
        def sem(name):
            return ex.enter_context(nc.semaphore(name))
        q_raw, k_raw, v_raw, table_raw = sem("q_raw"), sem("k_raw"), sem("v_raw"), sem("table_raw")
        consts, q_hi, k_hi, k_hi_low, q_lo, k_lo = (sem("consts"), sem("q_hi"), sem("k_hi"), sem("k_hi_low"), sem("q_lo"),
                                                    sem("k_lo"))
        table_hi, table_lo, v_turned, v_hi, v_lo = (sem("table_hi"), sem("table_lo"), sem("v_turned"), sem("v_hi"),
                                                    sem("v_lo"))
        max_scored, max_taken, max_ready, row_turned, row_copied = (sem("max_scored"), sem("max_taken"), sem("max_ready"),
                                                                    sem("row_turned"), sem("row_copied"))
        weights = sem("weights")
        scored, exp_done, lo_pool, lo_dve, pv_done = sem("scored"), sem("exp_done"), sem("lo_pool"), sem("lo_dve"), sem("pv_done")
        ln_done, rden_done, scaled, out_hi, out_lo = sem("ln_done"), sem("rden_done"), sem("scaled"), sem("out_hi"), sem("out_lo")

        def side_read(item):
            what, h, j = item
            if what == "max":
                return max_taken, NM * h + j + 1
            if what == "values":
                return v_lo, 2 * (kv_count(h) - 1) + j + 1
            return row_copied, 3 * h + j + 1

        with nc.Block() as block:
            @block.sync
            def _(sp):
                sp.wait_ge(c.heads_stored, 16 * 3)
                for h in range(1, HEADS):
                    sp.wait_ge(q_hi, 3 * h)
                    sp.wait_ge(q_lo, 3 * h)
                    if kind(h) == "A":
                        sp.dma_start(c.rq[0:64, :], c.s_z[QAN + 64 * h:QAN + 64 * h + 64, :]).then_inc(q_raw, 16)
                        sp.dma_start(c.rq[64:96, :], c.s_z[QAR + 32 * h:QAR + 32 * h + 32, :]).then_inc(q_raw, 16)
                    else:
                        row = QB + 64 * (h - 4) if h < 8 else QC + 64 * (h - 8)
                        for half in range(2):
                            sp.dma_start(c.rq[64 * half:64 * half + 64, :], c.s_z[row:row + 64, :]).then_inc(q_raw, 16)
                    if not new_kv(h):
                        continue
                    n = kv_count(h) - 1
                    sp.wait_ge(k_lo, 3 * n)
                    if kind(h) != "A" and n > 4:
                        sp.wait_ge(k_hi_low, 3 * (n - 4))
                    if kind(h) == "A":
                        sp.dma_start(c.rk[0:64, :], c.s_z[KAN + 64 * h:KAN + 64 * h + 64, :]).then_inc(k_raw, 16)
                        sp.dma_start(c.rk[64:96, :], c.s_z[KAR:KAR + 32, :]).then_inc(k_raw, 16)
                        vrow = VA + 64 * h
                    else:
                        krow, vrow = (KB + 64 * (h - 4), VB + 64 * (h - 4)) if h < 8 else (KC_ROW + 64 * kv(h), VC + 64 * kv(h))
                        for half in range(2):
                            sp.dma_start(c.rk[64 * half:64 * half + 64, :], c.s_z[krow:krow + 64, :]).then_inc(k_raw, 16)
                    if kind(h) == "B":
                        if h > 4:
                            sp.wait_ge(table_lo, 2 * (h - 4))
                        for i in range(2):
                            src = bass.AP(tensor=c.s_lines.tensor, offset=(h - 4) * P * N_DIST + P - 1 + i * GW // 2,
                                          ap=[[N_DIST - 1, P], [1, GW // 2]])
                            sp.dma_start(c.graw[i][:], src).then_inc(table_raw, 16)
                    sp.wait_ge(v_turned, 2 * n)
                    sp.dma_start(c.vt[0:64, :], c.s_z[vrow:vrow + 64, :]).then_inc(v_raw, 16)
                sp.wait_ge(scored, NS * 14)
                for i in range(2):
                    sp.dma_start(c.raw[i][:], out_unit(c, L, i)).then_inc(weights, 16)
                sp.wait_ge(weights, 32)

            @block.tensor
            def _(pe):
                def scores(g):
                    h, i = divmod(g, NS)
                    block, q0, w, kt, first, last = STEPS[i]
                    out = bank(c, ST + g % 3, w)
                    q1, q2, k1, k2 = c.q1[h % 3], c.q2[h % 3], c.k1[kv(h)], c.k2[kv(h)]
                    if g >= 3:
                        pe.wait_ge(exp_done, 2 * (g - 2))
                    if i == 0:
                        pe.wait_ge(q_lo, 3 * (h + 1))
                        pe.wait_ge(k_lo, 3 * kv_count(h))
                        if h < 2:
                            pe.wait_ge(consts, 3 * (h + 1))
                        if h in (4, 5):
                            pe.wait_ge(consts, h + 3)
                        if h >= 4 and new_kv(h):
                            pe.wait_ge(k_hi_low, 3 * (kv_count(h) - 4))
                        if kind(h) == "B":
                            pe.wait_ge(table_lo, 2 * (h - 3))
                    if first:
                        pe.wait_ge(row_copied, 3 * h + block + 1)
                    ks, qs = slice(kt * P, kt * P + P), slice(q0, q0 + w)
                    if kind(h) == "A":
                        prods = [(k1[0:97, ks], q1[0:97, qs]), (k2[0:96, ks], q1[0:96, qs]), (k1[0:96, ks], q2[0:96, qs])]
                    else:
                        prods = [(k1[:, ks], q1[:, qs]), (k2[0:65, ks], q2[0:65, qs])]
                    if kind(h) == "B":
                        x0 = (q0 - kt * P) + 896
                        prods += [(c.ident_r[:], c.gh[h % 2][:, x0:x0 + w]), (c.ident_r[:], c.gl[h % 2][:, x0:x0 + w])]
                    for k, (a, b) in enumerate(prods):
                        mm = pe.matmul(out, a, b, start=(k == 0), stop=(k == len(prods) - 1))
                    mm.then_inc(scored, 1)

                def values(g):
                    h, i = divmod(g, NS)
                    block, q0, w, kt, first, last = STEPS[i]
                    if first and h >= 1:
                        pe.wait_ge(scaled, 3 * (h - 1) + block + 1)
                    if i == 0:
                        pe.wait_ge(v_lo, 2 * kv_count(h))
                    out = bank(c, OB + block, w)
                    pe.wait_ge(exp_done, 2 * g + 1)
                    pe.matmul(out, c.vh[kv(h)][:, kt, :], c.ph[g % RING][:, 0:w], start=first, stop=False)
                    pe.matmul(out, c.vl[kv(h)][:, kt, :], c.ph[g % RING][:, 0:w], start=False, stop=False)
                    who = pl_engine(g)
                    pe.wait_ge(lo_dve if who == "dve" else lo_pool, pl_count(g, who))
                    pe.matmul(out, c.vh[kv(h)][:, kt, :], c.pl[g % RING][:, 0:w], start=False, stop=last).then_inc(pv_done, 1)

                def max_scores(h, j, b):
                    qt, k0, w, kb = MAXES[j]
                    pe.wait_ge(q_hi, 3 * h + qt // 4 + 1)
                    if kind(h) == "A":
                        pe.wait_ge(k_hi, 3 * (kv_count(h) - 1) + kb + 1)
                    else:
                        pe.wait_ge(k_lo, 3 * (kv_count(h) - 1) + kb + 1)
                    if kind(h) == "B":
                        pe.wait_ge(table_hi, 2 * (h - 3))
                    r = 96 if kind(h) == "A" else P
                    out = bank(c, b, w)
                    mm = pe.matmul(out, c.q1[h % 3][0:r, qt * P:qt * P + P], c.k1[kv(h)][0:r, k0:k0 + w], start=True, stop=kind(h) != "B")
                    if kind(h) == "B":
                        for kk in range(w // P):
                            x0 = qt * P - (k0 + kk * P) + 896
                            mm = pe.matmul(out[:, kk * P:kk * P + P], c.gh[h % 2][:, x0:x0 + P], c.ident_r[:],
                                           start=False, stop=(kk == w // P - 1))
                    mm.then_inc(max_scored, 1)

                def turn_values(h, part, b):
                    if h >= 1:
                        pe.wait_ge(v_raw, 16 * (kv_count(h) - 1))
                    for t in (range(8) if part == 0 else range(8, 10)):
                        mm = pe.transpose(bank(c, b, 64, off=(t % 8) * 64), c.vt[0:64, t * P:t * P + P], c.ident[0:64, 0:64])
                    mm.then_inc(v_turned, 1)

                def turn_row(h, r, b):
                    if r == 1:
                        pe.wait_ge(max_taken, NM * h + 10)
                    else:
                        pe.wait_ge(max_ready, 2 * h + r // 2 + 1)
                    for k, qt in enumerate(range(*ROW_TILES[r])):
                        mm = pe.matmul(bank(c, b, P, slice(0, 1), off=k * P), c.m[:, qt:qt + 1], c.ident[:], start=True, stop=True)
                    mm.then_inc(row_turned, 1)

                n = 0
                for g in range(-2 * NS, G_TOTAL + PV_LAG):
                    if 0 <= g < G_TOTAL:
                        scores(g)
                    for item in side_work(*divmod(g, NS)):
                        if n >= 2:
                            pe.wait_ge(*side_read(side_order[n - 2]))
                        what, h, j = item
                        if what == "max":
                            max_scores(h, j, side_bank[item])
                        elif what == "values":
                            turn_values(h, j, side_bank[item])
                        else:
                            turn_row(h, j, side_bank[item])
                        n += 1
                    if g >= PV_LAG:
                        values(g - PV_LAG)

            @block.scalar
            def _(act):
                act.preload_act_table_set(LOG_SET)

                def split_q(h, b):
                    t0, w = BLOCKS[b]
                    if h >= 1:
                        act.wait_ge(q_raw, 32 * h)
                    if h >= 3:
                        act.wait_ge(scored, NS * (h - 2))
                    r = 96 if kind(h) == "A" else P
                    act.activation(c.q1[h % 3][0:r, t0:t0 + w], c.rq[0:r, t0:t0 + w], ACT.Copy).then_inc(q_hi, 1)

                def split_k(h, b):
                    t0, w = BLOCKS[b]
                    if h >= 1:
                        act.wait_ge(k_raw, 32 * (kv_count(h) - 1))
                    if h == 1 and b == 0:
                        act.wait_ge(c.heads_stored, 16 * 3)
                    if h >= 2:
                        act.wait_ge(scored, NS * (h - 1))
                    if kind(h) == "A":
                        act.activation(c.k1[kv(h)][0:96, t0:t0 + w], c.rk[0:96, t0:t0 + w], ACT.Copy).then_inc(k_hi, 1)
                    else:
                        act.activation(c.k1[kv(h)][:, t0:t0 + w], c.rk[:, t0:t0 + w], ACT.Copy).then_inc(k_hi, 1)
                        act.activation(c.k2[kv(h)][0:64, t0:t0 + w], c.rk[0:64, t0:t0 + w], ACT.Copy).then_inc(k_hi_low, 1)

                def split_table(h, i):
                    act.wait_ge(table_raw, 32 * (h - 3))
                    act.activation(c.gh[h % 2][:, i * GW // 2:(i + 1) * GW // 2], c.graw[i][:], ACT.Copy).then_inc(table_hi, 1)

                def copy_row(h, r, b):
                    act.wait_ge(row_turned, 3 * h + r + 1)
                    t0, t1 = (x * P for x in ROW_TILES[r])
                    row = c.q1[h % 3][96:97, t0:t1] if kind(h) == "A" else c.q2[h % 3][64:65, t0:t1]
                    act.activation(row, bank(c, b, t1 - t0, slice(0, 1)), ACT.Copy).then_inc(row_copied, 1)

                def denominators(o):
                    q0, w, rows = out_block(o)
                    act.wait_ge(pv_done, o // 3 * NS + LAST[o % 3] + 1)
                    if o >= 1:
                        act.wait_ge(scaled, o)
                    act.activation(c.ln_den[0:64, 0:w], bank(c, OB + o % 3, w, slice(64, P)), ACT.Ln).then_inc(ln_done, 1)
                    act.wait_ge(ln_done, o + 1)
                    act.activation(c.rden[0:64, 0:w], c.ln_den[0:64, 0:w], ACT.Exp, scale=-1.0).then_inc(rden_done, 1)

                for g in range(-2 * NS, G_END):
                    h, i = divmod(g, NS)
                    if 0 <= g < G_TOTAL:
                        w = STEPS[i][2]
                        scores = bank(c, ST + g % 3, w)
                        act.wait_ge(scored, g + 1)
                        if g >= RING:
                            act.wait_ge(pv_done, g - RING + 1)
                        act.activation(c.ph[g % RING][:, 0:w], scores, ACT.Exp, scale=STEP_SCALE[kind(h)]).then_inc(exp_done, 1)
                        act.activation(c.p[g % RING][:, 0:w], scores, ACT.Exp, scale=STEP_SCALE[kind(h)]).then_inc(exp_done, 1)
                    if i in (9, 11, 13) and h + 2 < HEADS:
                        split_q(h + 2, (i - 9) // 2)
                    if i < 3 and new_kv(h + 1):
                        split_k(h + 1, i)
                    if i in (3, 4) and kind(h + 1) == "B":
                        split_table(h + 1, i - 3)
                    for what, head, j in side_work(h, i):
                        if what == "row":
                            copy_row(head, j, side_bank[what, head, j])
                    for o in ended(g, PV_LAG + 1):
                        denominators(o)

            @block.gpsimd
            def _(pool):
                before = [None, None, 0]

                def settle(rows, semaphore, count):
                    if before[0] is not None and before[0] != rows:
                        pool.wait_ge(before[1], before[2])
                    before[:] = [rows, semaphore, count]

                def lo_q(h, b):
                    t0, w = BLOCKS[b]
                    r = 96 if kind(h) == "A" else 64
                    pool.wait_ge(q_hi, 3 * h + b + 1)
                    settle((0, r), q_lo, 3 * h + b + 1)
                    pool.tensor_tensor(c.q2[h % 3][0:r, t0:t0 + w], c.rq[0:r, t0:t0 + w], c.q1[h % 3][0:r, t0:t0 + w].bitcast(F32),
                                       ALU.subtract).then_inc(q_lo, 1)

                def lo_k(h, b):
                    t0, w = BLOCKS[b]
                    n = 3 * (kv_count(h) - 1) + b + 1
                    pool.wait_ge(k_hi, n)
                    if kind(h) == "A":
                        rows, out = slice(0, 96), c.k2[kv(h)]
                    else:
                        rows, out = slice(64, P), c.k1[kv(h)]
                    settle((rows.start, rows.stop), k_lo, n)
                    pool.tensor_tensor(out[rows, t0:t0 + w], c.rk[rows, t0:t0 + w], c.k1[kv(h)][rows, t0:t0 + w].bitcast(F32),
                                       ALU.subtract).then_inc(k_lo, 1)

                def lo_table(h, i):
                    sl = slice(i * GW // 2, (i + 1) * GW // 2)
                    n = 2 * (h - 4) + i + 1
                    pool.wait_ge(table_hi, n)
                    settle((0, P), table_lo, n)
                    pool.tensor_tensor(c.gl[h % 2][:, sl], c.graw[i][:], c.gh[h % 2][:, sl].bitcast(F32), ALU.subtract).then_inc(table_lo, 1)

                def lo_output(o):
                    q0, w, rows = out_block(o)
                    pool.wait_ge(out_hi, o + 1)
                    settle((rows.start, rows.stop), out_lo, o + 1)
                    pool.tensor_tensor(c.hl[rows, o // 6, q0:q0 + w], c.ot[rows, 0:w], c.hh[rows, o // 6, q0:q0 + w].bitcast(F32),
                                       ALU.subtract).then_inc(out_lo, 1)

                def stationary_constants(slot):
                    if slot == 1:
                        pool.wait_ge(c.heads_stored, 16 * 3)
                    settle((96, 97), consts, 3 * slot + 1)
                    pool.memset(c.k1[slot][96:97, :].bitcast(F32), 1.0).then_inc(consts, 1)
                    settle((0, P), consts, 3 * slot + 3)
                    pool.memset(c.vh[slot][:, :, 64:P].bitcast(F32), 1.0).then_inc(consts, 1)
                    pool.memset(c.vl[slot][:, :, 64:P].bitcast(F32), 0.0).then_inc(consts, 1)

                for g in range(-2 * NS, G_END):
                    h, i = divmod(g, NS)
                    if 0 <= g < G_TOTAL and pl_engine(g) == "pool":
                        w = STEPS[i][2]
                        pool.wait_ge(exp_done, 2 * g + 2)
                        if g >= RING:
                            pool.wait_ge(pv_done, g - RING + 1)
                        settle((0, P), lo_pool, pl_count(g, "pool"))
                        pool.tensor_tensor(c.pl[g % RING][:, 0:w], c.p[g % RING][:, 0:w], c.ph[g % RING][:, 0:w].bitcast(F32),
                                           ALU.subtract).then_inc(lo_pool, 1)
                    if i in (9, 11, 13) and h + 2 < HEADS:
                        lo_q(h + 2, (i - 9) // 2)
                    if i < 3 and new_kv(h + 1):
                        lo_k(h + 1, i)
                    if i in (4, 5) and kind(h + 1) == "B":
                        lo_table(h + 1, i - 4)
                    if h == -1 and i in (4, 5):
                        stationary_constants(i - 4)
                    for o in ended(g, PV_LAG + 3):
                        lo_output(o)

            @block.vector
            def _(dve):
                def take_max(h, j, b):
                    qt, k0, w, kb = MAXES[j]
                    if h >= 1 and j == 0:
                        dve.wait_ge(max_ready, 2 * h)
                    if h >= 1 and j == 8:
                        dve.wait_ge(row_turned, 3 * h - 1)
                    dve.wait_ge(max_scored, NM * h + j + 1)
                    if qt < 8:
                        dve.tensor_reduce(c.mx[:, qt, kb:kb + 1], bank(c, b, w), AX.X, ALU.max).then_inc(max_taken, 1)
                    else:
                        dve.tensor_reduce(c.m[:, qt:qt + 1], bank(c, b, w), AX.X, ALU.max, negate=True).then_inc(max_taken, 1)
                    if j in (7, 17):
                        r = j // 16
                        dve.wait_ge(max_taken, NM * h + j + 1)
                        if h >= 1:
                            dve.wait_ge(row_turned, 3 * (h - 1) + 2 * r + 1)
                        dve.tensor_reduce(c.m[:, 4 * r:4 * r + 4], c.mx[:, 4 * r:4 * r + 4, :], AX.X, ALU.max, negate=True).then_inc(max_ready, 1)

                def split_values(h, part, b):
                    n = kv_count(h) - 1
                    tiles, nt = (slice(0, 8), 8) if part == 0 else (slice(8, 10), 2)
                    src = bank(c, b, 64 * nt).rearrange("p (t v) -> p t v", v=64)
                    dve.wait_ge(v_turned, 2 * n + part + 1)
                    if h >= 2:
                        dve.wait_ge(pv_done, NS * (h - 1))
                    dve.tensor_copy(c.vh[kv(h)][:, tiles, 0:64], src).then_inc(v_hi, 1)
                    dve.wait_ge(v_hi, 2 * n + part + 1)
                    dve.tensor_tensor(c.vl[kv(h)][:, tiles, 0:64], src, c.vh[kv(h)][:, tiles, 0:64].bitcast(F32), ALU.subtract).then_inc(v_lo, 1)

                def scale_output(o):
                    q0, w, rows = out_block(o)
                    dve.wait_ge(rden_done, o + 1)
                    if o >= 1:
                        dve.wait_ge(out_lo, o)
                    dve.tensor_tensor(c.ot[rows, 0:w], bank(c, OB + o % 3, w, slice(0, 64)), c.rden[0:64, 0:w], ALU.mult).then_inc(scaled, 1)
                    dve.wait_ge(scaled, o + 1)
                    dve.tensor_copy(c.hh[rows, o // 6, q0:q0 + w], c.ot[rows, 0:w]).then_inc(out_hi, 1)

                for g in range(-2 * NS, G_END):
                    h, i = divmod(g, NS)
                    if i == 1 and h + 1 in (4, 5):
                        dve.wait_ge(scored, NS * h)
                        dve.memset(c.k2[kv(h + 1)][64:65, :].bitcast(F32), 1.0).then_inc(consts, 1)
                    for what, head, j in side_work(h, i):
                        if what == "max":
                            take_max(head, j, side_bank[what, head, j])
                        elif what == "values":
                            split_values(head, j, side_bank[what, head, j])
                    if 0 <= g < G_TOTAL and pl_engine(g) == "dve":
                        w = STEPS[i][2]
                        dve.wait_ge(exp_done, 2 * g + 2)
                        if g >= RING:
                            dve.wait_ge(pv_done, g - RING + 1)
                        dve.tensor_tensor(c.pl[g % RING][:, 0:w], c.p[g % RING][:, 0:w], c.ph[g % RING][:, 0:w].bitcast(F32),
                                          ALU.subtract).then_inc(lo_dve, 1)
                    for o in ended(g, PV_LAG + 2):
                        scale_output(o)
        end_phase(nc, [c.latents_stored, c.heads_stored, q_raw, k_raw, v_raw, table_raw, consts, q_hi, k_hi, k_hi_low, q_lo, k_lo, table_hi, table_lo, v_turned, v_hi,
                       v_lo, max_scored, max_taken, max_ready, row_turned, row_copied, scored, exp_done, lo_pool, lo_dve,
                       pv_done, ln_done, rden_done, scaled, out_hi, out_lo, weights])



def output_projection(nc, c, L):
    items = [(n, b, t0, w) for n in range(1, KC) for b, (t0, w) in enumerate(BLOCKS)]
    with ExitStack() as ex:
        def sem(name):
            return ex.enter_context(nc.semaphore(name))
        raw_arrived = [sem("raw_arrived0"), sem("raw_arrived1")]
        w_hi, w_lo, w_used, evacuated = sem("w_hi"), sem("w_lo"), sem("w_used"), sem("evacuated")
        first_squared, squared, summed, residual = sem("first_squared"), sem("squared"), sem("summed"), sem("residual")
        with nc.Block() as block:
            @block.sync
            def _(sp):
                for n in range(2, KC):
                    load_weights(sp, c, n, c.raw[n % 2][:], out_unit(c, L, n), raw_arrived, w_lo)
                for k in range(XO_EARLY):
                    sp.dma_start(c.xo[k][:], c.s_x[:, k, :]).then_inc(residual, 16)
                sp.wait_ge(residual, 16 * XO_EARLY)

            @block.tensor
            def _(pe):
                for n in range(KC):
                    pe.wait_ge(w_lo, n + 1)
                    if n >= 2:
                        pe.wait_ge(evacuated, n - 1)
                    project(pe, c, n % 2, n % 2).then_inc(w_used, 1)

            @block.scalar
            def _(act):
                for i in range(2):
                    act.activation(c.wh[i][:], c.raw[i][:], ACT.Copy).then_inc(w_hi, 1)
                for n in range(KC):
                    act.wait_ge(w_used, n + 1)
                    act.activation(c.y[:, n, :], unit_psum(c, n % 2), ACT.Copy).then_inc(evacuated, 1)
                    act.wait_ge(evacuated, n + 1)
                    if n == 0:
                        act.activation(c.acc[:], c.y[:, 0, :], ACT.Square).then_inc(first_squared, 1)
                    for x, (m, b, t0, w) in enumerate(items):
                        if m == n:
                            if x >= 2:
                                act.wait_ge(summed, x - 1)
                            act.activation(c.out_sq[x % 2][:, 0:w], c.y[:, n, t0:t0 + w], ACT.Square).then_inc(squared, 1)
                    if n + 2 < KC:
                        split_hi(act, c, n + 2, raw_arrived, w_used, w_hi, arrivals=(n + 2) // 2)

            @block.gpsimd
            def _(pool):
                for n in range(KC):
                    split_lo(pool, c, n, w_hi, w_lo)

            @block.vector
            def _(dve):
                dve.wait_ge(first_squared, 1)
                for x, (n, b, t0, w) in enumerate(items):
                    dve.wait_ge(squared, x + 1)
                    if x >= 3:
                        dve.wait_ge(summed, x - 2)
                    dve.tensor_tensor(c.acc[:, t0:t0 + w], c.acc[:, t0:t0 + w], c.out_sq[x % 2][:, 0:w], ALU.add).then_inc(summed, 1)
        end_phase(nc, raw_arrived + [w_hi, w_lo, w_used, evacuated, first_squared, squared, summed, residual])



def gated_mlp(nc, c, L):
    DOWN_BANKS = [3, 4, 5, 6, 7] * 4 + [3, 4, 6, 7]
    LAST_BANKS = [6, 7, 0, 1, 2, 3, 4, 5]

    def first(i):
        return 4 + 6 * (i - 1)

    with ExitStack() as ex:
        def sem(name):
            return ex.enter_context(nc.semaphore(name))
        raw_arrived = [sem("raw_arrived0"), sem("raw_arrived1")]
        w_hi, w_lo, w_used = sem("w_hi"), sem("w_lo"), sem("w_used")
        centred, shifted, gelu_done, gated, act_hi, act_lo = (sem("centred"), sem("shifted"),
            sem("gelu_done"), sem("gated"), sem("act_hi"), sem("act_lo"))
        down_done, down_added, cleared, left = sem("down_done"), sem("down_added"), sem("cleared"), sem("left")
        squared, summed, residual, act_lo1 = sem("squared"), sem("summed"), sem("residual"), sem("act_lo1")
        with nc.Block() as block:
            def down_src(i, k):
                return c.w_down[bass.ds(L, 1), bass.ds((i * 2 + k) * P, P), :].rearrange("a p n -> p (a n)")

            @block.sync
            def _(sp):
                def load(n, parity, src, flat=False):
                    sp.wait_ge(w_lo, n - 3)
                    dst = c.raw[parity][:].rearrange("p k n -> p (k n)") if flat else c.raw[parity][:]
                    sp.dma_start(dst, src).then_inc(raw_arrived[parity], 16)

                with sp.Fori(1, FF_PAIRS) as i:
                    n = first(i)
                    load(n, 0, up_unit(c, L, i, 0))
                    load(n + 1, 1, down_src(i - 1, 0), True)
                    load(n + 2, 0, down_src(i - 1, 1), True)
                    load(n + 3, 1, up_unit(c, L, i, 1))
                    load(n + 4, 0, up_unit(c, L, i, 2))
                    load(n + 5, 1, up_unit(c, L, i, 3))
                n = first(FF_PAIRS)
                load(n, 0, down_src(FF_PAIRS - 1, 0), True)
                load(n + 1, 1, down_src(FF_PAIRS - 1, 1), True)
                sp.wait_ge(act_lo, FF_PAIRS)
                sp.wait_ge(act_lo1, 3 * FF_PAIRS)
                for k in range(XO_EARLY):
                    sp.dma_start(c.xo[k][:], c.s_x[:, k, :]).then_inc(residual, 16)
                sp.wait_ge(residual, 16 * XO_EARLY)

            @block.tensor
            def _(pe):
                def up(n, slot, m, half, downs=None):
                    pe.wait_ge(w_lo, n - 1)
                    if downs is not None:
                        pe.wait_ge(down_added, downs * 24 - 2)
                    pe.wait_ge(shifted, m - 1)
                    project(pe, c, slot, half).then_inc(w_used, 1)

                def down(n, slots, it, wait=True):
                    pe.wait_ge(w_lo, n)
                    pe.wait_ge(act_lo, it)
                    pe.wait_ge(act_lo1, it * 3)
                    for u in range(24):
                        o, (t0, w) = u // 3, BLOCKS[u % 3]
                        if u == 0:
                            pe.wait_ge(shifted, 4 * it)
                        elif u == 3 and wait:
                            pe.wait_ge(down_added, (it - 1) * 24)
                        elif u >= 5:
                            pe.wait_ge(down_added, (it - 1) * 24 + u - (3 if u >= 22 else 4))
                        last = product(pe, bank(c, DOWN_BANKS[u], w),
                                       [(c.wh[s][:, o, :], c.wl[s][:, o, :], c.ah[:, k, t0:t0 + w], c.al[:, k, t0:t0 + w])
                                        for k, s in enumerate(slots)])
                        if u == 23:
                            last.then_inc(w_used, 2)
                        else:
                            last.then_inc(down_done, 1)

                def down_last():
                    it = FF_PAIRS

                    def products(u, k):
                        o, (t0, w) = u // 3, BLOCKS[u % 3]
                        out, s = bank(c, LAST_BANKS[u % 8], w), 1 + k
                        wh, wl = c.wh[s][:, o, :], c.wl[s][:, o, :]
                        pe.matmul(out, wh, c.ah[:, k, t0:t0 + w], start=(k == 0), stop=False)
                        pe.matmul(out, wh, c.al[:, k, t0:t0 + w], start=False, stop=False)
                        return pe.matmul(out, wl, c.ah[:, k, t0:t0 + w], start=False, stop=(k == 1))

                    pe.wait_ge(w_lo, first(it))
                    pe.wait_ge(act_lo, it)
                    pe.wait_ge(shifted, 4 * it - 1)
                    pe.wait_ge(down_added, (it - 1) * 24)
                    for u in range(8):
                        if u == 5:
                            pe.wait_ge(shifted, 4 * it)
                        products(u, 0)
                    pe.wait_ge(act_lo1, it * 3)
                    for u in range(24):
                        if u >= 8:
                            pe.wait_ge(down_added, (it - 1) * 24 + u - 7)
                            products(u, 0)
                        last = products(u, 1)
                        if u == 23:
                            last.then_inc(w_used, 2)
                        else:
                            last.then_inc(down_done, 1)

                up(2, 2, 2, 0)
                up(3, 0, 3, 1)
                n = first(1)
                up(n, 1, 4, 0)
                down(n + 1, (2, 0), 1, False)
                up(n + 3, 1, 5, 1, downs=1)
                up(n + 4, 2, 6, 0)
                up(n + 5, 0, 7, 1)
                with pe.Fori(2, FF_PAIRS) as i:
                    n = first(i)
                    up(n, 1, 4 * i, 0)
                    down(n + 1, (2, 0), i)
                    up(n + 3, 1, 4 * i + 1, 1, downs=i)
                    up(n + 4, 2, 4 * i + 2, 0)
                    up(n + 5, 0, 4 * i + 3, 1)
                down_last()

            def split(act, n, slot, parity, raws, wait=True, slot_used=True):
                if wait:
                    act.wait_ge(raw_arrived[parity], 16 * (raws - 2))
                if slot_used:
                    act.wait_ge(w_used, n - 4)
                act.activation(c.wh[slot][:], c.raw[parity][:], ACT.Copy).then_inc(w_hi, 1)

            @block.scalar
            def _(act):
                def centre(i, unit, used, wait=True):
                    if wait:
                        act.wait_ge(w_used, used - 2)
                    j = i * 2 + unit // 2 + (unit % 2) * (D_FF // P)
                    act.activation(c.cb[unit][:], unit_psum(c, unit % 2), ACT.Identity, scale=c.conv[:, 1, bass.ds(j, 1)],
                                   bias=c.conv[:, 3, bass.ds(j, 1)]).then_inc(centred, 1)

                def gelu(i, k):
                    act.wait_ge(shifted, i * 4 + 2 * k + 1)
                    act.activation(c.cb[2 * k][:], c.cb[2 * k][:], ACT.Gelu_apprx_tanh).then_inc(gelu_done, 1)

                def hi(i, k):
                    if k == 0:
                        act.wait_ge(gated, i * 4 + 1)
                        act.activation(c.ah[:, 0, :], c.cb[0][:], ACT.Copy).then_inc(act_hi, 1)
                    else:
                        for b, (t0, w) in enumerate(BLOCKS):
                            act.wait_ge(gated, i * 4 + 2 + b)
                            act.activation(c.ah[:, 1, t0:t0 + w], c.cb[2][:, t0:t0 + w], ACT.Copy).then_inc(act_hi, 1)

                centre(0, 0, 1, False)
                split(act, 2, 2, 0, 2, False, False)
                split(act, 3, 0, 1, 2, False, False)
                gelu(0, 0)
                centre(0, 1, 2, False)
                split(act, 4, 1, 0, 3, slot_used=False)
                hi(0, 0)
                centre(0, 2, 3)
                split(act, 5, 2, 1, 3)
                gelu(0, 1)
                centre(0, 3, 4)
                hi(0, 1)
                with act.Fori(1, FF_PAIRS) as i:
                    n = first(i)
                    half = 2 + 3 * (i - 1)
                    split(act, n + 2, 0, 0, half + 2)
                    act.wait_ge(act_lo, i)
                    act.wait_ge(act_lo1, i * 3)
                    centre(i, 0, n + 1)
                    split(act, n + 3, 1, 1, half + 2)
                    gelu(i, 0)
                    split(act, n + 4, 2, 0, half + 3)
                    split(act, n + 5, 0, 1, half + 3)
                    centre(i, 1, n + 4)
                    split(act, n + 6, 1, 0, half + 4)
                    hi(i, 0)
                    centre(i, 2, n + 5)
                    split(act, n + 7, 2, 1, half + 4)
                    gelu(i, 1)
                    centre(i, 3, n + 6)
                    hi(i, 1)
                for u in range(24):
                    o, (t0, w) = u // 3, BLOCKS[u % 3]
                    act.wait_ge(down_added, (FF_PAIRS - 1) * 24 + u + 1)
                    if u >= 5:
                        act.wait_ge(summed, u - 4)
                    act.activation(c.acc[:, t0:t0 + w] if u < 3 else c.mlp_sq[u % 2][:, 0:w], c.y[:, o, t0:t0 + w],
                                   ACT.Square).then_inc(squared, 1)

            @block.gpsimd
            def _(pool):
                def lo(n, slot, parity):
                    pool.wait_ge(w_hi, n - 1)
                    pool.tensor_tensor(c.wl[slot][:], c.raw[parity][:], c.wh[slot][:].bitcast(F32), ALU.subtract).then_inc(w_lo, 1)

                def act_low(i):
                    pool.wait_ge(act_hi, i * 4 + 1)
                    pool.tensor_tensor(c.al[:, 0, :], c.cb[0][:], c.ah[:, 0, :].bitcast(F32), ALU.subtract).then_inc(act_lo, 1)

                lo(2, 2, 0)
                lo(3, 0, 1)
                pool.memset(c.y[:], 0.0).then_inc(cleared, 1)
                lo(4, 1, 0)
                act_low(0)
                lo(5, 2, 1)
                with pool.Fori(1, FF_PAIRS) as i:
                    n = first(i)
                    lo(n + 2, 0, 0)
                    lo(n + 3, 1, 1)
                    lo(n + 4, 2, 0)
                    lo(n + 5, 0, 1)
                    lo(n + 6, 1, 0)
                    act_low(i)
                    lo(n + 7, 2, 1)
                for u in range(3, 24):
                    t0, w = BLOCKS[u % 3]
                    pool.wait_ge(squared, u + 1)
                    if u >= 6:
                        pool.wait_ge(summed, u - 5)
                    pool.tensor_tensor(c.acc[:, t0:t0 + w], c.acc[:, t0:t0 + w], c.mlp_sq[u % 2][:, 0:w], ALU.add).then_inc(summed, 1)

            @block.vector
            def _(dve):
                def shift(i, unit):
                    m = i * 4 + unit
                    j = i * 2 + unit // 2 + (unit % 2) * (D_FF // P)
                    dve.wait_ge(centred, m + 1)
                    for seg, (t0, s) in enumerate(SEGS):
                        dve.scalar_tensor_tensor(out=c.cb[unit][:, t0 + 1:t0 + s], in0=unit_psum(c, unit % 2, t0, t0 + s - 1),
                                                 scalar=c.conv[:, 0, bass.ds(j, 1)], in1=c.cb[unit][:, t0 + 1:t0 + s],
                                                 op0=ALU.mult, op1=ALU.add).then_inc(left, 1)
                    dve.wait_ge(left, m * 2 + 2)
                    for seg, (t0, s) in enumerate(SEGS):
                        mm = dve.scalar_tensor_tensor(out=c.cb[unit][:, t0:t0 + s - 1], in0=unit_psum(c, unit % 2, t0 + 1, t0 + s),
                                                      scalar=c.conv[:, 2, bass.ds(j, 1)], in1=c.cb[unit][:, t0:t0 + s - 1],
                                                      op0=ALU.mult, op1=ALU.add)
                    mm.then_inc(shifted, 1)

                def gate(i, k):
                    dve.wait_ge(gelu_done, i * 2 + k + 1)
                    dve.wait_ge(shifted, i * 4 + 2 * k + 2)
                    if k == 0:
                        dve.tensor_tensor(c.cb[0][:], c.cb[0][:], c.cb[1][:], ALU.mult).then_inc(gated, 1)
                        return
                    for t0, w in BLOCKS:
                        dve.tensor_tensor(c.cb[2][:, t0:t0 + w], c.cb[2][:, t0:t0 + w], c.cb[3][:, t0:t0 + w], ALU.mult).then_inc(gated, 1)
                    for b, (t0, w) in enumerate(BLOCKS):
                        dve.wait_ge(act_hi, i * 4 + 2 + b)
                        dve.tensor_tensor(c.al[:, 1, t0:t0 + w], c.cb[2][:, t0:t0 + w], c.ah[:, 1, t0:t0 + w].bitcast(F32),
                                          ALU.subtract).then_inc(act_lo1, 1)

                def add_down(it):
                    for u in range(24):
                        o, (t0, w) = u // 3, BLOCKS[u % 3]
                        if u == 23:
                            dve.wait_ge(w_used, first(it) + 1)
                        else:
                            dve.wait_ge(down_done, (it - 1) * 23 + u + 1)
                        dve.tensor_tensor(c.y[:, o, t0:t0 + w], bank(c, DOWN_BANKS[u], w), c.y[:, o, t0:t0 + w], ALU.add).then_inc(down_added, 1)

                for unit in range(4):
                    shift(0, unit)
                    if unit % 2:
                        gate(0, unit // 2)
                dve.wait_ge(cleared, 1)
                with dve.Fori(1, FF_PAIRS) as i:
                    shift(i, 0)
                    add_down(i)
                    for unit in range(1, 4):
                        shift(i, unit)
                        if unit % 2:
                            gate(i, unit // 2)
                for u in range(24):
                    o, (t0, w) = u // 3, BLOCKS[u % 3]
                    if u == 23:
                        dve.wait_ge(w_used, first(FF_PAIRS))
                    else:
                        dve.wait_ge(down_done, (FF_PAIRS - 1) * 23 + u + 1)
                    dve.tensor_tensor(c.y[:, o, t0:t0 + w], bank(c, LAST_BANKS[u % 8], w), c.y[:, o, t0:t0 + w], ALU.add).then_inc(down_added, 1)
        end_phase(nc, raw_arrived + [w_hi, w_lo, w_used, centred, shifted, gelu_done, gated, act_hi, act_lo,
                                     down_done, down_added, cleared, left, squared, summed, residual, act_lo1])


def encoder(nc, c):
    c.s_x = nc.dram_tensor("residual", (P, KC, T), F32, kind="Internal").ap()
    c.s_z = nc.dram_tensor("heads", (Z_ROWS, T), F32, kind="Internal").ap()
    c.s_line = nc.dram_tensor("distance_lines", (H_B, N_DIST), F32, kind="Internal").ap()
    c.s_lines = nc.dram_tensor("distance_tables", (H_B, P, N_DIST), F32, kind="Internal").ap()
    place_buffers(nc, c)
    c.latents_stored = nc.alloc_semaphore("latents_stored")
    c.heads_stored = nc.alloc_semaphore("heads_stored")
    load_constants(nc, c)
    turn_input(nc, c)
    with nc.Fori(0, DEPTH) as L:
        split_normed(nc, c, L, G_MIX_PRE, lambda i: w_in_chunk(c, L, P * i))
        latent_projections(nc, c, L)
        head_projections(nc, c, L)
        attention(nc, c, L)
        output_projection(nc, c, L)
        add_normed(nc, c, L, G_MIX_POST, G_FFN_PRE, lambda i: up_unit(c, L, 0, i))
        gated_mlp(nc, c, L)
        add_normed(nc, c, L, G_FFN_POST)
    turn_output(nc, c)



def rope_tables(positions, n_freq):
    inv = np.float32(10000.0) ** (-np.arange(n_freq, dtype=np.float32) / np.float32(n_freq))
    ang = positions.astype(np.float32)[None, :] * inv.astype(np.float32)[:, None]
    return np.cos(ang).astype(np.float32), np.sin(ang).astype(np.float32)


def swap_halves(n, width):
    m = np.zeros((n, n), np.float32)
    h = width // 2
    for g in range(0, n, width):
        for i in range(h):
            m[g + h + i, g + i] = -1.0
            m[g + i, g + h + i] = 1.0
    return m


def distance_constants():
    dist = 1023 - np.arange(N_DIST)
    half, exact = 16, 8
    n = np.abs(dist)
    large = exact + (np.log(np.maximum(n, 1) / exact) / math.log(1024 / exact) * (half - exact)).astype(np.int32)
    bucket = np.where(dist > 0, half, 0) + np.where(n < exact, n, np.minimum(large, half - 1))
    onehot = (bucket[None, :] == np.arange(32)[:, None]).astype(np.float32)
    count = np.zeros(N_DIST, np.int64)
    for window, dilation in ((128, 1), (512, 4), (2048, 16)):
        count += (n % dilation == 0) & (n // dilation <= window // (2 * dilation))
    logc = np.where(count > 0, np.log(np.maximum(count, 1)), MASKED).astype(np.float32)
    return onehot, np.ascontiguousarray(np.broadcast_to(logc, (H_B, N_DIST)))


def shape_constants():
    pos = np.concatenate([np.arange(s) for _, s in SEGS])
    cos_a, sin_a = rope_tables(pos, 16)
    cos_r, sin_r = rope_tables(pos // 64, 16)
    cos_l, sin_l = rope_tables(pos % 64, 16)
    onehot, logc = distance_constants()
    return {
        "cos_a": np.tile(cos_a, (8, 1)), "sin_a": np.tile(sin_a, (8, 1)),
        "cos_c": np.tile(np.concatenate([cos_r, cos_r, cos_l, cos_l]), (2, 1)),
        "sin_c": np.tile(np.concatenate([sin_r, sin_r, sin_l, sin_l]), (2, 1)),
        "onehot": onehot, "logc": logc, "ident": np.eye(P, dtype=np.float32), "ones": np.ones((P, P), np.float32),
        "block_ones": np.kron(np.eye(2, dtype=np.float32), np.ones((64, 64), np.float32)),
        "perm_c": swap_halves(P, 32), "perm_a": swap_halves(P, 32),
    }


INPUTS = ("x_prompt", "x_sample", "rel_bias", "norm_mix_pre", "norm_mix_post", "w_in", "q_lora_norm", "w_uq", "kv_norm",
          "w_ukv", "c_q_norm", "c_k_norm", "w_out", "norm_ffn_pre", "norm_ffn_post", "w_up", "conv_w", "conv_b", "w_down")


def kernel(**inputs):
    from concourse import bacc
    from concourse.bass_utils import run_bass_kernel_spmd

    nc = bacc.Bacc("TRN2", target_bir_lowering=False, num_devices=1)
    c = Ctx()
    arrays = {}

    def declare(name, a):
        a = np.ascontiguousarray(a)
        arrays[name] = a
        return nc.dram_tensor(name, a.shape, mybir.dt.from_np(a.dtype), kind="ExternalInput").ap()

    (c.x_prompt, c.x_sample, c.rel_bias, c.norm_mix_pre, c.norm_mix_post, c.w_in, c.q_lora_norm, c.w_uq, c.kv_norm, c.w_ukv,
     c.c_q_norm, c.c_k_norm, c.w_out, c.norm_ffn_pre, c.norm_ffn_post, c.w_up, c.conv_w, c.conv_b, c.w_down) = [
        declare(f"in_{name}", inputs[name]) for name in INPUTS]
    k = {name: declare(f"const_{name}", a) for name, a in shape_constants().items()}
    c.d_cos_a, c.d_sin_a, c.d_cos_c, c.d_sin_c, c.d_onehot, c.d_logc = (k["cos_a"], k["sin_a"], k["cos_c"], k["sin_c"],
                                                                        k["onehot"], k["logc"])
    c.d_ident, c.d_ones, c.d_block_ones, c.d_perm_c, c.d_perm_a = (k["ident"], k["ones"], k["block_ones"], k["perm_c"], k["perm_a"])
    c.y_prompt = nc.dram_tensor("y_prompt", (1, 1024, D), F32, kind="ExternalOutput").ap()
    c.y_sample = nc.dram_tensor("y_sample", (1, 256, D), F32, kind="ExternalOutput").ap()
    encoder(nc, c)
    r = run_bass_kernel_spmd(nc, [arrays], core_ids=[0])
    return r.results[0]["y_prompt"], r.results[0]["y_sample"]
```
